# Optimizing a Trainium2 kernel written in Bass

```python
import jax
import jax.numpy as jnp
from jax import lax
import numpy as np

D_MODEL = 1024
BATCH = 1
SEQ = 256
DEPTH = 2

HEAD_DIM = 64
MIX_HEADS = 12
MIX_WIDTH = MIX_HEADS * HEAD_DIM
MEM_HEADS = 4
MEM_WIDTH = MEM_HEADS * HEAD_DIM
MEM_TOKENS = 256
DECAY_LORA = 64
ICLR_LORA = 64
VALUE_LORA = 32
GATE_LORA = 128
A_COLS_FIRST = 3 * MIX_WIDTH + DECAY_LORA + ICLR_LORA + GATE_LORA
A_COLS_REST = A_COLS_FIRST + VALUE_LORA
N_A_LAYERS = DEPTH // 2
N_B_LAYERS = DEPTH - N_A_LAYERS
N_DENSE = (DEPTH + 1) // 2
N_MOE = DEPTH // 2
D_FF = 2816
N_EXPERTS = 8
TOP_K = 2
Q_BLOCK = 128
LN_EPS = 1e-5
GN_EPS = 64e-5
DEEPNORM_ALPHA = (2 * DEPTH) ** 0.25
DEEPNORM_BETA = (8 * DEPTH) ** -0.25

kernel_name = 'hybrid_rwkv7_stickbreak_yoco_moe'

def _f32(t):
    return t.astype(jnp.float32)

def layer_norm(x, g, b):
    xf = _f32(x)
    mu = jnp.mean(xf, -1, keepdims=True)
    var = jnp.mean(jnp.square(xf - mu), -1, keepdims=True)
    y = (xf - mu) * lax.rsqrt(var + LN_EPS)
    return (y * _f32(g) + _f32(b)).astype(x.dtype)

def split_heads(t):
    return t.reshape(t.shape[0], t.shape[1], -1, HEAD_DIM)

def wkv7_scan(r, w, k, v, a, b):
    bsz, _, h, n = r.shape

    def step(S, inp):
        r_t, w_t, k_t, v_t, a_t, b_t = inp
        sa = jnp.einsum('bhij,bhj->bhi', S, a_t)
        S = S * w_t[:, :, None, :] + sa[..., None] * b_t[:, :, None, :] + v_t[..., None] * k_t[:, :, None, :]
        return S, jnp.einsum('bhij,bhj->bhi', S, r_t)

    xs = tuple(jnp.moveaxis(t, 1, 0) for t in (r, w, k, v, a, b))
    s0 = jnp.zeros((bsz, h, n, n), jnp.float32)
    _, ys = lax.scan(step, s0, xs)
    return jnp.moveaxis(ys, 0, 1)

def rwkv7_time_mix(proj, mu, vec, w_up, a_up, g_up, r_k, v_gate, v_first):
    has_vres = v_gate is not None
    bsz, seq, _ = proj.shape
    prev = jnp.pad(proj[:, :-1], ((0, 0), (1, 0), (0, 0)))
    xs = proj + mu * (prev - proj)
    sizes = [MIX_WIDTH] * 3 + [DECAY_LORA, ICLR_LORA] + ([VALUE_LORA] if has_vres else []) + [GATE_LORA]
    parts = jnp.split(xs, np.cumsum(sizes)[:-1].tolist(), axis=-1)
    r, k, v, wd, ad = parts[:5]
    gd = parts[-1]
    w0, a0, k_k, k_a, lnx_g, lnx_b = (vec[i] for i in range(6))
    log_w = -jax.nn.softplus(-(w0 + jnp.tanh(wd) @ w_up)) - 0.5
    decay = jnp.exp(-jnp.exp(_f32(log_w)))
    a = jax.nn.sigmoid(a0 + ad @ a_up)
    if has_vres:
        v0, v_up = v_gate
        v = v + (v_first - v) * jax.nn.sigmoid(v0 + parts[5] @ v_up)
    else:
        v_first = v
    g = jax.nn.sigmoid(gd) @ g_up
    kk = _f32(split_heads(k * k_k))
    kk = kk / jnp.maximum(jnp.linalg.norm(kk, axis=-1, keepdims=True), 1e-12)
    k = k * (1 + (a - 1) * k_a)
    rh, kh, vh = _f32(split_heads(r)), _f32(split_heads(k)), _f32(split_heads(v))
    ah = _f32(split_heads(a))
    y = wkv7_scan(rh, split_heads(decay), kh, vh, -kk, kk * ah)
    mu_y = jnp.mean(y, -1, keepdims=True)
    var_y = jnp.mean(jnp.square(y - mu_y), -1, keepdims=True)
    y = ((y - mu_y) * lax.rsqrt(var_y + GN_EPS)).reshape(bsz, seq, MIX_WIDTH)
    y = y * _f32(lnx_g) + _f32(lnx_b)
    bonus = jnp.sum(rh * kh * _f32(r_k), -1, keepdims=True) * vh
    y = y + bonus.reshape(bsz, seq, MIX_WIDTH)
    return y.astype(proj.dtype) * g, v_first

def stick_breaking_attention(q, k, v):
    bsz, seq, h, n = q.shape
    scale = n ** -0.5
    outs = []
    for blk in range(seq // Q_BLOCK):
        t0 = blk * Q_BLOCK
        kv_len = t0 + Q_BLOCK
        z = _f32(jnp.einsum('bqhd,bkhd->bhqk', q[:, t0:kv_len], k[:, :kv_len])) * scale
        q_pos = t0 + jnp.arange(Q_BLOCK)
        k_pos = jnp.arange(kv_len)
        causal = k_pos[None, :] < q_pos[:, None]
        log_1m = jnp.where(causal, jax.nn.log_sigmoid(-z), 0.0)
        log_rest = lax.cumsum(log_1m, axis=3, reverse=True) - log_1m
        wts = jnp.where(causal, jnp.exp(jax.nn.log_sigmoid(z) + log_rest), 0.0)
        outs.append(jnp.einsum('bhqk,bkhd->bqhd', wts.astype(v.dtype), v[:, :kv_len]))
    return jnp.concatenate(outs, axis=1).reshape(bsz, seq, h * n)

def memory_attention(q_mem, mem, w_mem_kv):
    mk, mv = jnp.split(mem @ w_mem_kv, 2, axis=-1)
    q, mk, mv = split_heads(q_mem), split_heads(mk), split_heads(mv)
    s = _f32(jnp.einsum('bthd,bmhd->bhtm', q, mk)) * (HEAD_DIM ** -0.5)
    p = jax.nn.softmax(s, axis=-1).astype(mv.dtype)
    o = jnp.einsum('bhtm,bmhd->bthd', p, mv)
    return o.reshape(q_mem.shape)

def swiglu(x, w_gate_up, w_down):
    gate, up = jnp.split(x @ w_gate_up, 2, axis=-1)
    return (jax.nn.silu(gate) * up) @ w_down

def moe_swiglu(x, w_router, w_gate_up, w_down):
    logits = _f32(x @ w_router)
    top_logits, top_idx = lax.top_k(logits, TOP_K)
    top_w = jax.nn.softmax(top_logits, axis=-1)
    combine = jnp.sum(jax.nn.one_hot(top_idx, N_EXPERTS, dtype=jnp.float32) * top_w[..., None], axis=-2).astype(x.dtype)
    y = jnp.zeros_like(x)
    for e in range(N_EXPERTS):
        y = y + combine[..., e:e + 1] * swiglu(x, w_gate_up[e], w_down[e])
    return y

def setup_inputs(seed: int = 0) -> dict:
    key = jax.random.key(seed)
    ks = iter(jax.random.split(key, 48))

    def nrm(shape, scale):
        return jax.random.normal(next(ks), shape, jnp.float32) * scale

    def unif(shape, lo, hi):
        return jax.random.uniform(next(ks), shape, jnp.float32, minval=lo, maxval=hi)

    d_in = D_MODEL ** -0.5
    x = nrm((BATCH, SEQ, D_MODEL), 1.0)
    mem = nrm((BATCH, MEM_TOKENS, D_MODEL), 1.0)
    a_w_in_first = nrm((D_MODEL, A_COLS_FIRST + MEM_WIDTH), d_in)
    a_w_in_rest = nrm((N_A_LAYERS - 1, D_MODEL, A_COLS_REST + MEM_WIDTH), d_in)
    a_mu_first = unif((A_COLS_FIRST,), 0.0, 1.0)
    a_mu_rest = unif((N_A_LAYERS - 1, A_COLS_REST), 0.0, 1.0)
    a_vec = jnp.stack([
        unif((N_A_LAYERS, MIX_WIDTH), -6.0, 1.0),
        nrm((N_A_LAYERS, MIX_WIDTH), 0.5),
        0.85 + nrm((N_A_LAYERS, MIX_WIDTH), 0.05),
        1.0 + nrm((N_A_LAYERS, MIX_WIDTH), 0.05),
        1.0 + nrm((N_A_LAYERS, MIX_WIDTH), 0.05),
        nrm((N_A_LAYERS, MIX_WIDTH), 0.01),
    ], axis=1)
    a_w_up = nrm((N_A_LAYERS, DECAY_LORA, MIX_WIDTH), 0.5 * DECAY_LORA ** -0.5)
    a_a_up = nrm((N_A_LAYERS, ICLR_LORA, MIX_WIDTH), ICLR_LORA ** -0.5)
    a_g_up = nrm((N_A_LAYERS, GATE_LORA, MIX_WIDTH), GATE_LORA ** -0.5)
    a_v0 = nrm((N_A_LAYERS - 1, MIX_WIDTH), 0.5)
    a_v_up = nrm((N_A_LAYERS - 1, VALUE_LORA, MIX_WIDTH), VALUE_LORA ** -0.5)
    a_r_k = nrm((N_A_LAYERS, MIX_HEADS, HEAD_DIM), 0.1)
    b_w_in = nrm((N_B_LAYERS, D_MODEL, MIX_WIDTH + MEM_WIDTH), d_in)
    w_kv_shared = nrm((D_MODEL, 2 * MIX_WIDTH), d_in)
    mem_kv = nrm((DEPTH, D_MODEL, 2 * MEM_WIDTH), d_in)
    w_o = nrm((DEPTH, MIX_WIDTH + MEM_WIDTH, D_MODEL), (MIX_WIDTH + MEM_WIDTH) ** -0.5 * DEEPNORM_BETA)
    ln = jnp.stack([
        1.0 + nrm((DEPTH, D_MODEL), 0.05), nrm((DEPTH, D_MODEL), 0.01),
        1.0 + nrm((DEPTH, D_MODEL), 0.05), nrm((DEPTH, D_MODEL), 0.01),
    ], axis=1)
    ffn_gate_up = nrm((N_DENSE, D_MODEL, 2 * D_FF), d_in)
    ffn_down = nrm((N_DENSE, D_FF, D_MODEL), D_FF ** -0.5 * DEEPNORM_BETA)
    router = nrm((N_MOE, D_MODEL, N_EXPERTS), d_in)
    exp_gate_up = nrm((N_MOE, N_EXPERTS, D_MODEL, 2 * D_FF), d_in)
    exp_down = nrm((N_MOE, N_EXPERTS, D_FF, D_MODEL), D_FF ** -0.5 * DEEPNORM_BETA)
    return {'x': x, 'mem': mem, 'a_w_in_first': a_w_in_first, 'a_w_in_rest': a_w_in_rest,
            'a_mu_first': a_mu_first, 'a_mu_rest': a_mu_rest, 'a_vec': a_vec, 'a_w_up': a_w_up,
            'a_a_up': a_a_up, 'a_g_up': a_g_up, 'a_v0': a_v0, 'a_v_up': a_v_up, 'a_r_k': a_r_k,
            'b_w_in': b_w_in, 'w_kv_shared': w_kv_shared, 'mem_kv': mem_kv, 'w_o': w_o, 'ln': ln,
            'ffn_gate_up': ffn_gate_up, 'ffn_down': ffn_down, 'router': router,
            'exp_gate_up': exp_gate_up, 'exp_down': exp_down}

def reference(x, mem, a_w_in_first, a_w_in_rest, a_mu_first, a_mu_rest, a_vec, a_w_up, a_a_up, a_g_up,
              a_v0, a_v_up, a_r_k, b_w_in, w_kv_shared, mem_kv, w_o, ln, ffn_gate_up, ffn_down,
              router, exp_gate_up, exp_down):
    v_first = None
    k_sh = None
    v_sh = None
    for l in range(DEPTH):
        if l < N_A_LAYERS:
            w_in = a_w_in_first if l == 0 else a_w_in_rest[l - 1]
            mu = a_mu_first if l == 0 else a_mu_rest[l - 1]
            v_gate = None if l == 0 else (a_v0[l - 1], a_v_up[l - 1])
            proj = x @ w_in
            n_cols = proj.shape[-1] - MEM_WIDTH
            q_mem = proj[..., n_cols:]
            tok, v_first = rwkv7_time_mix(proj[..., :n_cols], mu, a_vec[l], a_w_up[l], a_a_up[l],
                                          a_g_up[l], a_r_k[l], v_gate, v_first)
        else:
            proj = x @ b_w_in[l - N_A_LAYERS]
            q, q_mem = proj[..., :MIX_WIDTH], proj[..., MIX_WIDTH:]
            tok = stick_breaking_attention(split_heads(q), k_sh, v_sh)
        mo = memory_attention(q_mem, mem, mem_kv[l])
        mix = jnp.concatenate([tok, mo], axis=-1) @ w_o[l]
        x = layer_norm(DEEPNORM_ALPHA * x + mix, ln[l, 0], ln[l, 1])
        if l % 2 == 0:
            ff = swiglu(x, ffn_gate_up[l // 2], ffn_down[l // 2])
        else:
            ff = moe_swiglu(x, router[l // 2], exp_gate_up[l // 2], exp_down[l // 2])
        x = layer_norm(DEEPNORM_ALPHA * x + ff, ln[l, 2], ln[l, 3])
        if l == N_A_LAYERS - 1:
            kv = x @ w_kv_shared
            k_sh = split_heads(kv[..., :MIX_WIDTH])
            v_sh = split_heads(kv[..., MIX_WIDTH:])
    return x


_drawn_inputs = setup_inputs


def setup_inputs(seed=0):
    import zlib

    import numpy as np

    out = dict(_drawn_inputs(seed))
    spreads = {}
    factors = {'a_w_up': 4.809}
    for name, (base, spread) in spreads.items():
        noise = np.random.default_rng([zlib.crc32(name.encode()), seed]).standard_normal(out[name].shape)
        drawn = base * np.exp(spread * noise) if base else spread * noise
        out[name] = jnp.asarray(drawn.astype(out[name].dtype))
    for name, factor in factors.items():
        out[name] = (out[name] * factor).astype(out[name].dtype)
    return out
```

```python
from contextlib import ExitStack

import concourse.bass as bass
from concourse import mybir

F32 = mybir.dt.float32
F32R = mybir.dt.float32r
I32 = mybir.dt.int32
U32 = mybir.dt.uint32
ALU = mybir.AluOpType
ACT = mybir.ActivationFunctionType
AX_X = mybir.AxisListType.X

P = 128
T = 256
D = 1024
KT = D // P
NT = T // P
HEADS = 12
HD = 64
MIX = HEADS * HD
TILES = MIX // P
MEMH = 4
FF = 2816
FT = FF // P
EXPERTS = 8
EXTRA = 3
ALPHA = 4 ** 0.25
LN_EPS = 1e-5
GN_EPS = 64e-5
BETA = 0.6065306597126334
SCALE = HD ** -0.5

PIECE = 1024
PIECES = 6
SLOT = 3 * PIECE
SLOTS = 8
SEMS = 8


class Slab:

    def __init__(self, kind, loads, offset, size):
        self.kind, self.loads, self.offset, self.size = kind, loads, offset, size
        self.waits = 0
        self.first = None
        self.down = None


def plan_front(nslabs_before_ffn, nslabs_after_ffn):
    slabs = [Slab("A", None, 2 * PIECE * (n % 3), 2 * PIECE) for n in range(nslabs_before_ffn)]
    slabs += [Slab("B", None, SLOT * (n % 6), SLOT) for n in range(FT)]
    slabs += [Slab("A", None, SLOT * ((FT + n) % 6), 2 * PIECE) for n in range(nslabs_after_ffn)]
    pieces = []
    for n, s in enumerate(slabs):
        s.first = len(pieces)
        pieces += [(n, 0), (n, 1)]
        if s.kind == "B" and n > nslabs_before_ffn:
            slabs[n - 1].down = len(pieces)
            pieces.append((n - 1, 2))
        if s.kind == "B" and n == nslabs_before_ffn + FT - 1:
            s.down = len(pieces)
            pieces.append((n, 2))
    for n, s in enumerate(slabs):
        last = [m for m in range(n) if slabs[m].offset < s.offset + s.size and s.offset < slabs[m].offset + slabs[m].size]
        s.waits = max([max(slabs[m].first + 1, slabs[m].down or 0) + 1 for m in last], default=0)
    return slabs, pieces


def plan_pass():
    pieces = []
    for j in range(FT):
        pieces += [(j, 0), (j, 1)]
        if j >= 2:
            pieces.append((j - 2, 2))
    return pieces + [(FT - 2, 2), (FT - 1, 2)]


MOE_SLOT = [j % SLOTS for j in range(FT)]


def program(nc, x, mem, a_w_in_first, a_mu_first, a_vec, a_w_up, a_a_up, a_g_up, a_r_k, b_w_in,
            w_kv_shared, mem_kv, w_o, ln, ffn_gate_up, ffn_down, router, exp_gate_up, exp_down, out,
            dbg=None):
    with ExitStack() as ctx:
        def sem(name):
            return ctx.enter_context(nc.semaphore(name))

        base = nc.sbuf_base
        end = nc.sbuf_usable_end
        ctx.enter_context(nc.sbuf_tensor("arena", [P, (end - base) // 4 - 16], F32))
        base = (base + 31) // 32 * 32

        class Region:

            def __init__(self, at, limit):
                self.at, self.limit = at, limit

            def __call__(self, name, shape, dt=F32):
                n = 4
                for s in shape[1:]:
                    n *= s
                t = nc.alloc_sbuf_tensor_at(name, shape, dt, offset=self.at)
                self.at += (n + 31) // 32 * 32
                assert self.at <= self.limit, (name, self.at - self.limit)
                return t

        main = Region(base, end - 64)
        RAW = main("raw", [P, SLOTS * SLOT])
        WH = main("w_hi", [P, PIECES, PIECE], F32R)
        WL = main("w_lo", [P, PIECES, PIECE], F32R)
        X = main("x_tok", [P, NT, D])
        th_at = main.at
        TH = main("operand_hi", [P, KT, T], F32R)
        TL = main("operand_lo", [P, KT, T], F32R)
        gb_at = main.at
        GB = main("ln_rows", [P, 2, D])
        ID = main("ident", [P, P])
        SI = main("mask_after_upto", [P, 2, P])
        LS = main("mask_before", [P, P])
        BD = main("mask_blocks16", [P, P])
        LV = main("mask_levels", [P, 3, P])
        BO = main("ones_per_head", [P, P])
        NTRI = main("minus_suffix", [P, P])
        NONE = main("minus_ones", [P, P])
        IO = main("iota_row", [P, P])
        COLS = main("cols", [P, P])
        OMMU = main("one_minus_mu", [P, 20])
        OMKA = main("one_minus_ka", [P, 6])
        BN = main("bn", [P, NT, 2, 6])
        MV = main("mean_var", [P, NT, 2])
        RS = main("rstd", [P, NT])
        NM = main("minus_mean_rstd", [P, NT])
        EC = main("pow_exponent", [P, NT])
        SMX = main("smax", [P, MEMH, NT])
        SSM = main("ssum", [P, MEMH, NT])
        SRI = main("srecip", [P, MEMH, NT])
        EPS = main("eps", [P, 1])
        ONE = main("ones", [P, P])
        BM = main("mid", [P, 2, TILES, NT])
        WM = main("w_mid", [P, TILES])
        SC = main("state_scale", [P, TILES])
        mk_at = main.at
        MK = main("mem_keys", [P, 2, 2, T])
        MVA = main("mem_values", [P, 2, NT, T])
        free_at = main.at
        limit = end - 64

        l0 = Region(base + 4 * 2 * SLOT, base + 4 * SLOTS * SLOT)
        AR = l0("a_r", [P, TILES, NT, 2, P])
        BT = l0("b_scaled", [P, TILES, T])
        KK = l0("k_scaled", [P, TILES, T])
        V = l0("v_chan", [P, TILES, T])
        G = l0("gate", [P, TILES, T])
        CS = l0("decay_sum", [P, TILES, NT, P + 1])
        vt_at = l0.at
        VT = l0("v_tok", [P, NT, MIX])
        BKT = l0("bk_tok", [P, TILES, 2, P])
        Y = l0("y_tok", [P, NT, MIX])
        y_at = l0.at - 4 * NT * MIX
        S0 = l0("state", [P, TILES, HD])
        WUP = l0("wa_up", [P, MIX])
        GUP = l0("g_up", [P, MIX])
        WD = l0("wd_ad", [P, T])
        GD = l0("gd", [P, T])
        RN = nc.alloc_sbuf_tensor_at("rnorm", [P, TILES, T], F32, offset=y_at)
        YSQ = nc.alloc_sbuf_tensor_at("y_square", [P, NT, MIX], F32, offset=base + 4 * 2 * SLOT)
        memr = Region(vt_at, base + 4 * SLOTS * SLOT)
        MTH = memr("mem_hi", [P, KT, T], F32R)
        MTL = memr("mem_lo", [P, KT, T], F32R)
        TT = nc.alloc_sbuf_tensor_at("x_affine_chan", [P, 2, T], F32, offset=limit // 32 * 32 - 2048)
        small = Region(free_at, limit)
        QM = small("q_mem", [P, 2, T])
        lane_at = small.at
        ROWS = nc.alloc_sbuf_tensor_at("rows", [P, P], F32, offset=lane_at)
        EW = small("decay_to", [P, 2, NT, P + 1])
        EI = small("decay_from", [P, 2, NT, P])
        SQ = small("square", [P, 2, T])
        FM = small("k_factor", [P, 2, T])
        RK = small("rk", [P, 2, T])
        YT = nc.alloc_sbuf_tensor_at("y_norm_chan", [P, TILES, T], F32, offset=lane_at)
        GNS = nc.alloc_sbuf_tensor_at("gn_stats", [P, 4, NT, HEADS], F32, offset=lane_at + 4 * TILES * T)

        lanes = []
        for l in range(4):
            r = Region(th_at + 8192 * 0 + 6656 * l, limit) if l < 2 else Region(lane_at + 6656 * (l - 2), limit)
            lanes.append(dict(
                MR=r(f"mr{l}", [P, 2, P]), KR=r(f"kr{l}", [P, 2, P]), AL=r(f"al{l}", [P, P]),
                PX=r(f"px{l}", [P, 4, P]), LT=r(f"lt{l}", [P, 3, P]), Q1=r(f"q1{l}", [P, HD]), SA=r(f"sa{l}", [P, HD])))

        ma = Region(gb_at, gb_at + 8192)
        PR = ma("probs", [P, 2, NT, T])
        PT = ma("probs_t", [P, 2, NT, T])

        ff = Region(free_at, limit)
        FS = ff("ffn_silu", [P, NT, P])
        FH = ff("ffn_h", [P, NT, P])
        FHH = ff("ffn_ht_hi", [P, 2, T], F32R)
        FHL = ff("ffn_ht_lo", [P, 2, T], F32R)

        l1 = Region(base + 4 * 6 * SLOT, base + 4 * SLOTS * SLOT)
        KC = l1("k_chan", [P, TILES, T])
        VK = l1("vk_tok", [P, NT, MIX])
        QC = l1("q_chan", [P, TILES, T])
        QM1 = l1("q_mem1", [P, 2, T])
        l1t = Region(free_at, limit)
        SPA = l1t("softplus_a", [P, 2, 3, P])
        SP = l1t("softplus", [P, 2, 3, P])
        WT = l1t("weights_t", [P, 2, 3, P])

        me = Region(mk_at, limit)
        OH = me("out_hi", [P, 2, 512], F32R)
        OL = me("out_lo", [P, 2, 512], F32R)
        XGH = me("gathered_hi", [P, KT, P], F32R)
        XGL = me("gathered_lo", [P, KT, P], F32R)
        ES = me("exp_silu", [P, P])
        EH = me("exp_h", [P, P])
        EHH = me("exp_ht_hi", [P, 2, P], F32R)
        EHL = me("exp_ht_lo", [P, 2, P], F32R)
        DI = me("dispatch", [P, NT, P], F32R)
        DTN = me("dispatch_t_next", [P, NT, P], F32R)
        DTC = me("dispatch_t", [P, NT, P], F32R)
        NP = EXPERTS + EXTRA + 1
        RKP = me("rank_of_pass", [P, NT, NP])
        SLP = me("selected_of_pass", [P, NT, NP])
        CBP = me("weight_of_pass", [P, NT, NP])
        NUI = me("extras_int", [P, 4], I32)
        CPC = me("combine_of_slot_tok", [P, NT])
        CWN = me("slot_weight_next", [P, 1])
        CWC = me("slot_weight", [P, 1])
        ro = Region(free_at, free_at + 8192)
        LG = ro("logits", [P, NT, 8])
        MX8 = ro("top8", [P, NT, 8])
        IX8 = ro("top8_index", [P, NT, 8], U32)
        IXF = ro("top_index", [P, NT, 8])
        W12 = ro("top_weights", [P, NT, 4])
        OH1 = ro("one_hot1", [P, NT, 8])
        OH2 = ro("one_hot2", [P, NT, 8])
        SEL = ro("selected", [P, NT, 8])
        CMB = ro("combine", [P, NT, 8])
        RK8 = ro("rank", [P, NT, 8])
        OVR = ro("over", [P, 8])
        POS = ro("over_position", [P, 8])
        EXJ = ro("extra_is", [P, EXTRA, 8])
        PRD = ro("extra_products", [P, EXTRA, 3, NT, 8])
        PRE = ro("extra_index_products", [P, EXTRA, 8])
        ROW8 = IO[:, 0:EXPERTS]
        NUM = ro("extras", [P, 4])
        RTH = ro("router_raw", [P, KT, 8])
        RHI = ro("router_hi", [P, KT, 8], F32R)
        RLO = ro("router_lo", [P, KT, 8], F32R)

        bank = [ctx.enter_context(nc.psum_tensor(f"bank{b}", [P, 512], F32)) for b in range(8)]

        small_in = sem("small_in")
        mem_in, x_in = sem("mem_in"), sem("x_in")
        rows_in = sem("rows_in")
        router_in = sem("router_in")
        raw_in = [sem(f"raw_in{s}") for s in range(SEMS)]
        hi_done, lo_done, piece_used = sem("hi_done"), sem("lo_done"), sem("piece_used")
        consts_ready, cols_ready, mem_operand = sem("consts_ready"), sem("cols_ready"), sem("mem_operand")
        misc_ready, misc_act, misc_dve = sem("misc_ready"), sem("misc_act"), sem("misc_dve")
        a_ready, a_act, a_dve = sem("a_ready"), sem("a_act"), sem("a_dve")
        act_chain, dve_chain, pool_chain = sem("act_chain"), sem("dve_chain"), sem("pool_chain")
        lora_in_ready = sem("lora_in_ready")
        decay_ready, exp_ready, exp_used = sem("decay_ready"), sem("exp_ready"), sem("exp_used")
        square_ready, norm_sqrt, rk_ready = sem("square_ready"), sem("norm_sqrt"), sem("rk_ready")
        prep_done = sem("prep_done")
        lane_mm = [sem(f"lane_mm{l}") for l in range(4)]
        lane_act = [sem(f"lane_act{l}") for l in range(4)]
        lane_dve = [sem(f"lane_dve{l}") for l in range(4)]
        lane_pool = [sem(f"lane_pool{l}") for l in range(4)]
        state_ready = sem("state_ready")
        y_sqrt, y_ready, yt_bonus, yt_gated = sem("y_sqrt"), sem("y_ready"), sem("yt_bonus"), sem("yt_gated")
        y_var = sem("y_var")
        smax_ready, probs_ready, pt_ready = sem("smax_ready"), sem("probs_ready"), sem("pt_ready")
        psum_ready = sem("softmax_sum_ready")
        attn_hi = sem("attn_hi")
        res_ready, stats_ready, rstd_ready, xn_act, xn_dve = (sem("res_ready"), sem("stats_ready"), sem("rstd_ready"),
                                                              sem("xn_act"), sem("xn_dve"))
        x_ready = sem("x_ready")
        tr_hi = sem("tr_hi")
        gu_ready, silu_ready, h_ready, ht_ready, ht_hi, ht_lo = (sem("gu_ready"), sem("silu_ready"), sem("h_ready"),
                                                                 sem("ht_ready"), sem("ht_hi"), sem("ht_lo"))
        ffn_out = sem("ffn_out")
        stick_sp, stick_masked, cs_ready, stick_exp, stick_w, stick_ln = (sem("stick_sp"), sem("stick_masked"), sem("cs_ready"),
                                                                sem("stick_exp"), sem("stick_w"), sem("stick_ln"))
        x2_hi, x2_split = sem("x2_hi"), sem("x2_split")
        y_start = sem("y_start")
        top_ready, route_ready = sem("top_ready"), sem("route_ready")
        router_hi, router_split = sem("router_hi"), sem("router_split")
        eg_ready, es_ready, eh_ready, et_ready, eth_hi, eth_lo = (sem("eg_ready"), sem("es_ready"), sem("eh_ready"),
                                                                  sem("et_ready"), sem("eth_hi"), sem("eth_lo"))
        disp_ready, ring2_ready, ring2_free = sem("dispatch_ready"), sem("pair_ready"), sem("pair_free")
        out_hi_s, out_lo_s = sem("out_hi_ready"), sem("out_lo_ready")
        ring_act, ring_dve = sem("ring_emptied_act"), sem("ring_emptied_dve")
        cur_ready = sem("current_ready")
        top_diff, top_exp = sem("top_diff"), sem("top_exp")
        rank_ready, logits_ready = sem("rank_ready"), sem("logits_ready")
        cat_hi, cat_ready = sem("cat_hi"), sem("cat_ready")
        final_ready, stored = sem("final_ready"), sem("stored")

        A_BEFORE, A_AFTER = 19, 14
        slabs, pieces = plan_front(A_BEFORE, A_AFTER)
        NF = len(pieces)
        A_IDX = list(range(A_BEFORE)) + list(range(A_BEFORE + FT, len(slabs)))
        B0 = A_BEFORE
        W_ORDER = [9, 0, 1, 2, 3, 4, 5, 6, 7, 8, 10]

        def cols256(w, c):
            return w.rearrange("(k p) c -> p k c", p=P)[:, :, 256 * c:256 * c + 256]

        srcs = [cols256(mem_kv[0], 0), cols256(mem_kv[0], 1), cols256(mem_kv[1], 0), cols256(mem_kv[1], 1)]
        srcs += [cols256(a_w_in_first, c) for c in W_ORDER]
        srcs += [cols256(w_o[0], c) for c in range(4)]
        srcs += [cols256(w_kv_shared, c) for c in range(6)]
        srcs += [cols256(b_w_in[0], c) for c in range(4)]
        srcs += [cols256(w_o[1], c) for c in range(4)]

        def raw_a(off):
            return RAW[:, off:off + 2 * PIECE].rearrange("p (k c) -> p k c", k=KT)

        def raw_gu(off):
            return RAW[:, off:off + 2 * PIECE].rearrange("p (k g c) -> p k g c", k=KT, g=2)

        def gate_up(w):
            return w.rearrange("(k p) (g c) -> p k g c", p=P, g=2)

        for n, s in enumerate(A_IDX):
            slabs[s].loads = [(raw_a(slabs[s].offset), srcs[n])]
        for f in range(FT):
            s = slabs[B0 + f]
            w = gate_up(ffn_gate_up[0])
            s.loads = [(raw_gu(s.offset)[:, :, g, :], w[:, :, g, P * f:P * f + P]) for g in range(2)]
            s.loads.append((RAW[:, s.offset + 2 * PIECE:s.offset + SLOT], ffn_down[0, P * f:P * f + P, :]))
        sem_count = [0] * SEMS
        for n, s in enumerate(slabs):
            sem_count[n % SEMS] += 16 * len(s.loads)
            s.sem, s.count = raw_in[n % SEMS], sem_count[n % SEMS]
        MOE_BASE = list(sem_count)
        PER_PASS = [48 * MOE_SLOT.count(s) for s in range(SLOTS)]
        pass_pieces = plan_pass()
        PP = len(pass_pieces)
        DOWN_AT = {j: pass_pieces.index((j, 2)) for j in range(FT)}
        GU_AT = {j: pass_pieces.index((j, 0)) for j in range(FT)}
        last_use = {}
        for n, s in enumerate(slabs):
            for slot in range(SLOTS):
                if s.offset < SLOT * (slot + 1) and SLOT * slot < s.offset + s.size:
                    last_use[slot] = max(last_use.get(slot, 0), (s.down or s.first + 1) + 1)

        A_KIND = ["act"] * 4 + ["both"] * 10 + ["act"] + ["dve"] * 4 + ["act"] * 10 + ["dve"] * 4
        A_ACT = [sum(k in ("act", "both") for k in A_KIND[:n + 1]) for n in range(len(A_KIND))]
        A_DVE = [sum(k in ("dve", "both") for k in A_KIND[:n + 1]) for n in range(len(A_KIND))]

        uses = [("cols", 0, "dve")]
        uses += [("tr0", q, "dve") for q in range(4)] + [("tr1", q, "dve") for q in range(4)]
        for i in range(TILES):
            uses += [("up", i, "act"), ("gate", i, "act")]
        uses += [("norm", i, "dve") for i in range(TILES)]
        for i in range(TILES):
            uses += [("vt", i, "act"), ("bonus", i, "dve")]
        uses += [("bk", i, "act") for i in range(TILES)]

        def mem_uses(l):
            u = []
            for h in range(MEMH):
                if h == 0:
                    u += [(f"s{l}", 0, "act")]
                if h + 1 < MEMH:
                    u += [(f"s{l}", h + 1, "act")]
                u += [(f"pt{l}", h, "dve")]
                if h % 2:
                    u += [(f"mo{l}", h // 2, "dve")]
            return u

        uses += mem_uses(0)
        uses += [("yt", i, "act") for i in range(TILES)]
        uses += [("tr2", q, "dve") for q in range(4)]
        N_BEFORE_FFN = len(uses)
        uses += [("tr3", q, "dve") for q in range(4)]
        for s in range(HEADS + 2):
            if s < HEADS:
                uses.append(("z", s, "act"))
            if s >= 2 and s % 2 == 0:
                uses.append(("so", (s - 2) // 2, "dve"))
        uses += mem_uses(1)
        uses += [("tr4", q, "dve") for q in range(4)]
        USE = {(n, i): u for u, (n, i, _) in enumerate(uses)}

        def use_bank(name, i):
            return bank[2 + USE[name, i] % 6]

        def emptied(u):
            who = uses[u][2]
            return (misc_act if who == "act" else misc_dve), sum(w == who for _, _, w in uses[:u + 1])

        def wait_ready(eng, name, i):
            eng.wait_ge(misc_ready, USE[name, i] + 1)

        def wait_emptied(eng, name, i):
            eng.wait_ge(*emptied(USE[name, i]))

        def wait_bank(eng, name, i):
            u = USE[name, i]
            if u >= 6:
                eng.wait_ge(*emptied(u - 6))

        MU, VEC, RKC, LNC = 0, 20, 56, 62

        def col(n):
            return COLS[:, n:n + 1]

        def lncol(l, v, k):
            return col(LNC + 32 * l + 8 * v + k)

        NG = HEADS * NT // 4
        MM_N, ACT_N, DVE_N, POOL_N = 14, 10, 9, 4

        def job(g, l):
            return 4 * (g % 3) + l, g // 3

        RING = ["dve"] * 4 + ["act"] * 2 + ["dve"] * 2 + ["act"] * 2
        RING_ACT0, RING_DVE0, RING_ACT, RING_DVE = 4, 2, 4, 6
        RING0 = RING_ACT0 + RING_DVE0

        NONE_BEFORE = -1
        MOE_H0 = 2

        def ring_bank(r):
            return bank[5 + r % 2]

        def ring_count(p, r):
            n = sum(w == RING[r] for w in RING[:r + 1])
            if RING[r] == "act":
                return ring_act, p * RING_ACT + (RING_ACT0 + n)
            return ring_dve, p * RING_DVE + (RING_DVE0 + n)

        def ring_ready(p, r):
            return p * len(RING) + (RING0 + r + 1)

        XH = TH[:, :, :].rearrange("p k t -> p (k t)")
        XL = TL[:, :, :].rearrange("p k t -> p (k t)")

        def silu_view(b):
            return b[:, :].rearrange("p (t g c) -> p t g c", t=NT, g=2)

        block = ctx.enter_context(nc.Block())

        def which_ln(idx):
            return idx // 2, 2 * (idx % 2)

        @block.sync
        def _(sp):
            rows = ROWS[0:126, :]
            sp.dma_start(rows[0:20, :], a_mu_first.rearrange("(a p) -> a p", p=P)).then_inc(small_in, 16)
            sp.dma_start(rows[20:56, :], a_vec[0].rearrange("v (a p) -> (v a) p", p=P)).then_inc(small_in, 16)
            sp.dma_start(rows[56:62, :], a_r_k[0].rearrange("(a h) d -> a (h d)", h=2)).then_inc(small_in, 16)
            sp.dma_start(rows[62:126, :], ln.rearrange("l v (a p) -> (l v a) p", p=P)).then_inc(small_in, 16)
            sp.dma_start(GB[:, :, :], mem[0].rearrange("(t p) d -> p t d", p=P)).then_inc(mem_in, 16)
            sp.dma_start(X[:, :, :], x[0].rearrange("(t p) d -> p t d", p=P)).then_inc(x_in, 16)
            sp.dma_start(WUP[0:64, :], a_w_up[0]).then_inc(small_in, 16)
            sp.dma_start(WUP[64:128, :], a_a_up[0]).then_inc(small_in, 16)
            sp.dma_start(GUP[:, :], a_g_up[0]).then_inc(small_in, 16)

            def rows_of(idx):
                l, v = which_ln(idx)
                for r in range(2):
                    sp.dma_start(GB[:, r, :], ln[l, v + r].rearrange("(a d) -> a d", a=1).broadcast_to([P, D]))\
                        .then_inc(rows_in, 16)

            def load(n):
                s = slabs[n]
                if s.waits:
                    sp.wait_ge(lo_done, s.waits)
                for dst, src in s.loads:
                    sp.dma_start(dst, src).then_inc(s.sem, 16)

            for n in range(B0 + 2):
                if n == B0 + 0:
                    wait_emptied(sp, "mo0", 1)
                    rows_of(0)
                load(n)
            sp.wait_ge(yt_gated, TILES)
            for n in range(B0 + 2, len(slabs)):
                load(n)
                if n == B0 + 10:
                    sp.wait_ge(x_ready, 1)
                    rows_of(1)
            sp.wait_ge(x_ready, 2)
            wait_emptied(sp, "mo1", 1)
            rows_of(2)
            sp.dma_start(RTH[:, :, :], router[0].rearrange("(k p) e -> p k e", p=P)).then_inc(router_in, 16)

            def pass_loads(p, e):
                for j in range(FT):
                    s = MOE_SLOT[j]
                    before = [m for m in range(j) if MOE_SLOT[m] == s]
                    if before:
                        sp.wait_ge(lo_done, NF + PP * p + DOWN_AT[before[-1]] + 1)
                    else:
                        m = max(m for m in range(FT) if MOE_SLOT[m] == s)
                        sp.wait_ge(lo_done, NF + PP * (p - 1) + DOWN_AT[m] + 1)
                    off = SLOT * s
                    w = exp_gate_up[0].rearrange("e (k p) (g c) -> e p k g c", p=P, g=2)
                    for g in range(2):
                        sp.dma_start(raw_gu(off)[:, :, g, :], w[e, :, :, g, P * j:P * j + P]).then_inc(raw_in[s], 16)
                    sp.dma_start(RAW[:, off + 2 * PIECE:off + SLOT], exp_down[0][e, P * j:P * j + P, :]).then_inc(raw_in[s], 16)

            sp.wait_ge(lo_done, max(last_use[s] for s in range(6)))
            wait_emptied(sp, "mo1", 1)
            with sp.Fori(0, EXPERTS) as e:
                pass_loads(e, e)
            sp.wait_ge(route_ready, 1)
            n_extra = sp.value_load(NUI[0:1, 0:1], min_val=0, max_val=EXTRA)
            for j in range(EXTRA):
                with sp.If(n_extra > j):
                    e = sp.value_load(NUI[0:1, 1 + j:2 + j], min_val=0, max_val=EXPERTS - 1)
                    pass_loads(EXPERTS + j, e)
            sp.wait_ge(ring_dve, RING_DVE0 + RING_DVE * (n_extra + EXPERTS) + 4)
            rows_of(3)
            for t in range(NT):
                sp.wait_ge(*((final_ready, 1) if t == 0 else (x_ready, 4)))
                sp.dma_start(out[0, P * t:P * t + P, :], X[:, t, :]).then_inc(stored, 16)
            sp.wait_ge(stored, 16 * NT)


        @block.tensor
        def _(pe):
            def mm(out, lhsT, rhs, start=True, stop=True):
                return nc.tensor.matmul(out, lhsT, rhs, start=start, stop=stop, skip_group_check=True)

            def product(out, lh, ll, rh, rl, start, stop):
                mm(out, lh, rh, start, False)
                mm(out, lh, rl, False, False)
                return mm(out, ll, rh, False, stop)

            def transposes(name, src):
                for q in range(4):
                    wait_bank(pe, name, q)
                    b = use_bank(name, q)
                    for k in range(2):
                        for t in range(NT):
                            last = nc.tensor.transpose(b[:, k * T + t * P:k * T + t * P + P],
                                                       src[:, t, (2 * q + k) * P:(2 * q + k + 1) * P], ID[:, :])
                    last.then_inc(misc_ready, 1)

            def a_slab(a, channels, oh, ol):
                s = slabs[A_IDX[a]]
                if a >= 2:
                    if A_KIND[a - 2] != "dve":
                        pe.wait_ge(a_act, A_ACT[a - 2])
                    if A_KIND[a - 2] != "act":
                        pe.wait_ge(a_dve, A_DVE[a - 2])
                for pc in range(2):
                    q = s.first + pc
                    pe.wait_ge(lo_done, q + 1)
                    wh = WH[:, q % PIECES, :].rearrange("p (k c) -> p k c", k=4)
                    wl = WL[:, q % PIECES, :].rearrange("p (k c) -> p k c", k=4)
                    for kk in range(4):
                        k = 4 * pc + kk
                        for m in range(2):
                            o = bank[a % 2][:, T * m:T * m + T]
                            cut = slice(P * m, P * m + P)
                            first = k == 0 and m == 0
                            if channels:
                                last = product(o, wh[:, kk, cut], wl[:, kk, cut], oh[:, k, :], ol[:, k, :],
                                               first, k == KT - 1)
                            else:
                                last = product(o, oh[:, k, cut], ol[:, k, cut], wh[:, kk, :], wl[:, kk, :],
                                               first, k == KT - 1)
                    last.then_inc(piece_used, 1)

            pe.wait_ge(consts_ready, 1)
            pe.wait_ge(small_in, 7 * 16)
            nc.tensor.transpose(use_bank("cols", 0)[:, 0:126], ROWS[0:126, :], ID[0:126, 0:126]).then_inc(misc_ready, 1)
            pe.wait_ge(mem_in, 16)
            transposes("tr0", GB)
            wait_emptied(pe, "tr0", 3)
            for a in range(4):
                a_slab(a, a % 2 == 0, MTH, MTL)

            pe.wait_ge(x_in, 16)
            transposes("tr1", X)
            wait_emptied(pe, "tr1", 3)

            def lora(i):
                cut = slice(P * i, P * i + P)
                wait_bank(pe, "up", i)
                b = use_bank("up", i)
                mm(b[:, 0:T], WUP[0:HD, cut], WD[0:HD, :]).then_inc(misc_ready, 1)
                wait_bank(pe, "gate", i)
                mm(use_bank("gate", i)[:, T:2 * T], WUP[HD:P, cut], WD[HD:P, :])
                mm(use_bank("gate", i)[:, 0:T], GUP[:, cut], GD[:, :]).then_inc(misc_ready, 1)

            def norm(i):
                pe.wait_ge(square_ready, i + 1)
                wait_bank(pe, "norm", i)
                mm(use_bank("norm", i)[:, 0:T], BO[:, :], SQ[:, i % 2, :]).then_inc(misc_ready, 1)

            for a in range(4, 15):
                a_slab(a, True, TH, TL)
                if 5 <= a <= 7:
                    pe.wait_ge(lora_in_ready, 2)
                    for i in (2 * a - 10, 2 * a - 9):
                        lora(i)
                if 9 <= a <= 11:
                    for i in (2 * a - 18, 2 * a - 17):
                        norm(i)
            for i in range(TILES):
                pe.wait_ge(a_dve, A_DVE[13])
                wait_bank(pe, "vt", i)
                b = use_bank("vt", i)
                for c in range(NT):
                    last = nc.tensor.transpose(b[:, P * c:P * c + P], V[:, i, P * c:P * c + P], ID[:, :])
                last.then_inc(misc_ready, 1)
                pe.wait_ge(rk_ready, i + 1)
                wait_bank(pe, "bonus", i)
                mm(use_bank("bonus", i)[:, 0:T], BO[:, :], RK[:, i % 2, :]).then_inc(misc_ready, 1)
            for i in range(TILES):
                pe.wait_ge(exp_used, i + 1)
                wait_bank(pe, "bk", i)
                b = use_bank("bk", i)
                nc.tensor.transpose(b[:, 0:P], BT[:, i, 0:P], ID[:, :])
                nc.tensor.transpose(b[:, P:2 * P], KK[:, i, 0:P], ID[:, :]).then_inc(misc_ready, 1)

            wait_emptied(pe, "bk", TILES - 1)
            wait_emptied(pe, "bonus", TILES - 1)
            pe.wait_ge(a_act, A_ACT[14])
            for g in range(NG):
                for step in range(1, MM_N + 1):
                    for l in range(4):
                        h, c = job(g, l)
                        L = lanes[l]
                        i, hb = h // 2, HD * (h % 2)
                        rows = slice(hb, hb + HD)
                        PX = L["PX"]
                        b, other = bank[2 * l + step % 2], bank[2 * l + 1 - step % 2]
                        xt = PX[:, 2:4, :].rearrange("p a c -> p (a c)")

                        def act_at(n):
                            pe.wait_ge(lane_act[l], ACT_N * g + n)

                        def dve_at(n):
                            pe.wait_ge(lane_dve[l], DVE_N * g + n)

                        def pool_at(n):
                            pe.wait_ge(lane_pool[l], POOL_N * g + n)

                        if step == 1:
                            if g:
                                act_at(0)
                                dve_at(0)
                            ar = AR[rows, i, c, :, :].rearrange("p a c -> p (a c)")
                            tok = slice(P * c, P * c + P)
                            mm(bank[2 * l][:, 0:T], BT[rows, i, tok], ar)
                            mm(bank[2 * l][:, T:2 * T], KK[rows, i, tok], ar)
                            last = mm(bank[2 * l + 1][:, 0:P], AR[rows, i, c, 0, :], BT[rows, i, tok])
                        elif step == 2:
                            dve_at(3)
                            pool_at(3)
                            mm(b[:, 0:P], PX[:, 1, :], PX[:, 0, :])
                            last = mm(b[:, P:2 * P], PX[:, 0, :], PX[:, 1, :])
                        elif step in (3, 4):
                            act_at(step - 2)
                            if step == 4:
                                dve_at(4)
                            mm(b[:, 0:P], PX[:, 1, :], PX[:, 0, :])
                            mm(b[:, P:2 * P], PX[:, 0, :], PX[:, 1, :])
                            last = mm(other[:, 0:P], PX[:, 0, :], PX[:, 2, :])
                        elif step == 5:
                            act_at(3)
                            dve_at(5)
                            mm(b[:, 0:P], PX[:, 0, :], PX[:, 2, :])
                            if c:
                                pe.wait_ge(state_ready, h + 1)
                            last = mm(other[:, 0:HD], L["KR"][:, 0, :], VT[:, c, HD * h:HD * h + HD], True, c == 0)
                            if c:
                                last = mm(other[:, 0:HD], AR[rows, i, c, 0, :], S0[rows, i, :], False, True)
                        elif step == 6:
                            dve_at(6)
                            act_at(4)
                            last = nc.tensor.transpose(b[:, 0:P], PX[:, 2, :], ID[:, :])
                        elif step in (7, 9, 11):
                            lev = (step - 7) // 2
                            if step == 7:
                                pool_at(4)
                            else:
                                dve_at(6 + lev)
                            last = mm(b[:, 0:P], L["LT"][:, lev, :], PX[:, 2, :])
                        elif step in (8, 10, 12):
                            lev = (step - 8) // 2
                            act_at(6 + lev)
                            last = mm(b[:, 0:P], PX[:, 3, :], PX[:, 0, :])
                            if step < 12:
                                last = mm(b[:, P:2 * P], PX[:, 0, :], PX[:, 3, :])
                        elif step == 13:
                            dve_at(9)
                            last = mm(b[:, 0:HD], PX[:, 2, :], L["Q1"][:, :])
                        else:
                            act_at(9)
                            vt = VT[:, c, HD * h:HD * h + HD]
                            mm(b[:, 0:HD], L["MR"][:, 1, :], L["SA"][:, :], True, False)
                            last = mm(b[:, 0:HD], L["KR"][:, 1, :], vt, False, c == 0)
                            if c:
                                last = mm(b[:, 0:HD], AR[rows, i, c, 1, :], S0[rows, i, :], False, True)
                            else:
                                mm(b[rows, HD:2 * HD], BKT[:, i, 0, rows], L["SA"][:, :], True, False)
                                last = mm(b[rows, HD:2 * HD], BKT[:, i, 1, rows], vt, False, True)
                        last.then_inc(lane_mm[l], 1)
            for l in range(4):
                pe.wait_ge(lane_act[l], ACT_N * NG)

            def mem_attention(l, q):
                def scores(h):
                    i, hb = h // 2, HD * (h % 2)
                    wait_bank(pe, f"s{l}", h)
                    b = use_bank(f"s{l}", h)
                    for t in range(NT):
                        last = mm(b[:, T * t:T * t + T], q[hb:hb + HD, i, P * t:P * t + P], MK[hb:hb + HD, l, i, :])
                    last.then_inc(misc_ready, 1)

                for h in range(MEMH):
                    i, hb = h // 2, HD * (h % 2)
                    if h == 0:
                        scores(0)
                    if h + 1 < MEMH:
                        scores(h + 1)
                    pe.wait_ge(probs_ready, MEMH * l + h + 1)
                    wait_bank(pe, f"pt{l}", h)
                    b = use_bank(f"pt{l}", h)
                    for mt in range(2):
                        for t in range(NT):
                            last = nc.tensor.transpose(b[:, T * mt + P * t:T * mt + P * t + P],
                                                       PR[:, h % 2, t, P * mt:P * mt + P], ID[:, :])
                    last.then_inc(misc_ready, 1)
                    wait_emptied(pe, f"pt{l}", h)
                    if h % 2 == 0:
                        wait_bank(pe, f"mo{l}", i)
                    b = use_bank(f"mo{l}", i)
                    for mt in range(2):
                        last = mm(b[hb:hb + HD, 0:T], MVA[:, l, mt, HD * h:HD * h + HD], PT[:, h % 2, mt, :],
                                  mt == 0, mt == 1)
                    if h % 2:
                        last.then_inc(misc_ready, 1)

            mem_attention(0, QM)
            pe.wait_ge(y_ready, 1)
            for i in range(TILES):
                wait_bank(pe, "yt", i)
                b = use_bank("yt", i)
                for c in range(NT):
                    last = nc.tensor.transpose(b[:, P * c:P * c + P], Y[:, c, P * i:P * i + P], ID[:, :])
                last.then_inc(misc_ready, 1)
            pe.wait_ge(cat_ready, TILES)
            for a in range(15, 19):
                a_slab(a, False, TH, TL)

            def normed(idx, name):
                pe.wait_ge(xn_dve, idx + 1)
                pe.wait_ge(xn_act, idx + 1)
                transposes(name, X)
                wait_emptied(pe, name, 3)

            normed(0, "tr2")

            pe.wait_ge(a_dve, A_DVE[18])
            for f in range(FT + 1):
                if f < FT:
                    s = slabs[B0 + f]
                    if f >= 2:
                        pe.wait_ge(h_ready, f - 1)
                for pc in range(2):
                    if f < FT:
                        q = s.first + pc
                        pe.wait_ge(lo_done, q + 1)
                        wh = WH[:, q % PIECES, :].rearrange("p (k c) -> p k c", k=4)
                        wl = WL[:, q % PIECES, :].rearrange("p (k c) -> p k c", k=4)
                        for kk in range(4):
                            k = 4 * pc + kk
                            for t in range(NT):
                                cut = slice(P * t, P * t + P)
                                last = product(bank[f % 2][:, T * t:T * t + T], TH[:, k, cut], TL[:, k, cut],
                                               wh[:, kk, :], wl[:, kk, :], k == 0 and t == 0, k == KT - 1)
                        last.then_inc(piece_used, 1)
                    if pc == 0 and f:
                        pe.wait_ge(h_ready, f)
                        if f >= 3:
                            pe.wait_ge(ht_lo, f - 2)
                        b = bank[6 + (f - 1) % 2]
                        for t in range(NT):
                            last = nc.tensor.transpose(b[:, P * t:P * t + P], FH[:, t, :], ID[:, :])
                        last.then_inc(ht_ready, 1)
                if f:
                    pe.wait_ge(ht_lo, f)
                    q = slabs[B0 + f - 1].down
                    pe.wait_ge(lo_done, q + 1)
                    for t in range(NT):
                        cut = slice(P * t, P * t + P)
                        for half in range(2):
                            n = slice(512 * half, 512 * half + 512)
                            last = product(bank[2 + 2 * t + half][:, :], FHH[:, (f - 1) % 2, cut], FHL[:, (f - 1) % 2, cut],
                                           WH[:, q % PIECES, n], WL[:, q % PIECES, n], f == 1, f == FT)
                    last.then_inc(piece_used, 1)

            pe.wait_ge(ffn_out, 4)
            normed(1, "tr3")
            for a in range(19, 29):
                a_slab(a, a not in (22, 23, 24), TH, TL)
            pe.wait_ge(a_act, A_ACT[28])

            for s in range(HEADS + 2):
                if s < HEADS:
                    h = s
                    i, rows = h // 2, slice(HD * (h % 2), HD * (h % 2) + HD)
                    wait_bank(pe, "z", h)
                    b = use_bank("z", h)
                    mm(b[:, 0:T], KC[rows, i, 0:P], QC[rows, i, :], True, False)
                    mm(b[:, T:T + P], KC[rows, i, P:T], QC[rows, i, P:T], False, False).then_inc(misc_ready, 1)
                if 1 <= s <= HEADS:
                    h = s - 1
                    b = use_bank("z", h)
                    pe.wait_ge(stick_masked, h + 1)
                    sp_ = SP[:, h % 2, :, :].rearrange("p a c -> p (a c)")
                    mm(b[:, 0:T], NTRI[:, :], sp_[:, 0:T], False, False)
                    mm(b[:, P:T], NONE[:, :], sp_[:, T:T + P], False, False)
                    mm(b[:, T:T + P], NTRI[:, :], sp_[:, T:T + P], False, True).then_inc(cs_ready, 1)
                if s >= 2:
                    h = s - 2
                    i, rows = h // 2, slice(HD * (h % 2), HD * (h % 2) + HD)
                    if h % 2 == 0:
                        wait_bank(pe, "so", i)
                    b = use_bank("so", i)
                    pe.wait_ge(stick_w, h + 1)
                    wt = WT[:, h % 2, :, :].rearrange("p a c -> p (a c)")
                    mm(b[rows, 0:T], VK[:, 0, HD * h:HD * h + HD], wt[:, 0:T], True, False)
                    last = mm(b[rows, P:T], VK[:, 1, HD * h:HD * h + HD], wt[:, T:T + P], False, True)
                    if h % 2:
                        last.then_inc(misc_ready, 1)
            mem_attention(1, QM1)
            wait_emptied(pe, "mo1", 1)
            for a in range(29, 33):
                a_slab(a, False, TH, TL)
            normed(2, "tr4")

            pe.wait_ge(router_split, 1)
            pe.wait_ge(a_dve, A_DVE[32])
            for t in range(NT):
                cut = slice(P * t, P * t + P)
                for k in range(KT):
                    last = product(bank[0][:, 8 * t:8 * t + 8], TH[:, k, cut], TL[:, k, cut], RHI[:, k, :], RLO[:, k, :],
                                   k == 0 and t == 0, k == KT - 1)
            last.then_inc(logits_ready, 1)
            pe.wait_ge(top_ready, 1)
            mm(bank[1][:, 0:8], SI[:, 0, :], SEL[:, 0, :])
            mm(bank[1][:, 8:16], SI[:, 0, :], SEL[:, 1, :], False, False)
            mm(bank[1][:, 8:16], ONE[:, :], SEL[:, 0, :], False, True)
            mm(bank[1][:, 16:24], ONE[:, :], SEL[:, 0, :], False, False)
            mm(bank[1][:, 16:24], ONE[:, :], SEL[:, 1, :], False, True).then_inc(rank_ready, 1)

            def gather(p):
                for r in range(4, 8):
                    src = XH if r < 6 else XL
                    if r >= 6 or p is not NONE_BEFORE:
                        pe.wait_ge(*ring_count(p, r - 2))
                    b = ring_bank(r)
                    for d in range(4):
                        for t in range(NT):
                            at = D * t + P * (4 * (r % 2) + d)
                            last = mm(b[:, P * d:P * d + P], src[:, at:at + P], DI[:, t, :], d == 0 and t == 0, t == NT - 1)
                    last.then_inc(ring2_ready, 1)
                pe.wait_ge(*ring_count(p, 6))
                for t in range(NT):
                    last = nc.tensor.transpose(ring_bank(8)[:, P * t:P * t + P], DI[:, t, :].bitcast(F32), ID[:, :])
                last.then_inc(ring2_ready, 1)
                pe.wait_ge(*ring_count(p, 7))
                for t in range(NT):
                    last = mm(ring_bank(9)[:, 0:1], DI[:, t, :].bitcast(F32), CPC[:, t:t + 1], t == 0, t == NT - 1)
                last.then_inc(ring2_ready, 1)

            def scatter(p):
                pe.wait_ge(out_lo_s, 2 * p + 2)
                for r in range(4):
                    t, half = r // 2, r % 2
                    if r < 2:
                        pe.wait_ge(*ring_count(p - 1, 8 + r))
                    else:
                        pe.wait_ge(*ring_count(p, r - 2))
                    mm(ring_bank(r)[:, :], DTC[:, t, :], OH[:, half, :], True, False)
                    mm(ring_bank(r)[:, :], DTC[:, t, :], OL[:, half, :], False, True).then_inc(ring2_ready, 1)

            def expert(p):
                for j in range(FT + 2):
                    if j < FT:
                        pe.wait_ge(eh_ready, p * FT + (j - 1 + MOE_H0))
                        if j == 0:
                            pe.wait_ge(*ring_count(p - 1, 5))
                            pe.wait_ge(*ring_count(p - 1, 7))
                    for pc in range(2):
                        if j < FT:
                            r = GU_AT[j] + pc
                            pe.wait_ge(lo_done, p * PP + (NF + r + 1))
                            wh = WH[:, r % PIECES, :].rearrange("p (k c) -> p k c", k=4)
                            wl = WL[:, r % PIECES, :].rearrange("p (k c) -> p k c", k=4)
                            for kk in range(4):
                                k = 4 * pc + kk
                                last = product(bank[j % 2][:, 0:T], XGH[:, k, :], XGL[:, k, :], wh[:, kk, :], wl[:, kk, :],
                                               k == 0, k == KT - 1)
                            last.then_inc(piece_used, 1)
                        if pc == 0 and 1 <= j <= FT:
                            if j == FT:
                                pe.wait_ge(disp_ready, p * 3 + 6)
                                pe.wait_ge(cur_ready, p + 2)
                                gather(p)
                            pe.wait_ge(eh_ready, p * FT + (j + MOE_H0))
                            pe.wait_ge(eth_lo, p * FT + (j - 2 + MOE_H0))
                            nc.tensor.transpose(bank[4 + 3 * ((j - 1) % 2)][:, 0:P], EH[:, :], ID[:, :]).then_inc(et_ready, 1)
                    if j == 1:
                        scatter(p)
                    if j >= 2:
                        pe.wait_ge(eth_lo, p * FT + (j - 1 + MOE_H0))
                        r = DOWN_AT[j - 2]
                        pe.wait_ge(lo_done, p * PP + (NF + r + 1))
                        for half in range(2):
                            n = slice(512 * half, 512 * half + 512)
                            last = product(bank[2 + half][:, :], EHH[:, j % 2, :], EHL[:, j % 2, :],
                                           WH[:, r % PIECES, n], WL[:, r % PIECES, n], j == 2, j == FT + 1)
                        last.then_inc(piece_used, 1)

            pe.wait_ge(x2_split, 1)
            pe.wait_ge(disp_ready, 3)
            gather(NONE_BEFORE)
            with pe.Fori(0, EXPERTS) as p:
                expert(p)
            pe.wait_ge(route_ready, 1)
            n_extra = pe.value_load(NUI[0:1, 0:1], min_val=0, max_val=EXTRA)
            for j in range(EXTRA):
                with pe.If(n_extra > j):
                    expert(EXPERTS + j)
            scatter(n_extra + EXPERTS)

        @block.scalar
        def _(act):
            def copy(out, in_):
                return nc.scalar.activation(out, in_, ACT.Copy)

            chained = [0]

            def link(ins):
                chained[0] += 1
                ins.then_inc(act_chain, 1)
                act.wait_ge(act_chain, chained[0])

            split = [0]

            def split_to(q_end):
                for q in range(split[0], min(q_end, NF)):
                    n, pc = pieces[q]
                    s = slabs[n]
                    act.wait_ge(s.sem, s.count)
                    if q >= PIECES:
                        act.wait_ge(piece_used, q - PIECES + 1)
                    at = s.offset + PIECE * pc
                    copy(WH[:, q % PIECES, :], RAW[:, at:at + PIECE]).then_inc(hi_done, 1)
                split[0] = max(split[0], q_end)

            def a_filled(a):
                s = slabs[A_IDX[a]]
                split_to(s.first + PIECES)
                act.wait_ge(piece_used, s.first + 2)
                return bank[a % 2]

            def plain_hi(name, dst):
                for q in range(4):
                    wait_ready(act, name, q)
                    copy(dst[:, 2 * q:2 * q + 2, :].rearrange("p k t -> p (k t)"), use_bank(name, q)[:, :]).then_inc(tr_hi, 1)

            split_to(PIECES)
            plain_hi("tr0", MTH)
            for a in range(4):
                b = a_filled(a)
                dst = (MK if a % 2 == 0 else MVA)[:, a // 2, :, :].rearrange("p a c -> p (a c)")
                copy(dst, b[:, :]).then_inc(a_act, 1)
            plain_hi("tr1", TH)
            act.wait_ge(cols_ready, 1)

            def lora(i):
                wait_ready(act, "up", i)
                b = use_bank("up", i)
                nc.scalar.activation(CS[:, i, :, 1:P + 1], b[:, 0:T].rearrange("p (c t) -> p c t", c=NT), ACT.Sigmoid,
                                     bias=col(VEC + i)).then_inc(misc_act, 1)
                wait_ready(act, "gate", i)
                nc.scalar.activation(BT[:, i, :], use_bank("gate", i)[:, T:2 * T], ACT.Sigmoid, bias=col(VEC + 6 + i))
                copy(G[:, i, :], use_bank("gate", i)[:, 0:T]).then_inc(misc_act, 1)

            for a in range(4, 15):
                b = a_filled(a)
                w = W_ORDER[a - 4]
                if w == 10:
                    nc.scalar.activation(QM[:, :, :].rearrange("p a c -> p (a c)"), b[:, :], ACT.Copy, scale=SCALE).then_inc(a_act, 1)
                    continue
                for m in range(2):
                    tile = 2 * w + m
                    src = b[:, T * m:T * m + T]
                    if tile < 6:
                        dst = AR[:, tile, :, 1, :]
                        src = src.rearrange("p (c t) -> p c t", c=NT)
                    else:
                        dst = [KK, V][tile // 6 - 1][:, tile % 6, :] if tile < 18 else [WD, GD][tile - 18][:, :]
                    last = nc.scalar.activation(dst, src, ACT.Identity, scale=OMMU[:, tile:tile + 1])
                last.then_inc(a_act, 1)
                if a == 4:
                    act.wait_ge(a_dve, 1)
                    nc.scalar.activation(WD[0:HD, :], WD[0:HD, :], ACT.Tanh).then_inc(lora_in_ready, 1)
                    nc.scalar.activation(GD[:, :], GD[:, :], ACT.Sigmoid).then_inc(lora_in_ready, 1)
                if 5 <= a <= 7:
                    for i in (2 * a - 10, 2 * a - 9):
                        lora(i)
                if a == 12:
                    wait_emptied(act, "norm", TILES - 1)
                    nc.scalar.activation(RN[:, :, :], RN[:, :, :], ACT.Sqrt).then_inc(norm_sqrt, 1)

            def exps(i):
                if i >= 2:
                    act.wait_ge(exp_used, i - 1)
                for c in range(NT):
                    nc.scalar.activation(EW[:, i % 2, c, :], CS[:, i, c, :], ACT.Exp, scale=-BETA, bias=BM[:, 0, i, c:c + 1])
                    nc.scalar.activation(EI[:, i % 2, c, :], CS[:, i, c, 1:P + 1], ACT.Exp, scale=BETA, bias=BM[:, 1, i, c:c + 1])
                nc.scalar.activation(WM[:, i:i + 1], BM[:, 0, i, 1:2], ACT.Exp, scale=-1.0).then_inc(exp_ready, 1)

            act.wait_ge(decay_ready, 1)
            exps(0)
            exps(1)
            for i in range(TILES):
                wait_ready(act, "vt", i)
                copy(VT[:, :, P * i:P * i + P], use_bank("vt", i)[:, 0:T].rearrange("p (c t) -> p c t", c=NT)).then_inc(misc_act, 1)
            for i in range(2, TILES):
                exps(i)
            for i in range(TILES):
                wait_ready(act, "bk", i)
                copy(BKT[:, i, :, :].rearrange("p a c -> p (a c)"), use_bank("bk", i)[:, 0:T]).then_inc(misc_act, 1)
            split_to(slabs[A_IDX[15]].first + PIECES)

            LANE_COPY = {2: 1, 3: 2, 4: 3, 5: 4, 6: 5, 7: 6, 9: 7, 11: 8, 13: 9, 14: 10}
            for g in range(NG):
                for step in LANE_COPY:
                    for l in range(4):
                        h, c = job(g, l)
                        L = lanes[l]
                        i, hb = h // 2, HD * (h % 2)
                        rows = slice(hb, hb + HD)
                        PX = L["PX"]
                        b = bank[2 * l + step % 2]
                        act.wait_ge(lane_mm[l], MM_N * g + step)
                        if step <= 4:
                            last = copy(PX[:, 0:2, :].rearrange("p a c -> p (a c)"), b[:, 0:T])
                        elif step == 5:
                            last = copy(L["Q1"][:, :], bank[2 * l][:, 0:HD])
                        elif step == 6:
                            last = copy(PX[:, 3, :], b[:, 0:P])
                        elif step <= 11:
                            last = copy(PX[:, 0, :], b[:, 0:P])
                        elif step == 13:
                            last = copy(L["SA"][:, :], b[:, 0:HD])
                        else:
                            if c == 0:
                                nc.scalar.activation(S0[rows, i, :], b[rows, HD:2 * HD], ACT.Identity,
                                                     scale=SC[rows, i:i + 1]).then_inc(state_ready, 1)
                            last = copy(Y[:, c, HD * h:HD * h + HD], b[:, 0:HD])
                        last.then_inc(lane_act[l], 1)

            def mem_attention(l):
                def exps_of(h):
                    act.wait_ge(smax_ready, MEMH * l + h + 1)
                    if h >= 2:
                        wait_ready(act, f"pt{l}", h - 2)
                    b = use_bank(f"s{l}", h)
                    for t in range(NT):
                        last = nc.scalar.activation(PR[:, h % 2, t, :], b[:, T * t:T * t + T], ACT.Exp,
                                                    bias=SMX[:, h, t:t + 1], accum_out=SSM[:, h, t:t + 1])
                    last.then_inc(misc_act, 1)

                for h in range(MEMH):
                    if h == 0:
                        exps_of(0)
                    if h + 1 < MEMH:
                        exps_of(h + 1)
                    if h % 2:
                        wait_ready(act, f"mo{l}", h // 2)
                        copy(TH[:, 6 + h // 2, :], use_bank(f"mo{l}", h // 2)[:, 0:T]).then_inc(attn_hi, 1)

            act.wait_ge(y_var, 1)
            nc.scalar.activation(YSQ[:, :, :], Y[:, :, :], ACT.Square).then_inc(y_sqrt, 1)
            act.wait_ge(y_var, 2)
            nc.scalar.activation(GNS[:, 2, :, :], GNS[:, 1, :, :], ACT.Sqrt, scale=1.0 / HD, bias=EPS[:, 0:1]).then_inc(y_sqrt, 1)
            mem_attention(0)
            for i in range(TILES):
                wait_ready(act, "yt", i)
                nc.scalar.activation(YT[:, i, :], use_bank("yt", i)[:, 0:T], ACT.Identity,
                                     scale=col(VEC + 24 + i), bias=col(VEC + 30 + i)).then_inc(misc_act, 1)
            for i in range(TILES):
                act.wait_ge(yt_gated, i + 1)
                copy(TH[:, i, :], YT[:, i, :]).then_inc(cat_hi, 1)

            def normed(idx, name):
                act.wait_ge(rstd_ready, idx + 1)
                nc.scalar.activation(X[:, 1, :], X[:, 1, :], ACT.Identity, scale=RS[:, 1:2], bias=NM[:, 1:2]).then_inc(xn_act, 1)
                if name is None:
                    return
                l, v = which_ln(idx)
                for q in range(4):
                    wait_ready(act, name, q)
                    for k in range(2):
                        last = nc.scalar.activation(TH[:, 2 * q + k, :], use_bank(name, q)[:, T * k:T * k + T], ACT.Identity,
                                                    scale=lncol(l, v, 2 * q + k), bias=lncol(l, v + 1, 2 * q + k))
                    last.then_inc(tr_hi, 1)

            split_to(slabs[A_IDX[18]].first + PIECES)
            normed(0, "tr2")

            for f in range(FT + 1):
                if f < FT:
                    split_to(slabs[B0 + f].first + PIECES)
                if f:
                    act.wait_ge(ht_ready, f)
                    if f >= 3:
                        act.wait_ge(piece_used, slabs[B0 + f - 3].down + 1)
                    copy(FHH[:, (f - 1) % 2, :], bank[6 + (f - 1) % 2][:, 0:T]).then_inc(ht_hi, 1)
                if f < FT:
                    act.wait_ge(piece_used, slabs[B0 + f].first + 2)
                    if f:
                        act.wait_ge(h_ready, f)
                    nc.scalar.activation(FS[:, :, :], silu_view(bank[f % 2])[:, :, 0, :], ACT.Silu).then_inc(silu_ready, 1)
            split_to(slabs[A_IDX[19]].first + PIECES)
            normed(1, "tr3")
            for a in range(19, 29):
                b = a_filled(a)
                c = (a - 19) % 3
                if a < 22 or 25 <= a < 28:
                    dst = (KC if a < 22 else QC)[:, 2 * c:2 * c + 2, :].rearrange("p a c -> p (a c)")
                elif a < 25:
                    dst = VK[:, :, T * c:T * c + T]
                    b = b[:, :].rearrange("p (t c) -> p t c", t=NT)
                else:
                    dst = QM1[:, :, :].rearrange("p a c -> p (a c)")
                src = b if a in (22, 23, 24) else b[:, :]
                nc.scalar.activation(dst, src, ACT.Copy, scale=SCALE if a >= 25 else 1.0).then_inc(a_act, 1)

            split_to(slabs[A_IDX[29]].first + PIECES)
            for s in range(HEADS + 1):
                if s < HEADS:
                    h = s
                    wait_ready(act, "z", h)
                    z = use_bank("z", h)[:, 0:3 * P]
                    e = SPA[:, h % 2, :, :].rearrange("p a c -> p (a c)")
                    if h >= 2:
                        act.wait_ge(stick_sp, h - 1)
                    link(nc.scalar.activation(e, z, ACT.Abs))
                    link(nc.scalar.activation(e, e, ACT.Exp, scale=-1.0))
                    nc.scalar.activation(e, e, ACT.Ln, bias=1.0).then_inc(stick_ln, 1)
                if s:
                    h = s - 1
                    act.wait_ge(cs_ready, h + 1)
                    nc.scalar.activation(WT[:, h % 2, :, :].rearrange("p a c -> p (a c)"), use_bank("z", h)[:, 0:3 * P],
                                         ACT.Exp).then_inc(misc_act, 1)
                if s >= 3 and s % 2 == 1:
                    i = (s - 3) // 2
                    wait_ready(act, "so", i)
                    copy(TH[:, i, :], use_bank("so", i)[:, 0:T]).then_inc(attn_hi, 1)
            wait_ready(act, "so", TILES - 1)
            copy(TH[:, TILES - 1, :], use_bank("so", TILES - 1)[:, 0:T]).then_inc(attn_hi, 1)
            act.wait_ge(x_ready, 2)
            mem_attention(1)
            for a in range(29, 33):
                split_to(slabs[A_IDX[a]].first + PIECES)
            normed(2, "tr4")

            act.wait_ge(router_in, 16)
            copy(RHI[:, :, :], RTH[:, :, :]).then_inc(router_hi, 1)
            act.wait_ge(top_diff, 1)
            for t in range(NT):
                last = nc.scalar.activation(W12[:, t, 0:1], W12[:, t, 3:4], ACT.Exp)
            last.then_inc(top_exp, 1)
            act.wait_ge(logits_ready, 1)
            act.wait_ge(x_ready, 3)
            copy(XH, X[:, :, :].rearrange("p t d -> p (t d)")).then_inc(x2_hi, 1)

            def gathered(p):
                for r in (4, 5):
                    act.wait_ge(ring2_ready, ring_ready(p, r))
                    half = r % 2
                    copy(XGH[:, 4 * half:4 * half + 4, :].rearrange("p a c -> p (a c)"), ring_bank(r)[:, :]).then_inc(ring_act, 1)
                act.wait_ge(ring2_ready, ring_ready(p, 8))
                copy(DTN[:, :, :].rearrange("p a c -> p (a c)"), ring_bank(8)[:, 0:T]).then_inc(ring_act, 1)
                act.wait_ge(ring2_ready, ring_ready(p, 9))
                copy(CWN[:, :], ring_bank(9)[:, 0:1]).then_inc(ring_act, 1)

            def out_hi(p):
                for half in range(2):
                    nc.scalar.activation(OH[:, half, :], bank[2 + half][:, :], ACT.Copy, scale=CWC[:, 0:1]).then_inc(out_hi_s, 1)

            def expert(p):
                done = 0
                for j in range(FT + 1):
                    upto = min(GU_AT[j] + PIECES, PP) if j < FT else PP
                    for r in range(done, upto):
                        m, pc = pass_pieces[r]
                        s = MOE_SLOT[m]
                        if r == GU_AT[m]:
                            times = sum(MOE_SLOT[x] == s for x in range(m + 1))
                            act.wait_ge(raw_in[s], p * PER_PASS[s] + (MOE_BASE[s] + 48 * times))
                        act.wait_ge(piece_used, p * PP + (NF + r - PIECES + 1))
                        at = SLOT * s + PIECE * pc
                        copy(WH[:, r % PIECES, :], RAW[:, at:at + PIECE]).then_inc(hi_done, 1)
                    done = upto
                    if j == 0:
                        act.wait_ge(piece_used, p * PP + NF)
                        act.wait_ge(cur_ready, p + 1)
                        out_hi(p)
                    if j == FT:
                        gathered(p)
                    if j:
                        act.wait_ge(et_ready, p * FT + j)
                        copy(EHH[:, (j - 1) % 2, :], bank[4 + 3 * ((j - 1) % 2)][:, 0:P]).then_inc(eth_hi, 1)
                    if j < FT:
                        act.wait_ge(piece_used, p * PP + (NF + GU_AT[j] + 2))
                        act.wait_ge(eh_ready, p * FT + (j + MOE_H0))
                        nc.scalar.activation(ES[:, :], bank[j % 2][:, 0:P], ACT.Silu).then_inc(es_ready, 1)

            gathered(NONE_BEFORE)
            with act.Fori(0, EXPERTS) as p:
                expert(p)
            act.wait_ge(route_ready, 1)
            n_extra = act.value_load(NUI[0:1, 0:1], min_val=0, max_val=EXTRA)
            for j in range(EXTRA):
                with act.If(n_extra > j):
                    expert(EXPERTS + j)
            act.wait_ge(piece_used, (n_extra + EXPERTS) * PP + NF)
            act.wait_ge(cur_ready, n_extra + (EXPERTS + 1))
            out_hi(0)
            act.wait_ge(rstd_ready, 4)
            normed(3, None)

        @block.vector
        def _(dve):
            v = nc.vector
            chained = [0]

            def chain(ins):
                chained[0] += 1
                return ins.then_inc(dve_chain, 1)

            def settle():
                dve.wait_ge(dve_chain, chained[0])

            split = [0]

            def split_to(q_end):
                for q in range(split[0], min(q_end, NF)):
                    n, pc = pieces[q]
                    dve.wait_ge(hi_done, q + 1)
                    at = slabs[n].offset + PIECE * pc
                    v.tensor_tensor(WL[:, q % PIECES, :], RAW[:, at:at + PIECE], WH[:, q % PIECES, :].bitcast(F32),
                                    ALU.subtract).then_inc(lo_done, 1)
                split[0] = max(split[0], q_end)

            def low(out, full, hi):
                return v.tensor_tensor(out, full, hi.bitcast(F32), ALU.subtract)

            def plain_lo(name, hi, lo, base_count):
                for q in range(4):
                    dve.wait_ge(tr_hi, base_count + q + 1)
                    flat = lambda t: t[:, 2 * q:2 * q + 2, :].rearrange("p k t -> p (k t)")
                    low(flat(lo), use_bank(name, q)[:, :], flat(hi)).then_inc(misc_dve, 1)

            chain(v.memset(CS[:, :, :, 0:1], 0.0))
            wait_ready(dve, "cols", 0)
            v.tensor_copy(COLS[:, 0:126], use_bank("cols", 0)[:, 0:126]).then_inc(misc_dve, 1)
            dve.wait_ge(misc_dve, 1)
            v.tensor_scalar(OMMU[:, :], COLS[:, MU:MU + 20], -1.0, 1.0, ALU.mult, ALU.add)
            v.tensor_scalar(OMKA[:, :], COLS[:, VEC + 18:VEC + 24], -1.0, 1.0, ALU.mult, ALU.add).then_inc(cols_ready, 1)
            split_to(2)
            plain_lo("tr0", MTH, MTL, 0)
            for a in range(4):
                split_to(slabs[A_IDX[a]].first + PIECES)
            plain_lo("tr1", TH, TL, 4)

            def mixed(a, b):
                w = W_ORDER[a - 4]
                dve.wait_ge(a_act, A_ACT[a])
                for m in range(2):
                    tile = 2 * w + m
                    mu = col(MU + tile)
                    src = b[:, T * m:T * m + T]
                    if tile < 6:
                        dst = AR[:, tile, :, 1, :]
                        v.scalar_tensor_tensor(dst[:, 0, 1:P], src[:, 0:P - 1], mu, dst[:, 0, 1:P], ALU.mult, ALU.add)
                        last = v.scalar_tensor_tensor(dst[:, 1, :], src[:, P - 1:T - 1], mu, dst[:, 1, :], ALU.mult, ALU.add)
                    else:
                        dst = [KK, V][tile // 6 - 1][:, tile % 6, :] if tile < 18 else [WD, GD][tile - 18][:, :]
                        last = v.scalar_tensor_tensor(dst[:, 1:T], src[:, 0:T - 1], mu, dst[:, 1:T], ALU.mult, ALU.add)
                last.then_inc(a_dve, 1)

            for a in range(4, 14):
                split_to(slabs[A_IDX[a]].first + PIECES)
                mixed(a, bank[a % 2])
                if a == 8:
                    settle()
                    for i in range(TILES):
                        wait_emptied(dve, "up", i)
                        for c in range(NT):
                            s_ = CS[:, i, c, 1:P + 1]
                            chain(v.tensor_tensor_scan(s_, ONE[:, :], s_, 0.0, ALU.mult, ALU.add))
                    settle()
                    chain(v.tensor_scalar(BM[:, 0, :, :], CS[:, :, :, P // 2], BETA, None, ALU.mult))
                    v.tensor_scalar(BM[:, 1, :, :], CS[:, :, :, P // 2], -BETA, None, ALU.mult).then_inc(decay_ready, 1)
                if 9 <= a <= 11:
                    for i in (2 * a - 18, 2 * a - 17):
                        wait_ready(dve, "norm", i)
                        v.tensor_scalar(RN[:, i, :], use_bank("norm", i)[:, 0:T], 1e-24, None, ALU.max).then_inc(misc_dve, 1)
            split_to(slabs[A_IDX[14]].first + PIECES)

            dve.wait_ge(norm_sqrt, 1)
            chain(v.reciprocal(RN[:, :, :], RN[:, :, :]))
            settle()
            dve.wait_ge(square_ready, TILES)
            a_part = AR[:, :, :, 0, :]
            for i in range(TILES):
                chain(v.tensor_tensor(AR[:, i, :, 0, :], AR[:, i, :, 0, :], RN[:, i, :].rearrange("p (c t) -> p c t", c=NT), ALU.mult))
            for i in range(TILES):
                chain(v.tensor_scalar(FM[:, i % 2, :], BT[:, i, :], col(VEC + 18 + i), OMKA[:, i:i + 1], ALU.mult, ALU.add))
                settle()
                chain(v.tensor_tensor(KK[:, i, :], KK[:, i, :], FM[:, i % 2, :], ALU.mult))
                settle()
                if i >= 2:
                    wait_ready(dve, "bonus", i - 2)
                v.scalar_tensor_tensor(RK[:, i % 2, :].rearrange("p (c t) -> p c t", c=NT), AR[:, i, :, 1, :], col(RKC + i),
                                       KK[:, i, :].rearrange("p (c t) -> p c t", c=NT), ALU.mult, ALU.mult).then_inc(rk_ready, 1)
                if i >= 1:
                    bonus = i - 1
                    wait_ready(dve, "bonus", bonus)
                    wait_emptied(dve, "vt", bonus)
                    v.tensor_tensor(V[:, bonus, :], V[:, bonus, :], use_bank("bonus", bonus)[:, 0:T], ALU.mult).then_inc(misc_dve, 1)
                chain(v.tensor_tensor(BT[:, i, :].rearrange("p (c t) -> p c t", c=NT), BT[:, i, :].rearrange("p (c t) -> p c t", c=NT),
                                      AR[:, i, :, 0, :], ALU.mult))
            wait_ready(dve, "bonus", TILES - 1)
            wait_emptied(dve, "vt", TILES - 1)
            v.tensor_tensor(V[:, TILES - 1, :], V[:, TILES - 1, :], use_bank("bonus", TILES - 1)[:, 0:T], ALU.mult).then_inc(misc_dve, 1)
            dve.wait_ge(rk_ready, TILES)
            for i in range(TILES):
                dve.wait_ge(exp_ready, i + 1)
                settle()
                two = lambda t: t.rearrange("p (c t) -> p c t", c=NT)
                chain(v.tensor_tensor(AR[:, i, :, 1, :], AR[:, i, :, 1, :], EW[:, i % 2, :, 1:P + 1], ALU.mult))
                chain(v.scalar_tensor_tensor(AR[:, i, :, 0, :], AR[:, i, :, 0, :], -1.0, EW[:, i % 2, :, 0:P], ALU.mult, ALU.mult))
                chain(v.tensor_tensor(two(BT[:, i, :]), two(BT[:, i, :]), EI[:, i % 2, :, :], ALU.mult))
                chain(v.tensor_tensor(SC[:, i:i + 1], EW[:, i % 2, 0, P:P + 1], WM[:, i:i + 1], ALU.mult))
                v.tensor_tensor(two(KK[:, i, :]), two(KK[:, i, :]), EI[:, i % 2, :, :], ALU.mult).then_inc(exp_used, 1)
            split_to(slabs[A_IDX[15]].first + PIECES)

            for g in range(NG):
                for step in (1, 3, 4, 5, 8, 10, 12):
                    for l in range(4):
                        L = lanes[l]
                        PX = L["PX"]
                        b = bank[2 * l + step % 2]
                        dve.wait_ge(lane_mm[l], MM_N * g + step)
                        if step == 1:
                            if g:
                                dve.wait_ge(lane_pool[l], POOL_N * g)
                            si = SI[:, :, :].rearrange("p a c -> p (a c)")
                            flat = lambda t: t[:, :, :].rearrange("p a c -> p (a c)")
                            v.tensor_tensor(flat(L["MR"]), bank[2 * l][:, 0:T], si, ALU.mult).then_inc(lane_dve[l], 1)
                            v.tensor_tensor(flat(L["KR"]), bank[2 * l][:, T:2 * T], si, ALU.mult).then_inc(lane_dve[l], 1)
                            v.tensor_tensor(L["AL"][:, :], bank[2 * l + 1][:, 0:P], LS[:, :], ALU.mult).then_inc(lane_dve[l], 1)
                        elif step in (3, 4):
                            v.tensor_tensor(PX[:, 2, :], PX[:, 2, :], bank[2 * l + 1 - step % 2][:, 0:P], ALU.add).then_inc(lane_dve[l], 1)
                        elif step in (5, 12):
                            v.tensor_tensor(PX[:, 2, :], PX[:, 2, :], b[:, 0:P], ALU.add).then_inc(lane_dve[l], 1)
                        else:
                            xx = PX[:, 2:4, :].rearrange("p a c -> p (a c)")
                            v.tensor_tensor(xx, xx, b[:, 0:T], ALU.add).then_inc(lane_dve[l], 1)

            for l in range(4):
                dve.wait_ge(lane_act[l], ACT_N * NG)
            y3 = Y[:, :, :].rearrange("p c (h d) -> p (c h) d", d=HD)
            sq3 = YSQ[:, :, :].rearrange("p c (h d) -> p (c h) d", d=HD)

            def stat(n):
                return GNS[:, n, :, :].rearrange("p c h -> p (c h)")

            def spread(n):
                return stat(n).rearrange("p (h o) -> p h o", o=1).broadcast_to([P, NT * HEADS, HD])

            chain(v.tensor_reduce(stat(0), y3, AX_X, ALU.add))
            settle()
            chain(v.tensor_scalar(stat(0), stat(0), -1.0 / HD, None, ALU.mult))
            settle()
            v.tensor_tensor(y3, y3, spread(0), ALU.add).then_inc(y_var, 1)
            dve.wait_ge(y_sqrt, 1)
            v.tensor_reduce(stat(1), sq3, AX_X, ALU.add).then_inc(y_var, 1)
            dve.wait_ge(y_sqrt, 2)
            chain(v.reciprocal(stat(3), stat(2)))
            settle()
            v.tensor_tensor(y3, y3, spread(3), ALU.mult).then_inc(y_ready, 1)

            def mem_attention(l):
                def top(h):
                    wait_ready(dve, f"s{l}", h)
                    b = use_bank(f"s{l}", h)
                    chain(v.tensor_reduce(SMX[:, h, :], b[:, :].rearrange("p (t m) -> p t m", t=NT), AX_X, ALU.max))
                    settle()
                    v.tensor_scalar(SMX[:, h, :], SMX[:, h, :], -1.0, None, ALU.mult).then_inc(smax_ready, 1)

                for h in range(MEMH):
                    if h == 0:
                        top(0)
                    if h + 1 < MEMH:
                        top(h + 1)
                    wait_emptied(dve, f"s{l}", h)
                    chain(v.reciprocal(SRI[:, h, :], SSM[:, h, :]))
                    settle()
                    for t in range(NT):
                        last = v.tensor_scalar(PR[:, h % 2, t, :], PR[:, h % 2, t, :], SRI[:, h, t:t + 1], None, ALU.mult)
                    last.then_inc(probs_ready, 1)
                    wait_ready(dve, f"pt{l}", h)
                    v.tensor_copy(PT[:, h % 2, :, :].rearrange("p a c -> p (a c)"), use_bank(f"pt{l}", h)[:, :]).then_inc(misc_dve, 1)
                    if h % 2:
                        i = h // 2
                        dve.wait_ge(attn_hi, 2 * (l + 1) - 2 + i + 1 + (TILES if l else 0))
                        low(TL[:, 6 + i, :], use_bank(f"mo{l}", i)[:, 0:T], TH[:, 6 + i, :]).then_inc(misc_dve, 1)

            mem_attention(0)
            for i in range(TILES):
                dve.wait_ge(yt_bonus, i + 1)
                v.tensor_tensor(YT[:, i, :], YT[:, i, :], G[:, i, :], ALU.mult).then_inc(yt_gated, 1)
            for i in range(TILES):
                dve.wait_ge(cat_hi, i + 1)
                low(TL[:, i, :], YT[:, i, :], TH[:, i, :]).then_inc(cat_ready, 1)

            def residual(a):
                split_to(slabs[A_IDX[a]].first + PIECES)
                dve.wait_ge(piece_used, slabs[A_IDX[a]].first + 2)
                cut = slice(T * ((a - 15) % 14), T * ((a - 15) % 14) + T)
                v.scalar_tensor_tensor(X[:, :, cut], X[:, :, cut], ALPHA, bank[a % 2][:, :].rearrange("p (t c) -> p t c", t=NT),
                                       ALU.mult, ALU.add).then_inc(a_dve, 1)

            def stats(idx):
                for t in range(NT):
                    for half in range(2):
                        chain(v.bn_stats(BN[:, t, half, :], X[:, t, 512 * half:512 * half + 512]))
                settle()
                for t in range(NT):
                    v.bn_aggr(MV[:, t, :], BN[:, t, :, :]).then_inc(stats_ready, 1)
                dve.wait_ge(rstd_ready, idx + 1)
                v.tensor_scalar(X[:, 0, :], X[:, 0, :], MV[:, 0, 0:1], RS[:, 0:1], ALU.subtract, ALU.mult).then_inc(xn_dve, 1)

            def normed(idx, name, base_count):
                stats(idx)
                l, vv = which_ln(idx)
                for q in range(4):
                    dve.wait_ge(tr_hi, base_count + q + 1)
                    for k in range(2):
                        if q:
                            dve.wait_ge(misc_dve, emptied(USE[name, q - 1])[1])
                        chain(v.tensor_scalar(TT[:, k, :], use_bank(name, q)[:, T * k:T * k + T], lncol(l, vv, 2 * q + k),
                                              lncol(l, vv + 1, 2 * q + k), ALU.mult, ALU.add))
                    settle()
                    low(TL[:, 2 * q:2 * q + 2, :], TT[:, :, :], TH[:, 2 * q:2 * q + 2, :]).then_inc(misc_dve, 1)

            for a in range(15, 19):
                residual(a)
            dve.wait_ge(a_dve, A_DVE[18])
            normed(0, "tr2", 8)

            for f in range(FT + 1):
                if f < FT:
                    split_to(slabs[B0 + f].first + PIECES)
                if f:
                    dve.wait_ge(ht_hi, f)
                    low(FHL[:, (f - 1) % 2, :], bank[6 + (f - 1) % 2][:, 0:T], FHH[:, (f - 1) % 2, :]).then_inc(ht_lo, 1)
                if f < FT:
                    dve.wait_ge(silu_ready, f + 1)
                    if f:
                        dve.wait_ge(ht_ready, f)
                    v.tensor_tensor(FH[:, :, :], FS[:, :, :], silu_view(bank[f % 2])[:, :, 1, :], ALU.mult).then_inc(h_ready, 1)
            split_to(slabs[A_IDX[19]].first + PIECES)
            dve.wait_ge(piece_used, slabs[B0 + FT - 1].down + 1)
            dve.wait_ge(x_ready, 1)
            for t in range(NT):
                for half in range(2):
                    n = slice(512 * half, 512 * half + 512)
                    v.scalar_tensor_tensor(X[:, t, n], X[:, t, n], ALPHA, bank[2 + 2 * t + half][:, :],
                                           ALU.mult, ALU.add).then_inc(ffn_out, 1)
            dve.wait_ge(ffn_out, 4)
            normed(1, "tr3", 12)
            for a in range(19, 30):
                split_to(slabs[A_IDX[a]].first + PIECES)

            for s in range(HEADS + 2):
                if s < HEADS:
                    h = s
                    dve.wait_ge(stick_ln, h + 1)
                    if h >= 2:
                        dve.wait_ge(cs_ready, h - 1)
                    v.scalar_tensor_tensor(SP[:, h % 2, :, :].rearrange("p a c -> p (a c)"), use_bank("z", h)[:, 0:3 * P], 0.0,
                                           SPA[:, h % 2, :, :].rearrange("p a c -> p (a c)"), ALU.max, ALU.add).then_inc(stick_sp, 1)
                if s >= 3 and s % 2 == 1:
                    i = (s - 3) // 2
                    dve.wait_ge(attn_hi, 2 + i + 1)
                    low(TL[:, i, :], use_bank("so", i)[:, 0:T], TH[:, i, :]).then_inc(misc_dve, 1)
            mem_attention(1)
            dve.wait_ge(x_ready, 2)
            for a in range(29, 33):
                residual(a)
            dve.wait_ge(a_dve, A_DVE[32])

            def routing_inputs():
                dve.wait_ge(router_hi, 1)
                low(RLO[:, :, :], RTH[:, :, :], RHI[:, :, :]).then_inc(router_split, 1)

            normed(2, "tr4", 16)
            routing_inputs()

            dve.wait_ge(logits_ready, 1)
            chain(v.tensor_copy(LG[:, :, :].rearrange("p t e -> p (t e)"), bank[0][:, 0:16]))
            settle()
            for t in range(NT):
                chain(v.max(MX8[:, t, :], LG[:, t, :]))
            settle()
            for t in range(NT):
                chain(v.max_index(IX8[:, t, :], MX8[:, t, :], LG[:, t, :]))
                last = chain(v.tensor_tensor(W12[:, t, 3:4], MX8[:, t, 1:2], MX8[:, t, 0:1], ALU.subtract))
            settle()
            v.tensor_copy(IXF[:, :, :], IX8[:, :, :]).then_inc(top_diff, 1)
            dve.wait_ge(top_diff, 1)
            for t in range(NT):
                chain(v.tensor_scalar(OH1[:, t, :], ROW8, IXF[:, t, 0:1], None, ALU.is_equal))
                chain(v.tensor_scalar(OH2[:, t, :], ROW8, IXF[:, t, 1:2], None, ALU.is_equal))
            settle()
            v.tensor_tensor(SEL[:, :, :], OH1[:, :, :], OH2[:, :, :], ALU.add).then_inc(top_ready, 1)
            dve.wait_ge(top_exp, 1)
            chain(v.tensor_scalar(W12[:, :, 1:2], W12[:, :, 0:1], 1.0, None, ALU.add))
            settle()
            chain(v.reciprocal(W12[:, :, 1:2], W12[:, :, 1:2]))
            settle()
            chain(v.tensor_tensor(W12[:, :, 2:3], W12[:, :, 1:2], W12[:, :, 0:1], ALU.mult))
            settle()
            for t in range(NT):
                chain(v.tensor_scalar(OH1[:, t, :], OH1[:, t, :], W12[:, t, 1:2], None, ALU.mult))
            settle()
            for t in range(NT):
                chain(v.scalar_tensor_tensor(CMB[:, t, :], OH2[:, t, :], W12[:, t, 2:3], OH1[:, t, :], ALU.mult, ALU.add))
            dve.wait_ge(rank_ready, 1)
            chain(v.tensor_copy(RK8[:, :, :].rearrange("p t e -> p (t e)"), bank[1][:, 0:16]))
            chain(v.tensor_scalar(OVR[:, :], bank[1][:, 16:24], float(P), None, ALU.is_gt))
            settle()
            chain(v.tensor_tensor_scan(POS[:, :], ONE[:, 0:8], OVR[:, :], 0.0, ALU.mult, ALU.add))
            chain(v.memset(NUM[:, :], 0.0))
            settle()
            chain(v.tensor_copy(NUM[:, 0:1], POS[:, 7:8]))
            for j in range(EXTRA):
                chain(v.scalar_tensor_tensor(EXJ[:, j, :], POS[:, :], float(j + 1), OVR[:, :], ALU.is_equal, ALU.mult))
            settle()
            for j in range(EXTRA):
                chain(v.tensor_tensor(PRE[:, j, :], EXJ[:, j, :], ROW8, ALU.mult))
                for n, src in enumerate((RK8, SEL, CMB)):
                    for t in range(NT):
                        chain(v.tensor_tensor(PRD[:, j, n, t, :], src[:, t, :], EXJ[:, j, :], ALU.mult))
            settle()
            chain(v.tensor_reduce(NUM[:, 1:4], PRE[:, :, :], AX_X, ALU.add))
            for n, dst in enumerate((RKP, SLP, CBP)):
                for t in range(NT):
                    chain(v.tensor_reduce(dst[:, t, EXPERTS:EXPERTS + EXTRA], PRD[:, :, n, t, :], AX_X, ALU.add))
                chain(v.tensor_copy(dst[:, :, 0:EXPERTS], (RK8, SEL, CMB)[n][:, :, :]))
                chain(v.memset(dst[:, :, NP - 1:NP], 0.0))
            settle()
            chain(v.tensor_scalar(RKP[:, :, EXPERTS:NP - 1], RKP[:, :, EXPERTS:NP - 1], -float(P), None, ALU.add))
            v.tensor_copy(NUI[:, :], NUM[:, :]).then_inc(route_ready, 1)
            settle()
            dve.wait_ge(route_ready, 1)

            def dispatch(p):
                one = bass.ds(p, 1) if not isinstance(p, int) else slice(p, p + 1)
                for t in range(NT):
                    v.tensor_scalar(DI[:, t, :], IO[:, :], RKP[:, t, one], SLP[:, t, one], ALU.is_equal, ALU.mult)\
                        .then_inc(disp_ready, 1)
                v.tensor_copy(CPC[:, :], CBP[:, :, one].rearrange("p t o -> p (t o)")).then_inc(disp_ready, 1)

            dispatch(0)
            dve.wait_ge(x2_hi, 1)
            low(XL, X[:, :, :].rearrange("p t d -> p (t d)"), XH).then_inc(x2_split, 1)
            dve.wait_ge(x2_split, 1)
            v.tensor_scalar(X[:, :, :], X[:, :, :], ALPHA, None, ALU.mult).then_inc(y_start, 1)
            for n in range(MOE_H0):
                v.memset(EH[:, HD * n:HD * n + HD], 0.0).then_inc(eh_ready, 1)
                v.memset(EHL[:, n, :].bitcast(F32), 0.0).then_inc(eth_lo, 1)
            dve.wait_ge(y_start, 1)
            dve.wait_ge(eh_ready, MOE_H0)
            dve.wait_ge(eth_lo, MOE_H0)

            def gathered(p):
                for r in (6, 7):
                    dve.wait_ge(ring2_ready, ring_ready(p, r))
                    half = r % 2
                    v.tensor_copy(XGL[:, 4 * half:4 * half + 4, :].rearrange("p a c -> p (a c)"), ring_bank(r)[:, :]).then_inc(ring_dve, 1)

            def out_lo(p):
                for half in range(2):
                    dve.wait_ge(out_hi_s, 2 * p + (half + 1))
                    v.scalar_tensor_tensor(OL[:, half, :], bank[2 + half][:, :], CWC[:, 0:1], OH[:, half, :].bitcast(F32),
                                           ALU.mult, ALU.subtract).then_inc(out_lo_s, 1)

            def scattered(p):
                for r in range(4):
                    t, half = r // 2, r % 2
                    n = slice(512 * half, 512 * half + 512)
                    dve.wait_ge(ring2_ready, ring_ready(p, r))
                    v.tensor_tensor(X[:, t, n], X[:, t, n], ring_bank(r)[:, :], ALU.add).then_inc(ring_dve, 1)

            def expert(p):
                done = 0
                for j in range(FT + 1):
                    if j == 2:
                        dve.wait_ge(ring_dve, p * RING_DVE + RING_DVE0)
                        scattered(p)
                    upto = min(GU_AT[j] + PIECES, PP) if j < FT else PP
                    for r in range(done, upto):
                        m, pc = pass_pieces[r]
                        dve.wait_ge(hi_done, p * PP + (NF + r + 1))
                        at = SLOT * MOE_SLOT[m] + PIECE * pc
                        v.tensor_tensor(WL[:, r % PIECES, :], RAW[:, at:at + PIECE], WH[:, r % PIECES, :].bitcast(F32),
                                        ALU.subtract).then_inc(lo_done, 1)
                    done = upto
                    if j == 0:
                        out_lo(p)
                    if j == FT - 3:
                        dve.wait_ge(ring2_ready, ring_ready(p - 1, 9))
                        dispatch(p + 1)
                    if j == FT:
                        gathered(p)
                    if j:
                        dve.wait_ge(eth_hi, p * FT + j)
                        low(EHL[:, (j - 1) % 2, :], bank[4 + 3 * ((j - 1) % 2)][:, 0:P], EHH[:, (j - 1) % 2, :]).then_inc(eth_lo, 1)
                    if j < FT:
                        dve.wait_ge(es_ready, p * FT + (j + 1))
                        if j:
                            dve.wait_ge(et_ready, p * FT + j)
                        v.tensor_tensor(EH[:, :], ES[:, :], bank[j % 2][:, P:T], ALU.mult).then_inc(eh_ready, 1)

            gathered(NONE_BEFORE)
            with dve.Fori(0, EXPERTS) as p:
                expert(p)
            n_extra = dve.value_load(NUI[0:1, 0:1], min_val=0, max_val=EXTRA)
            for j in range(EXTRA):
                with dve.If(n_extra > j):
                    expert(EXPERTS + j)
            passes = n_extra + EXPERTS
            out_lo(passes)
            scattered(passes)
            dve.wait_ge(ring_dve, passes * RING_DVE + (RING_DVE0 + 4))
            stats(3)
            dve.wait_ge(xn_dve, 4)
            dve.wait_ge(rows_in, 4 * 32)
            chain(v.tensor_tensor(X[:, 0, :], X[:, 0, :], GB[:, 0, :], ALU.mult))
            settle()
            v.tensor_tensor(X[:, 0, :], X[:, 0, :], GB[:, 1, :], ALU.add).then_inc(final_ready, 1)

        @block.gpsimd
        def _(pool):
            g_ = nc.gpsimd
            chained = [0]

            def link(ins):
                chained[0] += 1
                ins.then_inc(pool_chain, 1)
                pool.wait_ge(pool_chain, chained[0])

            def select(t, pattern, base_, mult, op, fill):
                link(g_.affine_select(out=t, in_=t, compare_op=op, fill=fill, base=base_, pattern=pattern, channel_multiplier=mult))

            for t, value in ((ID, 0.0), (SI, 1.0), (LS, 1.0), (BD, 1.0), (LV, 1.0), (BO, 1.0), (NTRI, -1.0), (NONE, -1.0),
                             (ONE, 1.0), (EC, -0.5), (EPS, GN_EPS)):
                g_.memset(t[tuple([slice(None)] * len(t.shape))], value)
            link(g_.iota(IO[:, :], [[1, P]], base=0, channel_multiplier=0, allow_small_or_imprecise_dtypes=True))
            select(ID[:, :], [[-1, P]], 0, 1, ALU.not_equal, 1.0)
            select(SI[:, 0, :], [[1, P]], 0, -1, ALU.is_gt, 0.0)
            select(SI[:, 1, :], [[1, P]], 0, -1, ALU.is_ge, 0.0)
            select(LS[:, :], [[-1, P]], 0, 1, ALU.is_gt, 0.0)
            bd = BD[:, :].rearrange("p (b c) -> p b c", c=16)
            select(bd, [[-16, 8], [0, 16]], 0, 1, ALU.is_ge, 0.0)
            select(bd, [[16, 8], [0, 16]], 15, -1, ALU.is_ge, 0.0)
            bo = BO[:, :].rearrange("p (b c) -> p b c", c=HD)
            select(bo, [[-HD, 2], [0, HD]], 0, 1, ALU.is_ge, 0.0)
            select(bo, [[HD, 2], [0, HD]], HD - 1, -1, ALU.is_ge, 0.0)
            for lev in range(3):
                w = 16 << lev
                nb = P // (2 * w)
                lv = LV[:, lev, :].rearrange("p (b z c) -> p b z c", z=2, c=w)
                select(lv, [[0, nb], [-1, 2], [0, w]], 0, 0, ALU.is_ge, 0.0)
                select(lv, [[-2 * w, nb], [0, 2], [0, w]], -w, 1, ALU.is_ge, 0.0)
                select(lv, [[2 * w, nb], [0, 2], [0, w]], 2 * w - 1, -1, ALU.is_ge, 0.0)
            g_.affine_select(out=NTRI[:, :], in_=NTRI[:, :], compare_op=ALU.is_ge, fill=0.0, base=0, pattern=[[-1, P]],
                             channel_multiplier=1).then_inc(consts_ready, 1)
            pool.wait_ge(consts_ready, 1)

            pool.wait_ge(cols_ready, 1)
            for i in range(TILES):
                pool.wait_ge(a_dve, A_DVE[8 + i // 2])
                a2 = AR[:, i, :, 0, :]
                link(g_.tensor_scalar(a2, KK[:, i, :].rearrange("p (c t) -> p c t", c=NT), col(VEC + 12 + i), None, ALU.mult))
                if i >= 2:
                    wait_ready(pool, "norm", i - 2)
                g_.tensor_tensor(SQ[:, i % 2, :].rearrange("p (c t) -> p c t", c=NT), a2, a2, ALU.mult).then_inc(square_ready, 1)

            for g in range(NG):
                for l in range(4):
                    L = lanes[l]
                    PX = L["PX"]
                    pool.wait_ge(lane_dve[l], DVE_N * g + 1)
                    g_.tensor_tensor(PX[:, 1, :], L["MR"][:, 0, :], BD[:, :], ALU.mult).then_inc(lane_pool[l], 1)
                    pool.wait_ge(lane_dve[l], DVE_N * g + 3)
                    g_.tensor_tensor(PX[:, 0, :], L["AL"][:, :], BD[:, :], ALU.mult).then_inc(lane_pool[l], 1)
                    pool.wait_ge(lane_pool[l], POOL_N * g + 2)
                    g_.tensor_tensor(PX[:, 2, :], PX[:, 1, :], ID[:, :], ALU.add).then_inc(lane_pool[l], 1)
                for l in range(4):
                    L = lanes[l]
                    g_.tensor_tensor(L["LT"][:, :, :], L["AL"][:, :].rearrange("p (o c) -> p o c", o=1).broadcast_to([P, 3, P]),
                                     LV[:, :, :], ALU.mult).then_inc(lane_pool[l], 1)

            for i in range(TILES):
                wait_emptied(pool, "yt", i)
                g_.tensor_tensor(YT[:, i, :], YT[:, i, :], V[:, i, :], ALU.add).then_inc(yt_bonus, 1)

            def rstd(idx):
                pool.wait_ge(stats_ready, NT * (idx + 1))
                link(g_.tensor_scalar(RS[:, :], MV[:, :, 1], LN_EPS, None, ALU.add))
                link(g_.tensor_tensor(RS[:, :], RS[:, :], EC[:, :], ALU.pow))
                link(g_.tensor_scalar(NM[:, :], MV[:, :, 0], -1.0, None, ALU.mult))
                g_.tensor_tensor(NM[:, :], NM[:, :], RS[:, :], ALU.mult).then_inc(rstd_ready, 1)

            def affine(idx, name, tiles):
                if name:
                    wait_ready(pool, name, 3)
                pool.wait_ge(rows_in, 32 * (idx + 1))
                for t in tiles:
                    g_.tensor_tensor(X[:, t, :], X[:, t, :], GB[:, 0, :], ALU.mult).then_inc(pool_chain, 1)
                    chained[0] += 1
                pool.wait_ge(pool_chain, chained[0])
                for t in tiles:
                    last = g_.tensor_tensor(X[:, t, :], X[:, t, :], GB[:, 1, :], ALU.add)
                last.then_inc(x_ready, 1)

            rstd(0)
            affine(0, "tr2", (0, 1))
            rstd(1)
            affine(1, "tr3", (0, 1))
            for s in range(HEADS + 1):
                if s < HEADS:
                    h = s
                    pool.wait_ge(stick_sp, h + 1)
                    t = SP[:, h % 2, 0:3:2, :]
                    g_.affine_select(out=t, in_=t, compare_op=ALU.is_gt, fill=0.0, base=0, pattern=[[0, 2], [1, P]],
                                     channel_multiplier=-1).then_inc(stick_masked, 1)
                if s:
                    h = s - 1
                    wait_emptied(pool, "z", h)
                    t = WT[:, h % 2, 0:3:2, :]
                    g_.affine_select(out=t, in_=t, compare_op=ALU.is_gt, fill=0.0, base=0, pattern=[[0, 2], [1, P]],
                                     channel_multiplier=-1).then_inc(stick_w, 1)
            rstd(2)
            affine(2, "tr4", (0, 1))
            pool.wait_ge(route_ready, 1)
            g_.memset(CWC[:, :], 0.0)
            link(g_.memset(DTC[:, :, :].bitcast(F32), 0.0))
            g_.memset(OH[:, :, :].bitcast(F32), 0.0).then_inc(cur_ready, 1)

            def current(p):
                pool.wait_ge(ring2_ready, ring_ready(p, 3))
                pool.wait_ge(*ring_count(p - 1, 9))
                g_.tensor_tensor(DTC[:, :, :], DTN[:, :, :].bitcast(F32),
                                 ONE[:, :].rearrange("p (o c) -> p o c", o=1).broadcast_to([P, NT, P]), ALU.mult)
                g_.tensor_copy(CWC[:, :], CWN[:, :]).then_inc(cur_ready, 1)

            with pool.Fori(0, EXPERTS) as p:
                current(p)
            n_extra = pool.value_load(NUI[0:1, 0:1], min_val=0, max_val=EXTRA)
            for j in range(EXTRA):
                with pool.If(n_extra > j):
                    current(EXPERTS + j)
            rstd(3)
            pool.wait_ge(xn_act, 4)
            affine(3, None, (1,))


_INS = ["x", "mem", "a_w_in_first", "a_mu_first", "a_vec", "a_w_up", "a_a_up", "a_g_up", "a_r_k", "b_w_in",
        "w_kv_shared", "mem_kv", "w_o", "ln", "ffn_gate_up", "ffn_down", "router", "exp_gate_up", "exp_down"]


def kernel(**inputs):
    import numpy as np
    import concourse.bacc as bacc
    from concourse.bass_utils import run_bass_kernel_spmd

    nc = bacc.Bacc("TRN2", target_bir_lowering=False, num_devices=1)
    arrays, args = {}, []
    for name in _INS:
        a = np.ascontiguousarray(inputs[name])
        arrays[f"in_{name}"] = a
        args.append(nc.dram_tensor(f"in_{name}", a.shape, mybir.dt.from_np(a.dtype), kind="ExternalInput").ap())
    out = nc.dram_tensor("out", (1, T, D), F32, kind="ExternalOutput").ap()
    program(nc, *args, out)
    r = run_bass_kernel_spmd(nc, [arrays], core_ids=[0])
    return r.results[0]["out"]
```

```python
from contextlib import ExitStack

import concourse.bass as bass
from concourse import mybir

F32 = mybir.dt.float32
F32R = mybir.dt.float32r
I32 = mybir.dt.int32
U32 = mybir.dt.uint32
ALU = mybir.AluOpType
ACT = mybir.ActivationFunctionType
AX_X = mybir.AxisListType.X

P = 128
T = 256
D = 1024
KT = D // P
HALF = D // 2
NT = T // P
HEADS = 12
HD = 64
MIX = HEADS * HD
TILES = MIX // P
MEMH = 4
FF = 2816
FT = FF // P
EXPERTS = 8
EXTRA = 3
ALPHA = 4 ** 0.25
LN_EPS = 1e-5
GN_EPS = 64e-5
BETA = 0.6065306597126334
SCALE = HD ** -0.5

PIECE = 1024
PIECES = 6
SLOT = 3 * PIECE
SLOTS = 8
SEMS = 8


class Slab:

    def __init__(self, kind, loads, offset, size):
        self.kind, self.loads, self.offset, self.size = kind, loads, offset, size
        self.waits = 0
        self.first = None
        self.down = None


def plan_front(nslabs_before_ffn, nslabs_after_ffn):
    slabs = [Slab("A", None, 2 * PIECE * (n % 3), 2 * PIECE) for n in range(nslabs_before_ffn)]
    slabs += [Slab("B", None, SLOT * (n % 6), SLOT) for n in range(FT)]
    slabs += [Slab("A", None, SLOT * ((FT + n) % 6), 2 * PIECE) for n in range(nslabs_after_ffn)]
    pieces = []
    for n, s in enumerate(slabs):
        s.first = len(pieces)
        pieces += [(n, 0), (n, 1)]
        if s.kind == "B" and n > nslabs_before_ffn:
            slabs[n - 1].down = len(pieces)
            pieces.append((n - 1, 2))
        if s.kind == "B" and n == nslabs_before_ffn + FT - 1:
            s.down = len(pieces)
            pieces.append((n, 2))
    for n, s in enumerate(slabs):
        last = [m for m in range(n) if slabs[m].offset < s.offset + s.size and s.offset < slabs[m].offset + slabs[m].size]
        s.waits = max([max(slabs[m].first + 1, slabs[m].down or 0) + 1 for m in last], default=0)
    return slabs, pieces


def plan_pass():
    pieces = []
    for j in range(FT):
        pieces += [(j, 0), (j, 1)]
        if j >= 2:
            pieces.append((j - 2, 2))
    return pieces + [(FT - 2, 2), (FT - 1, 2)]


MOE_SLOT = [j % SLOTS for j in range(FT)]


def program(nc, x, mem, a_w_in_first, a_mu_first, a_vec, a_w_up, a_a_up, a_g_up, a_r_k, b_w_in,
            w_kv_shared, mem_kv, w_o, ln, ffn_gate_up, ffn_down, router, exp_gate_up, exp_down, out,
            dbg=None):
    with ExitStack() as ctx:
        def sem(name):
            return ctx.enter_context(nc.semaphore(name))

        base = nc.sbuf_base
        end = nc.sbuf_usable_end
        ctx.enter_context(nc.sbuf_tensor("arena", [P, (end - base) // 4 - 16], F32))
        base = (base + 31) // 32 * 32

        class Region:

            def __init__(self, at, limit):
                self.at, self.limit = at, limit

            def __call__(self, name, shape, dt=F32):
                n = 4
                for s in shape[1:]:
                    n *= s
                t = nc.alloc_sbuf_tensor_at(name, shape, dt, offset=self.at)
                self.at += (n + 31) // 32 * 32
                assert self.at <= self.limit, (name, self.at - self.limit)
                return t

        main = Region(base, end - 64)
        RAW = main("raw", [P, SLOTS * SLOT])
        WH = main("w_hi", [P, PIECES, PIECE], F32R)
        WL = main("w_lo", [P, PIECES, PIECE], F32R)
        X = main("x_tok", [P, NT, D])
        th_at = main.at
        TH = main("operand_hi", [P, KT, T], F32R)
        TL = main("operand_lo", [P, KT, T], F32R)
        gb_at = main.at
        GB = main("ln_rows", [P, 2, D])
        ID = main("ident", [P, P])
        SI = main("mask_after_upto", [P, 2, P])
        masks_at = main.at
        LS = main("mask_before", [P, P])
        BD = main("mask_blocks16", [P, P])
        LV = main("mask_levels", [P, 3, P])
        BO = main("ones_per_head", [P, P])
        masks_end = main.at
        NTRI = main("minus_suffix", [P, P])
        NONE = main("minus_ones", [P, P])
        IO = main("iota_row", [P, P])
        COLS = main("cols", [P, P])
        OMMU = main("one_minus_mu", [P, 20])
        OMKA = main("one_minus_ka", [P, 6])
        BN = main("bn", [P, NT, 4, 6])
        MV = main("mean_var", [P, NT, 2])
        RS = main("rstd", [P, NT])
        NM = main("minus_mean_rstd", [P, NT])
        EC = main("pow_exponent", [P, NT])
        SMX = main("smax", [P, MEMH, NT])
        SSM = main("ssum", [P, MEMH, NT])
        SRI = main("srecip", [P, MEMH, NT])
        EPS = main("eps", [P, 1])
        ONE = main("ones", [P, P])
        BM = main("mid", [P, 2, TILES, NT])
        WM = main("w_mid", [P, TILES])
        SC = main("state_scale", [P, TILES])
        mk_at = main.at
        MK = main("mem_keys", [P, 2, 2, T])
        MVA = main("mem_values", [P, 2, NT, T])
        free_at = main.at
        limit = end - 64

        l0 = Region(base + 4 * 2 * SLOT, base + 4 * SLOTS * SLOT)
        AR = l0("a_r", [P, TILES, NT, 2, P])
        BT = l0("b_scaled", [P, TILES, T])
        KK = l0("k_scaled", [P, TILES, T])
        V = l0("v_chan", [P, TILES, T])
        G = l0("gate", [P, TILES, T])
        CS = l0("decay_sum", [P, TILES, NT, P + 1])
        vt_at = l0.at
        VT = l0("v_tok", [P, NT, MIX])
        BKT = l0("bk_tok", [P, TILES, 2, P])
        Y = l0("y_tok", [P, NT, MIX])
        y_at = l0.at - 4 * NT * MIX
        S0 = l0("state", [P, TILES, HD])
        WUP = l0("wa_up", [P, MIX])
        GUP = l0("g_up", [P, MIX])
        WD = l0("wd_ad", [P, T])
        GD = l0("gd", [P, T])
        RN = nc.alloc_sbuf_tensor_at("rnorm", [P, TILES, T], F32, offset=y_at)
        YSQ = nc.alloc_sbuf_tensor_at("y_square", [P, NT, MIX], F32, offset=base + 4 * 2 * SLOT)
        memr = Region(vt_at, base + 4 * SLOTS * SLOT)
        MTH = memr("mem_hi", [P, KT, T], F32R)
        MTL = memr("mem_lo", [P, KT, T], F32R)
        small = Region(free_at, limit)
        QM = small("q_mem", [P, 2, T])
        lane_at = small.at
        ROWS = nc.alloc_sbuf_tensor_at("rows", [P, P], F32, offset=lane_at)
        EW = small("decay_to", [P, 2, NT, P + 1])
        EI = small("decay_from", [P, 2, NT, P])
        SQ = small("square", [P, 2, T])
        FM = small("k_factor", [P, 2, T])
        RK = small("rk", [P, 2, T])
        YT = nc.alloc_sbuf_tensor_at("y_norm_chan", [P, TILES, T], F32, offset=lane_at)
        GNS = nc.alloc_sbuf_tensor_at("gn_stats", [P, 4, NT, HEADS], F32, offset=lane_at + 4 * TILES * T)

        lanes = []
        for l in range(4):
            r = Region(th_at + 8192 * 0 + 6656 * l, limit) if l < 2 else Region(lane_at + 6656 * (l - 2), limit)
            lanes.append(dict(
                MR=r(f"mr{l}", [P, 2, P]), KR=r(f"kr{l}", [P, 2, P]), AL=r(f"al{l}", [P, P]),
                PX=r(f"px{l}", [P, 4, P]), LT=r(f"lt{l}", [P, 3, P]), Q1=r(f"q1{l}", [P, HD]), SA=r(f"sa{l}", [P, HD])))

        ma = Region(gb_at, gb_at + 8192)
        PR = ma("probs", [P, 2, NT, T])
        PT = ma("probs_t", [P, 2, NT, T])

        ff = Region(free_at, limit)
        FS = ff("ffn_silu", [P, NT, P])
        FH = ff("ffn_h", [P, NT, P])
        FHH = ff("ffn_ht_hi", [P, 2, T], F32R)
        FHL = ff("ffn_ht_lo", [P, 2, T], F32R)

        l1 = Region(base + 4 * 6 * SLOT, base + 4 * SLOTS * SLOT)
        KC = l1("k_chan", [P, TILES, T])
        VK = l1("vk_tok", [P, NT, MIX])
        QC = l1("q_chan", [P, TILES, T])
        QM1 = l1("q_mem1", [P, 2, T])
        l1t = Region(free_at, limit)
        MO = l1t("mem_out", [P, 2, T])
        SPA = l1t("softplus_a", [P, 2, 3, P])
        SP = l1t("softplus", [P, 3, 3, P])
        WT = l1t("weights_t", [P, 2, 3, P])

        me = Region(mk_at, limit)
        OH = me("out_hi", [P, 2, 512], F32R)
        OL = me("out_lo", [P, 2, 512], F32R)
        XGH = me("gathered_hi", [P, KT, P], F32R)
        XGL = me("gathered_lo", [P, KT, P], F32R)
        ES = me("exp_silu", [P, P])
        EH = me("exp_h", [P, P])
        EHH = me("exp_ht_hi", [P, 2, P], F32R)
        EHL = me("exp_ht_lo", [P, 2, P], F32R)
        DI = me("dispatch", [P, NT, P], F32R)
        DTN = me("dispatch_t_next", [P, NT, P], F32R)
        DTC = me("dispatch_t", [P, NT, P], F32R)
        NP = EXPERTS + EXTRA + 1
        RKP = me("rank_of_pass", [P, NT, NP])
        SLP = me("selected_of_pass", [P, NT, NP])
        CBP = me("weight_of_pass", [P, NT, NP])
        NUI = me("extras_int", [P, 4], I32)
        CPC = me("combine_of_slot_tok", [P, NT])
        CWN = me("slot_weight_next", [P, 1])
        CWC = me("slot_weight", [P, 1])
        ro = Region(me.at, limit)
        LG = ro("logits", [P, NT, 8])
        LGT = ro("logits_t", [8, T])
        MX8 = ro("top8", [P, NT, 8])
        IX8 = ro("top8_index", [P, NT, 8], U32)
        IXF = ro("top_index", [P, NT, 8])
        W12 = ro("top_weights", [P, NT, 4])
        OH1 = ro("one_hot1", [P, NT, 8])
        OH2 = ro("one_hot2", [P, NT, 8])
        SEL = ro("selected", [P, NT, 8])
        CMB = ro("combine", [P, NT, 8])
        RK8 = ro("rank", [P, NT, 8])
        OVR = ro("over", [P, 8])
        POS = ro("over_position", [P, 8])
        ro = Region(masks_at, masks_end)
        EXJ = ro("extra_is", [P, EXTRA, 8])
        PRD = ro("extra_products", [P, EXTRA, 3, NT, 8])
        PRE = ro("extra_index_products", [P, EXTRA, 8])
        ROW8 = IO[:, 0:EXPERTS]
        NUM = ro("extras", [P, 4])
        RTH = ro("router_raw", [P, KT, 8])
        RHI = ro("router_hi", [P, KT, 8], F32R)
        RLO = ro("router_lo", [P, KT, 8], F32R)

        bank = [ctx.enter_context(nc.psum_tensor(f"bank{b}", [P, 512], F32)) for b in range(8)]

        small_in = sem("small_in")
        mem_in, x_in = sem("mem_in"), sem("x_in")
        rows_in = sem("rows_in")
        router_in = sem("router_in")
        raw_in = [sem(f"raw_in{s}") for s in range(SEMS)]
        hi_done, lo_done, piece_used = sem("hi_done"), sem("lo_done"), sem("piece_used")
        consts_ready, cols_ready, mem_operand = sem("consts_ready"), sem("cols_ready"), sem("mem_operand")
        misc_ready, misc_act, misc_dve = sem("misc_ready"), sem("misc_act"), sem("misc_dve")
        a_ready, a_act, a_dve = sem("a_ready"), sem("a_act"), sem("a_dve")
        act_chain, dve_chain, pool_chain = sem("act_chain"), sem("dve_chain"), sem("pool_chain")
        lora_in_ready = sem("lora_in_ready")
        decay_ready, exp_ready, exp_used = sem("decay_ready"), sem("exp_ready"), sem("exp_used")
        square_ready, norm_sqrt, rk_ready = sem("square_ready"), sem("norm_sqrt"), sem("rk_ready")
        prep_done = sem("prep_done")
        lane_mm = [sem(f"lane_mm{l}") for l in range(4)]
        lane_act = [sem(f"lane_act{l}") for l in range(4)]
        lane_dve = [sem(f"lane_dve{l}") for l in range(4)]
        lane_pool = [sem(f"lane_pool{l}") for l in range(4)]
        state_ready = sem("state_ready")
        y_sqrt, y_ready, yt_bonus, yt_gated = sem("y_sqrt"), sem("y_ready"), sem("yt_bonus"), sem("yt_gated")
        y_var = sem("y_var")
        smax_ready, probs_ready, pt_ready = sem("smax_ready"), sem("probs_ready"), sem("pt_ready")
        psum_ready = sem("softmax_sum_ready")
        attn_hi = sem("attn_hi")
        stats_ready, rstd_ready, xn_act, x_parts = sem("stats_ready"), sem("rstd_ready"), sem("xn_act"), sem("x_parts_ready")
        res_part, logits_t_ready, logits_t_copied = sem("residual_part"), sem("logits_t_ready"), sem("logits_t_copied")
        x_ready = sem("x_ready")
        tr_hi = sem("tr_hi")
        gu_ready, silu_ready, h_ready, ht_ready, ht_hi, ht_lo = (sem("gu_ready"), sem("silu_ready"), sem("h_ready"),
                                                                 sem("ht_ready"), sem("ht_hi"), sem("ht_lo"))
        ffn_out = sem("ffn_out")
        stick_abs, stick_ln, stick_sp, stick_masked = sem("stick_abs"), sem("stick_ln"), sem("stick_sp"), sem("stick_masked")
        cs_ready, stick_w = sem("cs_ready"), sem("stick_w")
        mem_out_hi, mem_out_lo = sem("mem_out_hi"), sem("mem_out_lo")
        x2_hi, x2_split = sem("x2_hi"), sem("x2_split")
        y_start = sem("y_start")
        top_ready, route_ready = sem("top_ready"), sem("route_ready")
        router_hi, router_split = sem("router_hi"), sem("router_split")
        eg_ready, es_ready, eh_ready, et_ready, eth_hi, eth_lo = (sem("eg_ready"), sem("es_ready"), sem("eh_ready"),
                                                                  sem("et_ready"), sem("eth_hi"), sem("eth_lo"))
        disp_ready, ring2_ready, ring2_free = sem("dispatch_ready"), sem("pair_ready"), sem("pair_free")
        out_hi_s, out_lo_s = sem("out_hi_ready"), sem("out_lo_ready")
        ring_act, ring_dve = sem("ring_emptied_act"), sem("ring_emptied_dve")
        cur_ready = sem("current_ready")
        top_diff, top_exp = sem("top_diff"), sem("top_exp")
        rank_ready, logits_ready = sem("rank_ready"), sem("logits_ready")
        cat_hi, cat_ready = sem("cat_hi"), sem("cat_ready")
        final_ready, stored = sem("final_ready"), sem("stored")

        A_BEFORE, A_AFTER = 19, 14
        slabs, pieces = plan_front(A_BEFORE, A_AFTER)
        NF = len(pieces)
        A_IDX = list(range(A_BEFORE)) + list(range(A_BEFORE + FT, len(slabs)))
        B0 = A_BEFORE
        W_ORDER = [9, 0, 1, 2, 3, 4, 5, 6, 7, 8, 10]

        def cols256(w, c):
            return w.rearrange("(k p) c -> p k c", p=P)[:, :, 256 * c:256 * c + 256]

        srcs = [cols256(mem_kv[0], 0), cols256(mem_kv[0], 1), cols256(mem_kv[1], 0), cols256(mem_kv[1], 1)]
        srcs += [cols256(a_w_in_first, c) for c in W_ORDER]
        srcs += [cols256(w_o[0], c) for c in range(4)]
        srcs += [cols256(b_w_in[0], 3)]
        srcs += [cols256(w_kv_shared, c) for c in range(6)]
        srcs += [cols256(b_w_in[0], c) for c in range(3)]
        srcs += [cols256(w_o[1], c) for c in range(4)]

        def raw_a(off):
            return RAW[:, off:off + 2 * PIECE].rearrange("p (k c) -> p k c", k=KT)

        def raw_gu(off):
            return RAW[:, off:off + 2 * PIECE].rearrange("p (k g c) -> p k g c", k=KT, g=2)

        def gate_up(w):
            return w.rearrange("(k p) (g c) -> p k g c", p=P, g=2)

        for n, s in enumerate(A_IDX):
            slabs[s].loads = [(raw_a(slabs[s].offset), srcs[n])]
        for f in range(FT):
            s = slabs[B0 + f]
            w = gate_up(ffn_gate_up[0])
            s.loads = [(raw_gu(s.offset)[:, :, g, :], w[:, :, g, P * f:P * f + P]) for g in range(2)]
            s.loads.append((RAW[:, s.offset + 2 * PIECE:s.offset + SLOT], ffn_down[0, P * f:P * f + P, :]))
        sem_count = [0] * SEMS
        for n, s in enumerate(slabs):
            sem_count[n % SEMS] += 16 * len(s.loads)
            s.sem, s.count = raw_in[n % SEMS], sem_count[n % SEMS]
        MOE_BASE = list(sem_count)
        PER_PASS = [48 * MOE_SLOT.count(s) for s in range(SLOTS)]
        pass_pieces = plan_pass()
        PP = len(pass_pieces)
        DOWN_AT = {j: pass_pieces.index((j, 2)) for j in range(FT)}
        GU_AT = {j: pass_pieces.index((j, 0)) for j in range(FT)}
        last_use = {}
        for n, s in enumerate(slabs):
            for slot in range(SLOTS):
                if s.offset < SLOT * (slot + 1) and SLOT * slot < s.offset + s.size:
                    last_use[slot] = max(last_use.get(slot, 0), (s.down or s.first + 1) + 1)

        A_KIND = ["act"] * 4 + ["both"] * 10 + ["act"] + ["dve"] * 4 + ["act"] * 10 + ["dve"] * 4
        A_ACT = [sum(k in ("act", "both") for k in A_KIND[:n + 1]) for n in range(len(A_KIND))]
        A_DVE = [sum(k in ("dve", "both") for k in A_KIND[:n + 1]) for n in range(len(A_KIND))]

        uses = [("cols", 0, "dve")]
        uses += [("tr0", q, "dve") for q in range(4)] + [("tr1", q, "dve") for q in range(4)]
        for i in range(TILES):
            uses += [("up", i, "act"), ("gate", i, "act")]
        uses += [("norm", i, "dve") for i in range(TILES)]
        for i in range(TILES):
            uses += [("vt", i, "act"), ("bonus", i, "dve")]
        uses += [("bk", i, "act") for i in range(TILES)]

        def mem_uses(l):
            u = []
            for h in range(MEMH):
                if h == 0:
                    u += [(f"s{l}", 0, "act")]
                if h + 1 < MEMH:
                    u += [(f"s{l}", h + 1, "act")]
                u += [(f"pt{l}", h, "dve")]
                if h % 2:
                    u += [(f"mo{l}", h // 2, "dve")]
            return u

        def mem_step_uses(l, n):
            u = []
            if n < MEMH:
                u += [(f"s{l}", n, "act")]
            if 1 <= n <= MEMH:
                u += [(f"pt{l}", n - 1, "dve")]
            if n >= 3 and n % 2 == 1:
                u += [(f"mo{l}", (n - 3) // 2, "act")]
            return u

        uses += mem_uses(0)
        uses += [("yt", i, "act") for i in range(TILES)]
        uses += [("tr2", q, "dve") for q in range(4)]
        N_BEFORE_FFN = len(uses)
        uses += [("tr3", q, "dve") for q in range(4)]
        for n in range(MEMH + 2):
            uses += mem_step_uses(1, n)
        for s in range(HEADS + 3):
            if s < HEADS:
                uses.append(("z", s, "act"))
            if s >= 4 and s % 2 == 0:
                uses.append(("so", (s - 4) // 2, "dve"))
        uses += [("tr4", q, "dve") for q in range(4)]
        USE = {(n, i): u for u, (n, i, _) in enumerate(uses)}

        def use_bank(name, i):
            return bank[2 + USE[name, i] % 6]

        def emptied(u):
            who = uses[u][2]
            return (misc_act if who == "act" else misc_dve), sum(w == who for _, _, w in uses[:u + 1])

        def wait_ready(eng, name, i):
            eng.wait_ge(misc_ready, USE[name, i] + 1)

        def wait_emptied(eng, name, i):
            eng.wait_ge(*emptied(USE[name, i]))

        def wait_bank(eng, name, i):
            u = USE[name, i]
            if u >= 6:
                eng.wait_ge(*emptied(u - 6))

        MU, VEC, RKC = 0, 20, 56

        def col(n):
            return COLS[:, n:n + 1]

        NG = HEADS * NT // 4
        MEM1 = 21
        MM_N, ACT_N, DVE_N, POOL_N = 14, 10, 9, 4

        def job(g, l):
            return 4 * (g % 3) + l, g // 3

        RING = ["dve"] * 4 + ["act"] * 2 + ["dve"] * 2 + ["act"] * 2
        RING_ACT0, RING_DVE0, RING_ACT, RING_DVE = 4, 2, 4, 6
        RING0 = RING_ACT0 + RING_DVE0

        NONE_BEFORE = -1
        MOE_H0 = 2

        def ring_bank(r):
            return bank[5 + r % 2]

        def ring_count(p, r):
            n = sum(w == RING[r] for w in RING[:r + 1])
            if RING[r] == "act":
                return ring_act, p * RING_ACT + (RING_ACT0 + n)
            return ring_dve, p * RING_DVE + (RING_DVE0 + n)

        def ring_ready(p, r):
            return p * len(RING) + (RING0 + r + 1)

        AHEAD = 4

        def always(step):
            step()

        def last_passes(eng, expert, n_extra):
            def if_more_than(j):
                def follow(step):
                    with eng.If(n_extra > j):
                        step()
                return follow

            expert(EXPERTS - 1, if_more_than(0))
            for j in range(EXTRA):
                with eng.If(n_extra > j):
                    expert(EXPERTS + j, if_more_than(j + 1) if j + 1 < EXTRA else lambda step: None)

        XH = TH[:, :, :].rearrange("p k t -> p (k t)")
        XL = TL[:, :, :].rearrange("p k t -> p (k t)")

        def silu_view(b):
            return b[:, :].rearrange("p (t g c) -> p t g c", t=NT, g=2)

        block = ctx.enter_context(nc.Block())

        PARTS = [(0, 0), (1, 0), (0, 1)]

        def which_ln(idx):
            return idx // 2, 2 * (idx % 2)

        def rows_done(eng, idx):
            eng.wait_ge(x_parts, len(PARTS) * (idx + 1))
            eng.wait_ge(x_ready, idx + 1)

        @block.sync
        def _(sp):
            rows = ROWS[0:62, :]
            sp.dma_start(rows[0:20, :], a_mu_first.rearrange("(a p) -> a p", p=P)).then_inc(small_in, 16)
            sp.dma_start(rows[20:56, :], a_vec[0].rearrange("v (a p) -> (v a) p", p=P)).then_inc(small_in, 16)
            sp.dma_start(rows[56:62, :], a_r_k[0].rearrange("(a h) d -> a (h d)", h=2)).then_inc(small_in, 16)
            sp.dma_start(GB[:, :, :], mem[0].rearrange("(t p) d -> p t d", p=P)).then_inc(mem_in, 16)
            sp.dma_start(X[:, :, :], x[0].rearrange("(t p) d -> p t d", p=P)).then_inc(x_in, 16)
            sp.dma_start(WUP[0:64, :], a_w_up[0]).then_inc(small_in, 16)
            sp.dma_start(WUP[64:128, :], a_a_up[0]).then_inc(small_in, 16)
            sp.dma_start(GUP[:, :], a_g_up[0]).then_inc(small_in, 16)

            def rows_of(idx):
                l, v = which_ln(idx)
                for r in range(2):
                    sp.dma_start(GB[:, r, :], ln[l, v + r].rearrange("(a d) -> a d", a=1).broadcast_to([P, D]))\
                        .then_inc(rows_in, 16)

            def load(n):
                s = slabs[n]
                if s.waits:
                    sp.wait_ge(lo_done, s.waits)
                for dst, src in s.loads:
                    sp.dma_start(dst, src).then_inc(s.sem, 16)

            for n in range(B0 + 2):
                if n == B0 - 1:
                    wait_emptied(sp, "mo0", 1)
                    rows_of(0)
                load(n)
            sp.wait_ge(yt_gated, TILES)
            for n in range(B0 + 2, len(slabs)):
                load(n)
                if n == B0 + 10:
                    rows_done(sp, 0)
                    rows_of(1)
            rows_done(sp, 1)
            wait_emptied(sp, "mo1", 1)
            rows_of(2)
            wait_emptied(sp, "so", TILES - 1)
            sp.dma_start(RTH[:, :, :], router[0].rearrange("(k p) e -> p k e", p=P)).then_inc(router_in, 16)

            def pass_loads(p, e):
                for j in range(FT):
                    s = MOE_SLOT[j]
                    before = [m for m in range(j) if MOE_SLOT[m] == s]
                    if before:
                        sp.wait_ge(lo_done, NF + PP * p + DOWN_AT[before[-1]] + 1)
                    else:
                        m = max(m for m in range(FT) if MOE_SLOT[m] == s)
                        sp.wait_ge(lo_done, NF + PP * (p - 1) + DOWN_AT[m] + 1)
                    off = SLOT * s
                    w = exp_gate_up[0].rearrange("e (k p) (g c) -> e p k g c", p=P, g=2)
                    for g in range(2):
                        sp.dma_start(raw_gu(off)[:, :, g, :], w[e, :, :, g, P * j:P * j + P]).then_inc(raw_in[s], 16)
                    sp.dma_start(RAW[:, off + 2 * PIECE:off + SLOT], exp_down[0][e, P * j:P * j + P, :]).then_inc(raw_in[s], 16)

            sp.wait_ge(lo_done, max(last_use[s] for s in range(6)))
            with sp.Fori(0, EXPERTS) as e:
                pass_loads(e, e)
            sp.wait_ge(route_ready, 1)
            n_extra = sp.value_load(NUI[0:1, 0:1], min_val=0, max_val=EXTRA)
            for j in range(EXTRA):
                with sp.If(n_extra > j):
                    e = sp.value_load(NUI[0:1, 1 + j:2 + j], min_val=0, max_val=EXPERTS - 1)
                    pass_loads(EXPERTS + j, e)
            rows_done(sp, 2)
            rows_of(3)
            for t in range(NT):
                if t == 0:
                    sp.wait_ge(x_parts, len(PARTS) * 3 + 2)
                else:
                    rows_done(sp, 3)
                sp.dma_start(out[0, P * t:P * t + P, :], X[:, t, :]).then_inc(stored, 16)
            sp.wait_ge(stored, 16 * NT)


        @block.tensor
        def _(pe):
            def mm(out, lhsT, rhs, start=True, stop=True):
                return nc.tensor.matmul(out, lhsT, rhs, start=start, stop=stop, skip_group_check=True)

            def product(out, lh, ll, rh, rl, start, stop):
                mm(out, lh, rh, start, False)
                mm(out, lh, rl, False, False)
                return mm(out, ll, rh, False, stop)

            def transposes(name, src, before=lambda q: None):
                for q in range(4):
                    before(q)
                    wait_bank(pe, name, q)
                    b = use_bank(name, q)
                    for k in range(2):
                        for t in range(NT):
                            last = nc.tensor.transpose(b[:, k * T + t * P:k * T + t * P + P],
                                                       src[:, t, (2 * q + k) * P:(2 * q + k + 1) * P], ID[:, :])
                    last.then_inc(misc_ready, 1)

            def a_slab(a, channels, oh, ol):
                s = slabs[A_IDX[a]]
                if a >= 2:
                    if A_KIND[a - 2] != "dve":
                        pe.wait_ge(a_act, A_ACT[a - 2])
                    if A_KIND[a - 2] != "act":
                        pe.wait_ge(a_dve, A_DVE[a - 2])
                for pc in range(2):
                    q = s.first + pc
                    pe.wait_ge(lo_done, q + 1)
                    wh = WH[:, q % PIECES, :].rearrange("p (k c) -> p k c", k=4)
                    wl = WL[:, q % PIECES, :].rearrange("p (k c) -> p k c", k=4)
                    for kk in range(4):
                        k = 4 * pc + kk
                        for m in range(2):
                            o = bank[a % 2][:, T * m:T * m + T]
                            cut = slice(P * m, P * m + P)
                            first = k == 0 and m == 0
                            if channels:
                                last = product(o, wh[:, kk, cut], wl[:, kk, cut], oh[:, k, :], ol[:, k, :],
                                               first, k == KT - 1)
                            else:
                                last = product(o, oh[:, k, cut], ol[:, k, cut], wh[:, kk, :], wl[:, kk, :],
                                               first, k == KT - 1)
                    last.then_inc(piece_used, 1)

            pe.wait_ge(consts_ready, 1)
            pe.wait_ge(small_in, 6 * 16)
            nc.tensor.transpose(use_bank("cols", 0)[:, 0:62], ROWS[0:62, :], ID[0:62, 0:62]).then_inc(misc_ready, 1)
            pe.wait_ge(mem_in, 16)
            transposes("tr0", GB)
            wait_emptied(pe, "tr0", 3)
            for a in range(4):
                a_slab(a, a % 2 == 0, MTH, MTL)

            pe.wait_ge(x_in, 16)
            transposes("tr1", X)
            wait_emptied(pe, "tr1", 3)

            def lora(i):
                cut = slice(P * i, P * i + P)
                wait_bank(pe, "up", i)
                b = use_bank("up", i)
                mm(b[:, 0:T], WUP[0:HD, cut], WD[0:HD, :]).then_inc(misc_ready, 1)
                wait_bank(pe, "gate", i)
                mm(use_bank("gate", i)[:, T:2 * T], WUP[HD:P, cut], WD[HD:P, :])
                mm(use_bank("gate", i)[:, 0:T], GUP[:, cut], GD[:, :]).then_inc(misc_ready, 1)

            def norm(i):
                pe.wait_ge(square_ready, i + 1)
                wait_bank(pe, "norm", i)
                mm(use_bank("norm", i)[:, 0:T], BO[:, :], SQ[:, i % 2, :]).then_inc(misc_ready, 1)

            for a in range(4, 15):
                a_slab(a, True, TH, TL)
                if 5 <= a <= 7:
                    pe.wait_ge(lora_in_ready, 2)
                    for i in (2 * a - 10, 2 * a - 9):
                        lora(i)
                if 9 <= a <= 11:
                    for i in (2 * a - 18, 2 * a - 17):
                        norm(i)
            for i in range(TILES):
                pe.wait_ge(a_dve, A_DVE[13])
                wait_bank(pe, "vt", i)
                b = use_bank("vt", i)
                for c in range(NT):
                    last = nc.tensor.transpose(b[:, P * c:P * c + P], V[:, i, P * c:P * c + P], ID[:, :])
                last.then_inc(misc_ready, 1)
                pe.wait_ge(rk_ready, i + 1)
                wait_bank(pe, "bonus", i)
                mm(use_bank("bonus", i)[:, 0:T], BO[:, :], RK[:, i % 2, :]).then_inc(misc_ready, 1)
            for i in range(TILES):
                pe.wait_ge(exp_used, i + 1)
                wait_bank(pe, "bk", i)
                b = use_bank("bk", i)
                nc.tensor.transpose(b[:, 0:P], BT[:, i, 0:P], ID[:, :])
                nc.tensor.transpose(b[:, P:2 * P], KK[:, i, 0:P], ID[:, :]).then_inc(misc_ready, 1)

            wait_emptied(pe, "bk", TILES - 1)
            wait_emptied(pe, "bonus", TILES - 1)
            pe.wait_ge(a_act, A_ACT[14])
            for g in range(NG):
                for step in range(1, MM_N + 1):
                    for l in range(4):
                        h, c = job(g, l)
                        L = lanes[l]
                        i, hb = h // 2, HD * (h % 2)
                        rows = slice(hb, hb + HD)
                        PX = L["PX"]
                        b, other = bank[2 * l + step % 2], bank[2 * l + 1 - step % 2]
                        xt = PX[:, 2:4, :].rearrange("p a c -> p (a c)")

                        def act_at(n):
                            pe.wait_ge(lane_act[l], ACT_N * g + n)

                        def dve_at(n):
                            pe.wait_ge(lane_dve[l], DVE_N * g + n)

                        def pool_at(n):
                            pe.wait_ge(lane_pool[l], POOL_N * g + n)

                        if step == 1:
                            if g:
                                act_at(0)
                                dve_at(0)
                            ar = AR[rows, i, c, :, :].rearrange("p a c -> p (a c)")
                            tok = slice(P * c, P * c + P)
                            mm(bank[2 * l][:, 0:T], BT[rows, i, tok], ar)
                            mm(bank[2 * l][:, T:2 * T], KK[rows, i, tok], ar)
                            last = mm(bank[2 * l + 1][:, 0:P], AR[rows, i, c, 0, :], BT[rows, i, tok])
                        elif step == 2:
                            dve_at(3)
                            pool_at(3)
                            mm(b[:, 0:P], PX[:, 1, :], PX[:, 0, :])
                            last = mm(b[:, P:2 * P], PX[:, 0, :], PX[:, 1, :])
                        elif step in (3, 4):
                            act_at(step - 2)
                            if step == 4:
                                dve_at(4)
                            mm(b[:, 0:P], PX[:, 1, :], PX[:, 0, :])
                            mm(b[:, P:2 * P], PX[:, 0, :], PX[:, 1, :])
                            last = mm(other[:, 0:P], PX[:, 0, :], PX[:, 2, :])
                        elif step == 5:
                            act_at(3)
                            dve_at(5)
                            mm(b[:, 0:P], PX[:, 0, :], PX[:, 2, :])
                            if c:
                                pe.wait_ge(state_ready, h + 1)
                            last = mm(other[:, 0:HD], L["KR"][:, 0, :], VT[:, c, HD * h:HD * h + HD], True, c == 0)
                            if c:
                                last = mm(other[:, 0:HD], AR[rows, i, c, 0, :], S0[rows, i, :], False, True)
                        elif step == 6:
                            dve_at(6)
                            act_at(4)
                            last = nc.tensor.transpose(b[:, 0:P], PX[:, 2, :], ID[:, :])
                        elif step in (7, 9, 11):
                            lev = (step - 7) // 2
                            if step == 7:
                                pool_at(4)
                            else:
                                dve_at(6 + lev)
                            last = mm(b[:, 0:P], L["LT"][:, lev, :], PX[:, 2, :])
                        elif step in (8, 10, 12):
                            lev = (step - 8) // 2
                            act_at(6 + lev)
                            last = mm(b[:, 0:P], PX[:, 3, :], PX[:, 0, :])
                            if step < 12:
                                last = mm(b[:, P:2 * P], PX[:, 0, :], PX[:, 3, :])
                        elif step == 13:
                            dve_at(9)
                            last = mm(b[:, 0:HD], PX[:, 2, :], L["Q1"][:, :])
                        else:
                            act_at(9)
                            vt = VT[:, c, HD * h:HD * h + HD]
                            mm(b[:, 0:HD], L["MR"][:, 1, :], L["SA"][:, :], True, False)
                            last = mm(b[:, 0:HD], L["KR"][:, 1, :], vt, False, c == 0)
                            if c:
                                last = mm(b[:, 0:HD], AR[rows, i, c, 1, :], S0[rows, i, :], False, True)
                            else:
                                mm(b[rows, HD:2 * HD], BKT[:, i, 0, rows], L["SA"][:, :], True, False)
                                last = mm(b[rows, HD:2 * HD], BKT[:, i, 1, rows], vt, False, True)
                        last.then_inc(lane_mm[l], 1)
            for l in range(4):
                pe.wait_ge(lane_act[l], ACT_N * NG)

            def mem_attention(l, q):
                def scores(h):
                    i, hb = h // 2, HD * (h % 2)
                    wait_bank(pe, f"s{l}", h)
                    b = use_bank(f"s{l}", h)
                    for t in range(NT):
                        last = mm(b[:, T * t:T * t + T], q[hb:hb + HD, i, P * t:P * t + P], MK[hb:hb + HD, l, i, :])
                    last.then_inc(misc_ready, 1)

                for h in range(MEMH):
                    i, hb = h // 2, HD * (h % 2)
                    if h == 0:
                        scores(0)
                    if h + 1 < MEMH:
                        scores(h + 1)
                    pe.wait_ge(probs_ready, MEMH * l + h + 1)
                    wait_bank(pe, f"pt{l}", h)
                    b = use_bank(f"pt{l}", h)
                    for mt in range(2):
                        for t in range(NT):
                            last = nc.tensor.transpose(b[:, T * mt + P * t:T * mt + P * t + P],
                                                       PR[:, h % 2, t, P * mt:P * mt + P], ID[:, :])
                    last.then_inc(misc_ready, 1)
                    wait_emptied(pe, f"pt{l}", h)
                    if h % 2 == 0:
                        wait_bank(pe, f"mo{l}", i)
                    b = use_bank(f"mo{l}", i)
                    for mt in range(2):
                        last = mm(b[hb:hb + HD, 0:T], MVA[:, l, mt, HD * h:HD * h + HD], PT[:, h % 2, mt, :],
                                  mt == 0, mt == 1)
                    if h % 2:
                        last.then_inc(misc_ready, 1)

            def mem_step(l, q, n):
                if n < MEMH:
                    i, hb = n // 2, HD * (n % 2)
                    wait_bank(pe, f"s{l}", n)
                    b = use_bank(f"s{l}", n)
                    for t in range(NT):
                        last = mm(b[:, T * t:T * t + T], q[hb:hb + HD, i, P * t:P * t + P], MK[hb:hb + HD, l, i, :])
                    last.then_inc(misc_ready, 1)
                if 1 <= n <= MEMH:
                    h = n - 1
                    pe.wait_ge(probs_ready, MEMH * l + h + 1)
                    wait_bank(pe, f"pt{l}", h)
                    b = use_bank(f"pt{l}", h)
                    for mt in range(2):
                        for t in range(NT):
                            last = nc.tensor.transpose(b[:, T * mt + P * t:T * mt + P * t + P],
                                                       PR[:, h % 2, t, P * mt:P * mt + P], ID[:, :])
                    last.then_inc(misc_ready, 1)
                if n >= 2:
                    h = n - 2
                    i, hb = h // 2, HD * (h % 2)
                    wait_emptied(pe, f"pt{l}", h)
                    if h % 2 == 0:
                        wait_bank(pe, f"mo{l}", i)
                    b = use_bank(f"mo{l}", i)
                    for mt in range(2):
                        last = mm(b[hb:hb + HD, 0:T], MVA[:, l, mt, HD * h:HD * h + HD], PT[:, h % 2, mt, :],
                                  mt == 0, mt == 1)
                    if h % 2:
                        last.then_inc(misc_ready, 1)

            mem_attention(0, QM)
            pe.wait_ge(y_ready, 1)
            for i in range(TILES):
                wait_bank(pe, "yt", i)
                b = use_bank("yt", i)
                for c in range(NT):
                    last = nc.tensor.transpose(b[:, P * c:P * c + P], Y[:, c, P * i:P * i + P], ID[:, :])
                last.then_inc(misc_ready, 1)
            pe.wait_ge(cat_ready, TILES)
            for a in range(15, 19):
                a_slab(a, False, TH, TL)

            def normed(idx, name, after=lambda q: None):
                def parts_made(q):
                    if q == 0:
                        pe.wait_ge(x_parts, len(PARTS) * idx + 2)
                    elif q == 2:
                        rows_done(pe, idx)

                transposes(name, X, parts_made)
                for q in range(4):
                    wait_emptied(pe, name, q)
                    after(q)

            normed(0, "tr2")

            pe.wait_ge(a_dve, A_DVE[18])
            for f in range(FT + 1):
                if f < FT:
                    s = slabs[B0 + f]
                    if f >= 2:
                        pe.wait_ge(h_ready, f - 1)
                for pc in range(2):
                    if f < FT:
                        q = s.first + pc
                        pe.wait_ge(lo_done, q + 1)
                        wh = WH[:, q % PIECES, :].rearrange("p (k c) -> p k c", k=4)
                        wl = WL[:, q % PIECES, :].rearrange("p (k c) -> p k c", k=4)
                        for kk in range(4):
                            k = 4 * pc + kk
                            for t in range(NT):
                                cut = slice(P * t, P * t + P)
                                last = product(bank[f % 2][:, T * t:T * t + T], TH[:, k, cut], TL[:, k, cut],
                                               wh[:, kk, :], wl[:, kk, :], k == 0 and t == 0, k == KT - 1)
                        last.then_inc(piece_used, 1)
                    if pc == 0 and f:
                        pe.wait_ge(h_ready, f)
                        if f >= 3:
                            pe.wait_ge(ht_lo, f - 2)
                        b = bank[6 + (f - 1) % 2]
                        for t in range(NT):
                            last = nc.tensor.transpose(b[:, P * t:P * t + P], FH[:, t, :], ID[:, :])
                        last.then_inc(ht_ready, 1)
                if f:
                    pe.wait_ge(ht_lo, f)
                    q = slabs[B0 + f - 1].down
                    pe.wait_ge(lo_done, q + 1)
                    for t in range(NT):
                        cut = slice(P * t, P * t + P)
                        for half in range(2):
                            n = slice(512 * half, 512 * half + 512)
                            last = product(bank[2 + 2 * t + half][:, :], FHH[:, (f - 1) % 2, cut], FHL[:, (f - 1) % 2, cut],
                                           WH[:, q % PIECES, n], WL[:, q % PIECES, n], f == 1, f == FT)
                    last.then_inc(piece_used, 1)

            pe.wait_ge(ffn_out, 4)
            normed(1, "tr3")
            for a in range(19, 29):
                a_slab(a, a not in (23, 24, 25), TH, TL)
                if a == MEM1:
                    pe.wait_ge(a_act, A_ACT[19])
                if 0 <= a - MEM1 < MEMH + 2:
                    mem_step(1, QM1, a - MEM1)
            pe.wait_ge(a_act, A_ACT[28])

            for s in range(HEADS + 3):
                if s < HEADS:
                    h = s
                    i, rows = h // 2, slice(HD * (h % 2), HD * (h % 2) + HD)
                    wait_bank(pe, "z", h)
                    b = use_bank("z", h)
                    mm(b[:, 0:T], KC[rows, i, 0:P], QC[rows, i, :], True, False)
                    mm(b[:, T:T + P], KC[rows, i, P:T], QC[rows, i, P:T], False, False).then_inc(misc_ready, 1)
                if 2 <= s < HEADS + 2:
                    h = s - 2
                    b = use_bank("z", h)
                    pe.wait_ge(stick_masked, h + 1)
                    sp_ = SP[:, h % 3, :, :].rearrange("p a c -> p (a c)")
                    mm(b[:, 0:T], NTRI[:, :], sp_[:, 0:T], False, False)
                    mm(b[:, P:T], NONE[:, :], sp_[:, T:T + P], False, False)
                    mm(b[:, T:T + P], NTRI[:, :], sp_[:, T:T + P], False, True).then_inc(cs_ready, 1)
                if s >= 3:
                    h = s - 3
                    i, rows = h // 2, slice(HD * (h % 2), HD * (h % 2) + HD)
                    if h % 2 == 0:
                        wait_bank(pe, "so", i)
                    b = use_bank("so", i)
                    pe.wait_ge(stick_w, h + 1)
                    wt = WT[:, h % 2, :, :].rearrange("p a c -> p (a c)")
                    mm(b[rows, 0:T], VK[:, 0, HD * h:HD * h + HD], wt[:, 0:T], True, False)
                    last = mm(b[rows, P:T], VK[:, 1, HD * h:HD * h + HD], wt[:, T:T + P], False, True)
                    if h % 2:
                        last.then_inc(misc_ready, 1)
            wait_emptied(pe, "so", TILES - 1)
            pe.wait_ge(mem_out_lo, 1)
            for a in range(29, 33):
                a_slab(a, False, TH, TL)
            pe.wait_ge(a_dve, A_DVE[32])

            def logits(q):
                if q == 0:
                    pe.wait_ge(router_split, 1)
                for k in (2 * q, 2 * q + 1):
                    last = product(bank[0][0:EXPERTS, 0:T], RHI[:, k, :], RLO[:, k, :], TH[:, k, :], TL[:, k, :],
                                   k == 0, k == KT - 1)
                if q == 3:
                    last.then_inc(logits_t_ready, 1)

            normed(2, "tr4", logits)
            pe.wait_ge(logits_t_copied, 1)
            for t in range(NT):
                last = nc.tensor.transpose(bank[1][:, EXPERTS * t:EXPERTS * t + EXPERTS], LGT[:, P * t:P * t + P],
                                           ID[0:EXPERTS, 0:EXPERTS])
            last.then_inc(logits_ready, 1)

            pe.wait_ge(top_ready, 1)
            mm(bank[0][:, 0:16], SI[:, 0, :], SEL[:, :, :].rearrange("p t e -> p (t e)"), True, False)
            mm(bank[0][:, 8:16], ONE[:, :], SEL[:, 0, :], False, True)
            mm(bank[0][:, 16:24], ONE[:, :], SEL[:, 0, :], False, False)
            mm(bank[0][:, 16:24], ONE[:, :], SEL[:, 1, :], False, True).then_inc(rank_ready, 1)

            def gather(p, uses):
                for r in uses:
                    if p is NONE_BEFORE and r == 6:
                        pe.wait_ge(x2_split, 1)
                    src = XH if r < 6 else XL
                    if r >= 6 or p is not NONE_BEFORE:
                        pe.wait_ge(*ring_count(p, r - 2))
                    b = ring_bank(r)
                    for d in range(4):
                        for t in range(NT):
                            at = D * t + P * (4 * (r % 2) + d)
                            last = mm(b[:, P * d:P * d + P], src[:, at:at + P], DI[:, t, :], d == 0 and t == 0, t == NT - 1)
                    last.then_inc(ring2_ready, 1)

            def gather_slots(p):
                pe.wait_ge(*ring_count(p, 6))
                for t in range(NT):
                    last = nc.tensor.transpose(ring_bank(8)[:, P * t:P * t + P], DI[:, t, :].bitcast(F32), ID[:, :])
                last.then_inc(ring2_ready, 1)
                pe.wait_ge(*ring_count(p, 7))
                for t in range(NT):
                    last = mm(ring_bank(9)[:, 0:1], DI[:, t, :].bitcast(F32), CPC[:, t:t + 1], t == 0, t == NT - 1)
                last.then_inc(ring2_ready, 1)

            def scatter(p, uses):
                pe.wait_ge(out_lo_s, 2 * p + 2)
                for r in uses:
                    t, half = r // 2, r % 2
                    if r < 2:
                        pe.wait_ge(*ring_count(p - 1, 8 + r))
                    else:
                        pe.wait_ge(*ring_count(p, r - 2))
                    mm(ring_bank(r)[:, :], DTC[:, t, :], OH[:, half, :], True, False)
                    mm(ring_bank(r)[:, :], DTC[:, t, :], OL[:, half, :], False, True).then_inc(ring2_ready, 1)

            def expert(p):
                for j in range(FT + 2):
                    if j < FT:
                        pe.wait_ge(eh_ready, p * FT + (j - 1 + MOE_H0))
                        if j == 0:
                            pe.wait_ge(*ring_count(p - 1, 5))
                            pe.wait_ge(*ring_count(p - 1, 7))
                    for pc in range(2):
                        if j < FT:
                            r = GU_AT[j] + pc
                            pe.wait_ge(lo_done, p * PP + (NF + r + 1))
                            wh = WH[:, r % PIECES, :].rearrange("p (k c) -> p k c", k=4)
                            wl = WL[:, r % PIECES, :].rearrange("p (k c) -> p k c", k=4)
                            for kk in range(4):
                                k = 4 * pc + kk
                                last = product(bank[j % 2][:, 0:T], XGH[:, k, :], XGL[:, k, :], wh[:, kk, :], wl[:, kk, :],
                                               k == 0, k == KT - 1)
                            last.then_inc(piece_used, 1)
                        if pc == 0 and 1 <= j <= FT:
                            if j == FT:
                                pe.wait_ge(disp_ready, p * 3 + 6)
                                pe.wait_ge(cur_ready, p + 2)
                                gather(p, (4, 5))
                            pe.wait_ge(eh_ready, p * FT + (j + MOE_H0))
                            pe.wait_ge(eth_lo, p * FT + (j - 2 + MOE_H0))
                            nc.tensor.transpose(bank[4 + 3 * ((j - 1) % 2)][:, 0:P], EH[:, :], ID[:, :]).then_inc(et_ready, 1)
                    if j in (1, 2):
                        scatter(p, (0, 1) if j == 1 else (2, 3))
                    if j >= 2:
                        pe.wait_ge(eth_lo, p * FT + (j - 1 + MOE_H0))
                        r = DOWN_AT[j - 2]
                        pe.wait_ge(lo_done, p * PP + (NF + r + 1))
                        for half in range(2):
                            n = slice(512 * half, 512 * half + 512)
                            last = product(bank[2 + half][:, :], EHH[:, j % 2, :], EHL[:, j % 2, :],
                                           WH[:, r % PIECES, n], WL[:, r % PIECES, n], j == 2, j == FT + 1)
                        last.then_inc(piece_used, 1)
                    if j == FT:
                        gather(p, (6, 7))
                gather_slots(p)

            pe.wait_ge(x2_hi, 1)
            pe.wait_ge(disp_ready, 3)
            gather(NONE_BEFORE, (4, 5, 6, 7))
            gather_slots(NONE_BEFORE)
            with pe.Fori(0, EXPERTS) as p:
                expert(p)
            pe.wait_ge(route_ready, 1)
            n_extra = pe.value_load(NUI[0:1, 0:1], min_val=0, max_val=EXTRA)
            for j in range(EXTRA):
                with pe.If(n_extra > j):
                    expert(EXPERTS + j)
            scatter(n_extra + EXPERTS, (0, 1, 2, 3))

        @block.scalar
        def _(act):
            def copy(out, in_):
                return nc.scalar.activation(out, in_, ACT.Copy)

            chained = [0]

            def link(ins):
                chained[0] += 1
                ins.then_inc(act_chain, 1)
                act.wait_ge(act_chain, chained[0])

            split = [0]

            def split_to(q_end):
                for q in range(split[0], min(q_end, NF)):
                    n, pc = pieces[q]
                    s = slabs[n]
                    act.wait_ge(s.sem, s.count)
                    if q >= PIECES:
                        act.wait_ge(piece_used, q - PIECES + 1)
                    at = s.offset + PIECE * pc
                    copy(WH[:, q % PIECES, :], RAW[:, at:at + PIECE]).then_inc(hi_done, 1)
                split[0] = max(split[0], q_end)

            def a_filled(a):
                s = slabs[A_IDX[a]]
                split_to(s.first + PIECES)
                act.wait_ge(piece_used, s.first + 2)
                return bank[a % 2]

            def plain_hi(name, dst):
                for q in range(4):
                    wait_ready(act, name, q)
                    copy(dst[:, 2 * q:2 * q + 2, :].rearrange("p k t -> p (k t)"), use_bank(name, q)[:, :]).then_inc(tr_hi, 1)

            split_to(PIECES)
            plain_hi("tr0", MTH)
            for a in range(4):
                b = a_filled(a)
                dst = (MK if a % 2 == 0 else MVA)[:, a // 2, :, :].rearrange("p a c -> p (a c)")
                copy(dst, b[:, :]).then_inc(a_act, 1)
            plain_hi("tr1", TH)
            act.wait_ge(cols_ready, 1)

            def lora(i):
                wait_ready(act, "up", i)
                b = use_bank("up", i)
                nc.scalar.activation(CS[:, i, :, 1:P + 1], b[:, 0:T].rearrange("p (c t) -> p c t", c=NT), ACT.Sigmoid,
                                     bias=col(VEC + i)).then_inc(misc_act, 1)
                wait_ready(act, "gate", i)
                nc.scalar.activation(BT[:, i, :], use_bank("gate", i)[:, T:2 * T], ACT.Sigmoid, bias=col(VEC + 6 + i))
                copy(G[:, i, :], use_bank("gate", i)[:, 0:T]).then_inc(misc_act, 1)

            for a in range(4, 15):
                b = a_filled(a)
                w = W_ORDER[a - 4]
                if w == 10:
                    nc.scalar.activation(QM[:, :, :].rearrange("p a c -> p (a c)"), b[:, :], ACT.Copy, scale=SCALE).then_inc(a_act, 1)
                    continue
                for m in range(2):
                    tile = 2 * w + m
                    src = b[:, T * m:T * m + T]
                    if tile < 6:
                        dst = AR[:, tile, :, 1, :]
                        src = src.rearrange("p (c t) -> p c t", c=NT)
                    else:
                        dst = [KK, V][tile // 6 - 1][:, tile % 6, :] if tile < 18 else [WD, GD][tile - 18][:, :]
                    last = nc.scalar.activation(dst, src, ACT.Identity, scale=OMMU[:, tile:tile + 1])
                last.then_inc(a_act, 1)
                if a == 4:
                    act.wait_ge(a_dve, 1)
                    nc.scalar.activation(WD[0:HD, :], WD[0:HD, :], ACT.Tanh).then_inc(lora_in_ready, 1)
                    nc.scalar.activation(GD[:, :], GD[:, :], ACT.Sigmoid).then_inc(lora_in_ready, 1)
                if 5 <= a <= 7:
                    for i in (2 * a - 10, 2 * a - 9):
                        lora(i)
                if a == 12:
                    wait_emptied(act, "norm", TILES - 1)
                    nc.scalar.activation(RN[:, :, :], RN[:, :, :], ACT.Sqrt).then_inc(norm_sqrt, 1)

            def exps(i):
                if i >= 2:
                    act.wait_ge(exp_used, i - 1)
                for c in range(NT):
                    nc.scalar.activation(EW[:, i % 2, c, :], CS[:, i, c, :], ACT.Exp, scale=-BETA, bias=BM[:, 0, i, c:c + 1])
                    nc.scalar.activation(EI[:, i % 2, c, :], CS[:, i, c, 1:P + 1], ACT.Exp, scale=BETA, bias=BM[:, 1, i, c:c + 1])
                nc.scalar.activation(WM[:, i:i + 1], BM[:, 0, i, 1:2], ACT.Exp, scale=-1.0).then_inc(exp_ready, 1)

            act.wait_ge(decay_ready, 1)
            exps(0)
            exps(1)
            for i in range(TILES):
                wait_ready(act, "vt", i)
                copy(VT[:, :, P * i:P * i + P], use_bank("vt", i)[:, 0:T].rearrange("p (c t) -> p c t", c=NT)).then_inc(misc_act, 1)
            for i in range(2, TILES):
                exps(i)
            for i in range(TILES):
                wait_ready(act, "bk", i)
                copy(BKT[:, i, :, :].rearrange("p a c -> p (a c)"), use_bank("bk", i)[:, 0:T]).then_inc(misc_act, 1)
            split_to(slabs[A_IDX[15]].first + PIECES)

            LANE_COPY = {2: 1, 3: 2, 4: 3, 5: 4, 6: 5, 7: 6, 9: 7, 11: 8, 13: 9, 14: 10}
            for g in range(NG):
                for step in LANE_COPY:
                    for l in range(4):
                        h, c = job(g, l)
                        L = lanes[l]
                        i, hb = h // 2, HD * (h % 2)
                        rows = slice(hb, hb + HD)
                        PX = L["PX"]
                        b = bank[2 * l + step % 2]
                        act.wait_ge(lane_mm[l], MM_N * g + step)
                        if step <= 4:
                            last = copy(PX[:, 0:2, :].rearrange("p a c -> p (a c)"), b[:, 0:T])
                        elif step == 5:
                            last = copy(L["Q1"][:, :], bank[2 * l][:, 0:HD])
                        elif step == 6:
                            last = copy(PX[:, 3, :], b[:, 0:P])
                        elif step <= 11:
                            last = copy(PX[:, 0, :], b[:, 0:P])
                        elif step == 13:
                            last = copy(L["SA"][:, :], b[:, 0:HD])
                        else:
                            if c == 0:
                                nc.scalar.activation(S0[rows, i, :], b[rows, HD:2 * HD], ACT.Identity,
                                                     scale=SC[rows, i:i + 1]).then_inc(state_ready, 1)
                            last = copy(Y[:, c, HD * h:HD * h + HD], b[:, 0:HD])
                        last.then_inc(lane_act[l], 1)

            def mem_attention(l):
                def exps_of(h):
                    act.wait_ge(smax_ready, MEMH * l + h + 1)
                    if h >= 2:
                        wait_ready(act, f"pt{l}", h - 2)
                    b = use_bank(f"s{l}", h)
                    for t in range(NT):
                        last = nc.scalar.activation(PR[:, h % 2, t, :], b[:, T * t:T * t + T], ACT.Exp,
                                                    bias=SMX[:, h, t:t + 1], accum_out=SSM[:, h, t:t + 1])
                    last.then_inc(misc_act, 1)

                for h in range(MEMH):
                    if h == 0:
                        exps_of(0)
                    if h + 1 < MEMH:
                        exps_of(h + 1)
                    if h % 2:
                        wait_ready(act, f"mo{l}", h // 2)
                        copy(TH[:, 6 + h // 2, :], use_bank(f"mo{l}", h // 2)[:, 0:T]).then_inc(attn_hi, 1)

            act.wait_ge(y_var, 1)
            nc.scalar.activation(YSQ[:, :, :], Y[:, :, :], ACT.Square).then_inc(y_sqrt, 1)
            act.wait_ge(y_var, 2)
            nc.scalar.activation(GNS[:, 2, :, :], GNS[:, 1, :, :], ACT.Sqrt, scale=1.0 / HD, bias=EPS[:, 0:1]).then_inc(y_sqrt, 1)
            mem_attention(0)
            for i in range(TILES):
                wait_ready(act, "yt", i)
                nc.scalar.activation(YT[:, i, :], use_bank("yt", i)[:, 0:T], ACT.Identity,
                                     scale=col(VEC + 24 + i), bias=col(VEC + 30 + i)).then_inc(misc_act, 1)
            for i in range(TILES):
                act.wait_ge(yt_gated, i + 1)
                copy(TH[:, i, :], YT[:, i, :]).then_inc(cat_hi, 1)

            def mem_step(l, n):
                if n < MEMH:
                    act.wait_ge(smax_ready, MEMH * l + n + 1)
                    if n >= 2:
                        wait_ready(act, f"pt{l}", n - 2)
                    b = use_bank(f"s{l}", n)
                    for t in range(NT):
                        last = nc.scalar.activation(PR[:, n % 2, t, :], b[:, T * t:T * t + T], ACT.Exp,
                                                    bias=SMX[:, n, t:t + 1], accum_out=SSM[:, n, t:t + 1])
                    last.then_inc(misc_act, 1)
                if n >= 3 and n % 2 == 1:
                    i = (n - 3) // 2
                    wait_ready(act, f"mo{l}", i)
                    copy(MO[:, i, :], use_bank(f"mo{l}", i)[:, 0:T]).then_inc(misc_act, 1)

            def normed(idx, name):
                act.wait_ge(rstd_ready, idx + 1)
                part = X[:, 1, HALF:D]
                nc.scalar.activation(part, part, ACT.Identity, scale=RS[:, 1:2], bias=NM[:, 1:2]).then_inc(xn_act, 1)
                if name:
                    plain_hi(name, TH)

            split_to(slabs[A_IDX[18]].first + PIECES)
            normed(0, "tr2")

            for f in range(FT + 1):
                if f < FT:
                    split_to(slabs[B0 + f].first + PIECES)
                if f:
                    act.wait_ge(ht_ready, f)
                    if f >= 3:
                        act.wait_ge(piece_used, slabs[B0 + f - 3].down + 1)
                    copy(FHH[:, (f - 1) % 2, :], bank[6 + (f - 1) % 2][:, 0:T]).then_inc(ht_hi, 1)
                if f < FT:
                    act.wait_ge(piece_used, slabs[B0 + f].first + 2)
                    if f:
                        act.wait_ge(h_ready, f)
                    nc.scalar.activation(FS[:, :, :], silu_view(bank[f % 2])[:, :, 0, :], ACT.Silu).then_inc(silu_ready, 1)
            split_to(slabs[A_IDX[19]].first + PIECES)
            normed(1, "tr3")
            for a in range(19, 29):
                b = a_filled(a)
                c = (a - 20) % 3
                if a == 19:
                    dst = QM1[:, :, :].rearrange("p a c -> p (a c)")
                elif 23 <= a < 26:
                    dst = VK[:, :, T * c:T * c + T]
                else:
                    dst = (KC if a < 23 else QC)[:, 2 * c:2 * c + 2, :].rearrange("p a c -> p (a c)")
                src = b[:, :].rearrange("p (t c) -> p t c", t=NT) if 23 <= a < 26 else b[:, :]
                nc.scalar.activation(dst, src, ACT.Copy, scale=SCALE if a == 19 or a >= 26 else 1.0).then_inc(a_act, 1)
                if a == MEM1:
                    rows_done(act, 1)
                if 0 <= a - MEM1 < MEMH + 2:
                    mem_step(1, a - MEM1)
            wait_emptied(act, "mo1", 1)
            copy(TH[:, TILES:KT, :], MO[:, :, :]).then_inc(mem_out_hi, 1)

            nc.scalar.preload_act_table_set("natural_log_exp_and_others")
            split_to(slabs[A_IDX[29]].first + PIECES)
            for s in range(HEADS + 4):
                if s < HEADS:
                    wait_ready(act, "z", s)
                    e = SPA[:, s % 2, :, :].rearrange("p a c -> p (a c)")
                    if s >= 2:
                        act.wait_ge(stick_sp, s - 1)
                    nc.scalar.activation(e, use_bank("z", s)[:, 0:3 * P], ACT.Abs).then_inc(stick_abs, 1)
                if 2 <= s < HEADS + 2:
                    h = s - 2
                    act.wait_ge(cs_ready, h + 1)
                    nc.scalar.activation(WT[:, h % 2, :, :].rearrange("p a c -> p (a c)"), use_bank("z", h)[:, 0:3 * P],
                                         ACT.Exp).then_inc(misc_act, 1)
                if s >= 5 and s % 2 == 1:
                    i = (s - 5) // 2
                    wait_ready(act, "so", i)
                    copy(TH[:, i, :], use_bank("so", i)[:, 0:T]).then_inc(attn_hi, 1)
                if s < HEADS:
                    act.wait_ge(stick_abs, s + 1)
                    link(nc.scalar.activation(e, e, ACT.Exp, scale=-1.0))
                    nc.scalar.activation(e, e, ACT.Ln, bias=1.0).then_inc(stick_ln, 1)
            for a in range(29, 33):
                split_to(slabs[A_IDX[a]].first + PIECES)
            act.wait_ge(router_in, 16)
            copy(RHI[:, :, :], RTH[:, :, :]).then_inc(router_hi, 1)
            normed(2, "tr4")

            act.wait_ge(logits_t_ready, 1)
            rows_done(act, 2)
            copy(XH, X[:, :, :].rearrange("p t d -> p (t d)")).then_inc(x2_hi, 1)
            act.wait_ge(top_diff, 1)
            for t in range(NT):
                last = nc.scalar.activation(W12[:, t, 0:1], W12[:, t, 3:4], ACT.Exp)
            last.then_inc(top_exp, 1)

            def gathered(p):
                for r in (4, 5):
                    act.wait_ge(ring2_ready, ring_ready(p, r))
                    half = r % 2
                    copy(XGH[:, 4 * half:4 * half + 4, :].rearrange("p a c -> p (a c)"), ring_bank(r)[:, :]).then_inc(ring_act, 1)

            def gathered_slots(p):
                act.wait_ge(ring2_ready, ring_ready(p, 8))
                copy(DTN[:, :, :].rearrange("p a c -> p (a c)"), ring_bank(8)[:, 0:T]).then_inc(ring_act, 1)
                act.wait_ge(ring2_ready, ring_ready(p, 9))
                copy(CWN[:, :], ring_bank(9)[:, 0:1]).then_inc(ring_act, 1)

            def out_hi(p):
                for half in range(2):
                    nc.scalar.activation(OH[:, half, :], bank[2 + half][:, :], ACT.Copy, scale=CWC[:, 0:1]).then_inc(out_hi_s, 1)

            def hi_parts(p, first, end):
                for r in range(first, end):
                    m, pc = pass_pieces[r]
                    s = MOE_SLOT[m]
                    if r == GU_AT[m]:
                        times = sum(MOE_SLOT[x] == s for x in range(m + 1))
                        act.wait_ge(raw_in[s], p * PER_PASS[s] + (MOE_BASE[s] + 48 * times))
                    act.wait_ge(piece_used, p * PP + (NF + r - PIECES + 1))
                    at = SLOT * s + PIECE * pc
                    copy(WH[:, r % PIECES, :], RAW[:, at:at + PIECE]).then_inc(hi_done, 1)

            def expert(p, follow):
                done = AHEAD
                nc.scalar.preload_act_table(ACT.Silu)
                for j in range(FT + 1):
                    upto = AHEAD + 1 if j == 0 else min(GU_AT[min(j, FT - 1)] + PIECES, PP)
                    hi_parts(p, done, upto)
                    done = max(done, upto)
                    if j == FT - 1:
                        follow(lambda: hi_parts(p + 1, 0, 1))
                    if j == 0:
                        act.wait_ge(piece_used, p * PP + NF)
                        act.wait_ge(cur_ready, p + 1)
                        out_hi(p)
                    if j == FT:
                        follow(lambda: hi_parts(p + 1, 1, 3))
                        gathered(p)
                    if j:
                        act.wait_ge(et_ready, p * FT + j)
                        copy(EHH[:, (j - 1) % 2, :], bank[4 + 3 * ((j - 1) % 2)][:, 0:P]).then_inc(eth_hi, 1)
                    if j < FT:
                        act.wait_ge(piece_used, p * PP + (NF + GU_AT[j] + 2))
                        act.wait_ge(eh_ready, p * FT + (j + MOE_H0))
                        nc.scalar.activation(ES[:, :], bank[j % 2][:, 0:P], ACT.Silu).then_inc(es_ready, 1)
                follow(lambda: hi_parts(p + 1, 3, AHEAD))
                gathered_slots(p)

            hi_parts(0, 0, 3)
            gathered(NONE_BEFORE)
            gathered_slots(NONE_BEFORE)
            hi_parts(0, 3, AHEAD)
            with act.Fori(0, EXPERTS - 1) as p:
                expert(p, always)
            act.wait_ge(route_ready, 1)
            n_extra = act.value_load(NUI[0:1, 0:1], min_val=0, max_val=EXTRA)
            last_passes(act, expert, n_extra)
            act.wait_ge(piece_used, (n_extra + EXPERTS) * PP + NF)
            act.wait_ge(cur_ready, n_extra + (EXPERTS + 1))
            out_hi(0)
            act.wait_ge(rstd_ready, 4)
            normed(3, None)

        @block.vector
        def _(dve):
            v = nc.vector
            chained = [0]

            def chain(ins):
                chained[0] += 1
                return ins.then_inc(dve_chain, 1)

            def settle():
                dve.wait_ge(dve_chain, chained[0])

            split = [0]

            def split_to(q_end):
                for q in range(split[0], min(q_end, NF)):
                    n, pc = pieces[q]
                    dve.wait_ge(hi_done, q + 1)
                    at = slabs[n].offset + PIECE * pc
                    v.tensor_tensor(WL[:, q % PIECES, :], RAW[:, at:at + PIECE], WH[:, q % PIECES, :].bitcast(F32),
                                    ALU.subtract).then_inc(lo_done, 1)
                split[0] = max(split[0], q_end)

            def low(out, full, hi):
                return v.tensor_tensor(out, full, hi.bitcast(F32), ALU.subtract)

            def plain_lo(name, hi, lo, base_count):
                for q in range(4):
                    dve.wait_ge(tr_hi, base_count + q + 1)
                    flat = lambda t: t[:, 2 * q:2 * q + 2, :].rearrange("p k t -> p (k t)")
                    low(flat(lo), use_bank(name, q)[:, :], flat(hi)).then_inc(misc_dve, 1)

            chain(v.memset(CS[:, :, :, 0:1], 0.0))
            wait_ready(dve, "cols", 0)
            v.tensor_copy(COLS[:, 0:62], use_bank("cols", 0)[:, 0:62]).then_inc(misc_dve, 1)
            dve.wait_ge(misc_dve, 1)
            v.tensor_scalar(OMMU[:, :], COLS[:, MU:MU + 20], -1.0, 1.0, ALU.mult, ALU.add)
            v.tensor_scalar(OMKA[:, :], COLS[:, VEC + 18:VEC + 24], -1.0, 1.0, ALU.mult, ALU.add).then_inc(cols_ready, 1)
            split_to(2)
            plain_lo("tr0", MTH, MTL, 0)
            for a in range(4):
                split_to(slabs[A_IDX[a]].first + PIECES)
            plain_lo("tr1", TH, TL, 4)

            def mixed(a, b):
                w = W_ORDER[a - 4]
                dve.wait_ge(a_act, A_ACT[a])
                for m in range(2):
                    tile = 2 * w + m
                    mu = col(MU + tile)
                    src = b[:, T * m:T * m + T]
                    if tile < 6:
                        dst = AR[:, tile, :, 1, :]
                        v.scalar_tensor_tensor(dst[:, 0, 1:P], src[:, 0:P - 1], mu, dst[:, 0, 1:P], ALU.mult, ALU.add)
                        last = v.scalar_tensor_tensor(dst[:, 1, :], src[:, P - 1:T - 1], mu, dst[:, 1, :], ALU.mult, ALU.add)
                    else:
                        dst = [KK, V][tile // 6 - 1][:, tile % 6, :] if tile < 18 else [WD, GD][tile - 18][:, :]
                        last = v.scalar_tensor_tensor(dst[:, 1:T], src[:, 0:T - 1], mu, dst[:, 1:T], ALU.mult, ALU.add)
                last.then_inc(a_dve, 1)

            for a in range(4, 14):
                split_to(slabs[A_IDX[a]].first + PIECES)
                mixed(a, bank[a % 2])
                if a == 8:
                    settle()
                    for i in range(TILES):
                        wait_emptied(dve, "up", i)
                        for c in range(NT):
                            s_ = CS[:, i, c, 1:P + 1]
                            chain(v.tensor_tensor_scan(s_, ONE[:, :], s_, 0.0, ALU.mult, ALU.add))
                    settle()
                    chain(v.tensor_scalar(BM[:, 0, :, :], CS[:, :, :, P // 2], BETA, None, ALU.mult))
                    v.tensor_scalar(BM[:, 1, :, :], CS[:, :, :, P // 2], -BETA, None, ALU.mult).then_inc(decay_ready, 1)
                if 9 <= a <= 11:
                    for i in (2 * a - 18, 2 * a - 17):
                        wait_ready(dve, "norm", i)
                        v.tensor_scalar(RN[:, i, :], use_bank("norm", i)[:, 0:T], 1e-24, None, ALU.max).then_inc(misc_dve, 1)
            split_to(slabs[A_IDX[14]].first + PIECES)

            dve.wait_ge(norm_sqrt, 1)
            chain(v.reciprocal(RN[:, :, :], RN[:, :, :]))
            settle()
            dve.wait_ge(square_ready, TILES)
            a_part = AR[:, :, :, 0, :]
            for i in range(TILES):
                chain(v.tensor_tensor(AR[:, i, :, 0, :], AR[:, i, :, 0, :], RN[:, i, :].rearrange("p (c t) -> p c t", c=NT), ALU.mult))
            for i in range(TILES):
                chain(v.tensor_scalar(FM[:, i % 2, :], BT[:, i, :], col(VEC + 18 + i), OMKA[:, i:i + 1], ALU.mult, ALU.add))
                settle()
                chain(v.tensor_tensor(KK[:, i, :], KK[:, i, :], FM[:, i % 2, :], ALU.mult))
                settle()
                if i >= 2:
                    wait_ready(dve, "bonus", i - 2)
                v.scalar_tensor_tensor(RK[:, i % 2, :].rearrange("p (c t) -> p c t", c=NT), AR[:, i, :, 1, :], col(RKC + i),
                                       KK[:, i, :].rearrange("p (c t) -> p c t", c=NT), ALU.mult, ALU.mult).then_inc(rk_ready, 1)
                if i >= 1:
                    bonus = i - 1
                    wait_ready(dve, "bonus", bonus)
                    wait_emptied(dve, "vt", bonus)
                    v.tensor_tensor(V[:, bonus, :], V[:, bonus, :], use_bank("bonus", bonus)[:, 0:T], ALU.mult).then_inc(misc_dve, 1)
                chain(v.tensor_tensor(BT[:, i, :].rearrange("p (c t) -> p c t", c=NT), BT[:, i, :].rearrange("p (c t) -> p c t", c=NT),
                                      AR[:, i, :, 0, :], ALU.mult))
            wait_ready(dve, "bonus", TILES - 1)
            wait_emptied(dve, "vt", TILES - 1)
            v.tensor_tensor(V[:, TILES - 1, :], V[:, TILES - 1, :], use_bank("bonus", TILES - 1)[:, 0:T], ALU.mult).then_inc(misc_dve, 1)
            dve.wait_ge(rk_ready, TILES)
            for i in range(TILES):
                dve.wait_ge(exp_ready, i + 1)
                settle()
                two = lambda t: t.rearrange("p (c t) -> p c t", c=NT)
                chain(v.tensor_tensor(AR[:, i, :, 1, :], AR[:, i, :, 1, :], EW[:, i % 2, :, 1:P + 1], ALU.mult))
                chain(v.scalar_tensor_tensor(AR[:, i, :, 0, :], AR[:, i, :, 0, :], -1.0, EW[:, i % 2, :, 0:P], ALU.mult, ALU.mult))
                chain(v.tensor_tensor(two(BT[:, i, :]), two(BT[:, i, :]), EI[:, i % 2, :, :], ALU.mult))
                chain(v.tensor_tensor(SC[:, i:i + 1], EW[:, i % 2, 0, P:P + 1], WM[:, i:i + 1], ALU.mult))
                v.tensor_tensor(two(KK[:, i, :]), two(KK[:, i, :]), EI[:, i % 2, :, :], ALU.mult).then_inc(exp_used, 1)
            split_to(slabs[A_IDX[15]].first + PIECES)

            for g in range(NG):
                for step in (1, 3, 4, 5, 8, 10, 12):
                    for l in range(4):
                        L = lanes[l]
                        PX = L["PX"]
                        b = bank[2 * l + step % 2]
                        dve.wait_ge(lane_mm[l], MM_N * g + step)
                        if step == 1:
                            if g:
                                dve.wait_ge(lane_pool[l], POOL_N * g)
                            si = SI[:, :, :].rearrange("p a c -> p (a c)")
                            flat = lambda t: t[:, :, :].rearrange("p a c -> p (a c)")
                            v.tensor_tensor(flat(L["MR"]), bank[2 * l][:, 0:T], si, ALU.mult).then_inc(lane_dve[l], 1)
                            v.tensor_tensor(flat(L["KR"]), bank[2 * l][:, T:2 * T], si, ALU.mult).then_inc(lane_dve[l], 1)
                            v.tensor_tensor(L["AL"][:, :], bank[2 * l + 1][:, 0:P], LS[:, :], ALU.mult).then_inc(lane_dve[l], 1)
                        elif step in (3, 4):
                            v.tensor_tensor(PX[:, 2, :], PX[:, 2, :], bank[2 * l + 1 - step % 2][:, 0:P], ALU.add).then_inc(lane_dve[l], 1)
                        elif step in (5, 12):
                            v.tensor_tensor(PX[:, 2, :], PX[:, 2, :], b[:, 0:P], ALU.add).then_inc(lane_dve[l], 1)
                        else:
                            xx = PX[:, 2:4, :].rearrange("p a c -> p (a c)")
                            v.tensor_tensor(xx, xx, b[:, 0:T], ALU.add).then_inc(lane_dve[l], 1)

            for l in range(4):
                dve.wait_ge(lane_act[l], ACT_N * NG)
            y3 = Y[:, :, :].rearrange("p c (h d) -> p (c h) d", d=HD)
            sq3 = YSQ[:, :, :].rearrange("p c (h d) -> p (c h) d", d=HD)

            def stat(n):
                return GNS[:, n, :, :].rearrange("p c h -> p (c h)")

            def spread(n):
                return stat(n).rearrange("p (h o) -> p h o", o=1).broadcast_to([P, NT * HEADS, HD])

            chain(v.tensor_reduce(stat(0), y3, AX_X, ALU.add))
            settle()
            chain(v.tensor_scalar(stat(0), stat(0), -1.0 / HD, None, ALU.mult))
            settle()
            v.tensor_tensor(y3, y3, spread(0), ALU.add).then_inc(y_var, 1)
            dve.wait_ge(y_sqrt, 1)
            v.tensor_reduce(stat(1), sq3, AX_X, ALU.add).then_inc(y_var, 1)
            dve.wait_ge(y_sqrt, 2)
            chain(v.reciprocal(stat(3), stat(2)))
            settle()
            v.tensor_tensor(y3, y3, spread(3), ALU.mult).then_inc(y_ready, 1)

            def mem_attention(l):
                def top(h):
                    wait_ready(dve, f"s{l}", h)
                    b = use_bank(f"s{l}", h)
                    chain(v.tensor_reduce(SMX[:, h, :], b[:, :].rearrange("p (t m) -> p t m", t=NT), AX_X, ALU.max))
                    settle()
                    v.tensor_scalar(SMX[:, h, :], SMX[:, h, :], -1.0, None, ALU.mult).then_inc(smax_ready, 1)

                for h in range(MEMH):
                    if h == 0:
                        top(0)
                    if h + 1 < MEMH:
                        top(h + 1)
                    wait_emptied(dve, f"s{l}", h)
                    chain(v.reciprocal(SRI[:, h, :], SSM[:, h, :]))
                    settle()
                    for t in range(NT):
                        last = v.tensor_scalar(PR[:, h % 2, t, :], PR[:, h % 2, t, :], SRI[:, h, t:t + 1], None, ALU.mult)
                    last.then_inc(probs_ready, 1)
                    wait_ready(dve, f"pt{l}", h)
                    v.tensor_copy(PT[:, h % 2, :, :].rearrange("p a c -> p (a c)"), use_bank(f"pt{l}", h)[:, :]).then_inc(misc_dve, 1)
                    if h % 2:
                        i = h // 2
                        dve.wait_ge(attn_hi, 2 * (l + 1) - 2 + i + 1 + (TILES if l else 0))
                        low(TL[:, 6 + i, :], use_bank(f"mo{l}", i)[:, 0:T], TH[:, 6 + i, :]).then_inc(misc_dve, 1)

            def mem_step(l, n):
                if n < MEMH:
                    wait_ready(dve, f"s{l}", n)
                    b = use_bank(f"s{l}", n)
                    chain(v.tensor_reduce(SMX[:, n, :], b[:, :].rearrange("p (t m) -> p t m", t=NT), AX_X, ALU.max))
                    settle()
                    v.tensor_scalar(SMX[:, n, :], SMX[:, n, :], -1.0, None, ALU.mult).then_inc(smax_ready, 1)
                if 1 <= n <= MEMH:
                    h = n - 1
                    wait_ready(dve, f"pt{l}", h)
                    v.tensor_copy(PT[:, h % 2, :, :].rearrange("p a c -> p (a c)"), use_bank(f"pt{l}", h)[:, :]).then_inc(misc_dve, 1)
                if n < MEMH:
                    wait_emptied(dve, f"s{l}", n)
                    chain(v.reciprocal(SRI[:, n, :], SSM[:, n, :]))
                    settle()
                    for t in range(NT):
                        last = v.tensor_scalar(PR[:, n % 2, t, :], PR[:, n % 2, t, :], SRI[:, n, t:t + 1], None, ALU.mult)
                    last.then_inc(probs_ready, 1)

            mem_attention(0)
            for i in range(TILES):
                dve.wait_ge(yt_bonus, i + 1)
                v.tensor_tensor(YT[:, i, :], YT[:, i, :], G[:, i, :], ALU.mult).then_inc(yt_gated, 1)
            for i in range(TILES):
                dve.wait_ge(cat_hi, i + 1)
                low(TL[:, i, :], YT[:, i, :], TH[:, i, :]).then_inc(cat_ready, 1)

            def residual(a):
                split_to(slabs[A_IDX[a]].first + PIECES)
                dve.wait_ge(piece_used, slabs[A_IDX[a]].first + 2)
                cut = slice(T * ((a - 15) % 14), T * ((a - 15) % 14) + T)
                v.scalar_tensor_tensor(X[:, :, cut], X[:, :, cut], ALPHA, bank[a % 2][:, :].rearrange("p (t c) -> p t c", t=NT),
                                       ALU.mult, ALU.add).then_inc(a_dve, 1)
                dve.wait_ge(a_dve, A_DVE[a])
                for t in range(NT):
                    chain(v.bn_stats(BN[:, t, (a - 15) % 14, :], X[:, t, cut]))

            def half_stats(t, half):
                chain(v.bn_stats(BN[:, t, half, :], X[:, t, HALF * half:HALF * half + HALF]))

            def rows_normed(idx, chunks, parts=PARTS):
                settle()
                for t in range(NT):
                    v.bn_aggr(MV[:, t, :], BN[:, t, 0:chunks, :]).then_inc(stats_ready, 1)
                dve.wait_ge(stats_ready, NT * (idx + 1))
                dve.wait_ge(rows_in, 32 * (idx + 1))

                def part(t, half):
                    return X[:, t, HALF * half:HALF * half + HALF]

                for t, half in parts:
                    chain(v.scalar_tensor_tensor(part(t, half), part(t, half), MV[:, t, 0:1],
                                                 GB[:, 0, HALF * half:HALF * half + HALF], ALU.subtract, ALU.mult))
                settle()
                dve.wait_ge(rstd_ready, idx + 1)
                for t, half in parts:
                    v.scalar_tensor_tensor(part(t, half), part(t, half), RS[:, t:t + 1],
                                           GB[:, 1, HALF * half:HALF * half + HALF], ALU.mult, ALU.add).then_inc(x_parts, 1)

            for a in range(15, 19):
                residual(a)
            rows_normed(0, 4)
            plain_lo("tr2", TH, TL, 8)

            for f in range(FT + 1):
                if f < FT:
                    split_to(slabs[B0 + f].first + PIECES)
                if f:
                    dve.wait_ge(ht_hi, f)
                    low(FHL[:, (f - 1) % 2, :], bank[6 + (f - 1) % 2][:, 0:T], FHH[:, (f - 1) % 2, :]).then_inc(ht_lo, 1)
                if f < FT:
                    dve.wait_ge(silu_ready, f + 1)
                    if f:
                        dve.wait_ge(ht_ready, f)
                    v.tensor_tensor(FH[:, :, :], FS[:, :, :], silu_view(bank[f % 2])[:, :, 1, :], ALU.mult).then_inc(h_ready, 1)
            split_to(slabs[A_IDX[19]].first + PIECES)
            dve.wait_ge(piece_used, slabs[B0 + FT - 1].down + 1)
            rows_done(dve, 0)
            for t in range(NT):
                for half in range(2):
                    n = slice(512 * half, 512 * half + 512)
                    v.scalar_tensor_tensor(X[:, t, n], X[:, t, n], ALPHA, bank[2 + 2 * t + half][:, :],
                                           ALU.mult, ALU.add).then_inc(ffn_out, 1)
                    if t or half:
                        dve.wait_ge(ffn_out, 2 * t + half)
                        half_stats((2 * t + half - 1) // 2, (half + 1) % 2)
            dve.wait_ge(ffn_out, 4)
            half_stats(1, 1)
            rows_normed(1, 2)
            plain_lo("tr3", TH, TL, 12)
            for a in range(19, 29):
                split_to(slabs[A_IDX[a]].first + PIECES)
                if a == MEM1:
                    rows_done(dve, 1)
                if 0 <= a - MEM1 < MEMH + 2:
                    mem_step(1, a - MEM1)
            split_to(slabs[A_IDX[29]].first + PIECES)
            dve.wait_ge(mem_out_hi, 1)
            low(TL[:, TILES:KT, :], MO[:, :, :], TH[:, TILES:KT, :]).then_inc(mem_out_lo, 1)

            flat3 = lambda t: t.rearrange("p a c -> p (a c)")
            for s in range(HEADS + 5):
                if 1 <= s <= HEADS:
                    h = s - 1
                    dve.wait_ge(stick_ln, h + 1)
                    if h >= 3:
                        dve.wait_ge(cs_ready, h - 2)
                    v.scalar_tensor_tensor(flat3(SP[:, h % 3, :, :]), use_bank("z", h)[:, 0:3 * P], 0.0,
                                           flat3(SPA[:, h % 2, :, :]), ALU.max, ALU.add).then_inc(stick_sp, 1)
                if s >= 6 and s % 2 == 0:
                    i = (s - 6) // 2
                    dve.wait_ge(attn_hi, 2 + i + 1)
                    low(TL[:, i, :], use_bank("so", i)[:, 0:T], TH[:, i, :]).then_inc(misc_dve, 1)
            for a in range(29, 33):
                residual(a)
            rows_normed(2, 4)
            dve.wait_ge(router_hi, 1)
            low(RLO[:, :, :], RTH[:, :, :], RHI[:, :, :]).then_inc(router_split, 1)
            plain_lo("tr4", TH, TL, 16)

            dve.wait_ge(logits_t_ready, 1)
            v.tensor_copy(LGT[:, :], bank[0][0:EXPERTS, 0:T]).then_inc(logits_t_copied, 1)
            dve.wait_ge(logits_ready, 1)
            chain(v.tensor_copy(LG[:, :, :].rearrange("p t e -> p (t e)"), bank[1][:, 0:16]))
            settle()
            for t in range(NT):
                chain(v.max(MX8[:, t, :], LG[:, t, :]))
            settle()
            for t in range(NT):
                chain(v.max_index(IX8[:, t, :], MX8[:, t, :], LG[:, t, :]))
                last = chain(v.tensor_tensor(W12[:, t, 3:4], MX8[:, t, 1:2], MX8[:, t, 0:1], ALU.subtract))
            settle()
            v.tensor_copy(IXF[:, :, :], IX8[:, :, :]).then_inc(top_diff, 1)
            dve.wait_ge(top_diff, 1)
            for t in range(NT):
                chain(v.tensor_scalar(OH1[:, t, :], ROW8, IXF[:, t, 0:1], None, ALU.is_equal))
                chain(v.tensor_scalar(OH2[:, t, :], ROW8, IXF[:, t, 1:2], None, ALU.is_equal))
            settle()
            v.tensor_tensor(SEL[:, :, :], OH1[:, :, :], OH2[:, :, :], ALU.add).then_inc(top_ready, 1)
            dve.wait_ge(top_exp, 1)
            chain(v.tensor_scalar(W12[:, :, 1:2], W12[:, :, 0:1], 1.0, None, ALU.add))
            settle()
            chain(v.reciprocal(W12[:, :, 1:2], W12[:, :, 1:2]))
            settle()
            chain(v.tensor_tensor(W12[:, :, 2:3], W12[:, :, 1:2], W12[:, :, 0:1], ALU.mult))
            settle()
            for t in range(NT):
                chain(v.tensor_scalar(OH1[:, t, :], OH1[:, t, :], W12[:, t, 1:2], None, ALU.mult))
            settle()
            for t in range(NT):
                chain(v.scalar_tensor_tensor(CMB[:, t, :], OH2[:, t, :], W12[:, t, 2:3], OH1[:, t, :], ALU.mult, ALU.add))
            dve.wait_ge(rank_ready, 1)
            chain(v.tensor_copy(RK8[:, :, :].rearrange("p t e -> p (t e)"), bank[0][:, 0:16]))
            chain(v.tensor_scalar(OVR[:, :], bank[0][:, 16:24], float(P), None, ALU.is_gt))
            settle()
            for n, dst in enumerate((RKP, SLP, CBP)):
                chain(v.tensor_copy(dst[:, :, 0:EXPERTS], (RK8, SEL, CMB)[n][:, :, :]))
                chain(v.memset(dst[:, :, NP - 1:NP], 0.0))
            settle()

            def dispatch(p):
                one = bass.ds(p, 1) if not isinstance(p, int) else slice(p, p + 1)
                for t in range(NT):
                    v.tensor_scalar(DI[:, t, :], IO[:, :], RKP[:, t, one], SLP[:, t, one], ALU.is_equal, ALU.mult)\
                        .then_inc(disp_ready, 1)
                v.tensor_copy(CPC[:, :], CBP[:, :, one].rearrange("p t o -> p (t o)")).then_inc(disp_ready, 1)

            dispatch(0)
            dve.wait_ge(x2_hi, 1)
            low(XL, X[:, :, :].rearrange("p t d -> p (t d)"), XH).then_inc(x2_split, 1)

            chain(v.tensor_tensor_scan(POS[:, :], ONE[:, 0:8], OVR[:, :], 0.0, ALU.mult, ALU.add))
            chain(v.memset(NUM[:, :], 0.0))
            settle()
            chain(v.tensor_copy(NUM[:, 0:1], POS[:, 7:8]))
            for j in range(EXTRA):
                chain(v.scalar_tensor_tensor(EXJ[:, j, :], POS[:, :], float(j + 1), OVR[:, :], ALU.is_equal, ALU.mult))
            settle()
            for j in range(EXTRA):
                chain(v.tensor_tensor(PRE[:, j, :], EXJ[:, j, :], ROW8, ALU.mult))
                for n, src in enumerate((RK8, SEL, CMB)):
                    for t in range(NT):
                        chain(v.tensor_tensor(PRD[:, j, n, t, :], src[:, t, :], EXJ[:, j, :], ALU.mult))
            settle()
            chain(v.tensor_reduce(NUM[:, 1:4], PRE[:, :, :], AX_X, ALU.add))
            for n, dst in enumerate((RKP, SLP, CBP)):
                for t in range(NT):
                    chain(v.tensor_reduce(dst[:, t, EXPERTS:EXPERTS + EXTRA], PRD[:, :, n, t, :], AX_X, ALU.add))
            settle()
            chain(v.tensor_scalar(RKP[:, :, EXPERTS:NP - 1], RKP[:, :, EXPERTS:NP - 1], -float(P), None, ALU.add))
            v.tensor_copy(NUI[:, :], NUM[:, :]).then_inc(route_ready, 1)
            settle()
            dve.wait_ge(route_ready, 1)
            for n in range(MOE_H0):
                v.memset(EH[:, HD * n:HD * n + HD], 0.0).then_inc(eh_ready, 1)
                v.memset(EHL[:, n, :].bitcast(F32), 0.0).then_inc(eth_lo, 1)
            dve.wait_ge(eh_ready, MOE_H0)
            dve.wait_ge(eth_lo, MOE_H0)

            def gathered(p):
                for r in (6, 7):
                    dve.wait_ge(ring2_ready, ring_ready(p, r))
                    half = r % 2
                    v.tensor_copy(XGL[:, 4 * half:4 * half + 4, :].rearrange("p a c -> p (a c)"), ring_bank(r)[:, :]).then_inc(ring_dve, 1)

            def out_lo(p):
                for half in range(2):
                    dve.wait_ge(out_hi_s, 2 * p + (half + 1))
                    v.scalar_tensor_tensor(OL[:, half, :], bank[2 + half][:, :], CWC[:, 0:1], OH[:, half, :].bitcast(F32),
                                           ALU.mult, ALU.subtract).then_inc(out_lo_s, 1)

            def scattered(p, uses):
                for r in uses:
                    t, half = r // 2, r % 2
                    n = slice(512 * half, 512 * half + 512)
                    dve.wait_ge(ring2_ready, ring_ready(p, r))
                    v.tensor_tensor(X[:, t, n], X[:, t, n], ring_bank(r)[:, :], ALU.add).then_inc(ring_dve, 1)

            def lo_parts(p, first, end):
                for r in range(first, end):
                    m, pc = pass_pieces[r]
                    dve.wait_ge(hi_done, p * PP + (NF + r + 1))
                    at = SLOT * MOE_SLOT[m] + PIECE * pc
                    v.tensor_tensor(WL[:, r % PIECES, :], RAW[:, at:at + PIECE], WH[:, r % PIECES, :].bitcast(F32),
                                    ALU.subtract).then_inc(lo_done, 1)

            def expert(p, follow):
                done = AHEAD
                for j in range(FT + 1):
                    if j in (2, 3):
                        dve.wait_ge(ring_dve, p * RING_DVE + RING_DVE0)
                        scattered(p, (0, 1) if j == 2 else (2, 3))
                    upto = AHEAD + 1 if j == 0 else min(GU_AT[min(j, FT - 1)] + PIECES, PP)
                    lo_parts(p, done, upto)
                    done = max(done, upto)
                    if j == FT - 1:
                        follow(lambda: lo_parts(p + 1, 0, 1))
                    if j == 0:
                        out_lo(p)
                    if j == FT - 3:
                        dve.wait_ge(ring2_ready, ring_ready(p - 1, 9))
                        dispatch(p + 1)
                    if j == FT:
                        follow(lambda: lo_parts(p + 1, 1, 3))
                    if j:
                        dve.wait_ge(eth_hi, p * FT + j)
                        low(EHL[:, (j - 1) % 2, :], bank[4 + 3 * ((j - 1) % 2)][:, 0:P], EHH[:, (j - 1) % 2, :]).then_inc(eth_lo, 1)
                    if j < FT:
                        dve.wait_ge(es_ready, p * FT + (j + 1))
                        if j:
                            dve.wait_ge(et_ready, p * FT + j)
                        v.tensor_tensor(EH[:, :], ES[:, :], bank[j % 2][:, P:T], ALU.mult).then_inc(eh_ready, 1)
                follow(lambda: lo_parts(p + 1, 3, AHEAD))
                gathered(p)

            gathered(NONE_BEFORE)
            lo_parts(0, 0, 3)
            lo_parts(0, 3, AHEAD)
            v.tensor_scalar(X[:, :, :], X[:, :, :], ALPHA, None, ALU.mult).then_inc(y_start, 1)
            dve.wait_ge(y_start, 1)
            with dve.Fori(0, EXPERTS - 1) as p:
                expert(p, always)
            n_extra = dve.value_load(NUI[0:1, 0:1], min_val=0, max_val=EXTRA)
            last_passes(dve, expert, n_extra)
            passes = n_extra + EXPERTS
            out_lo(passes)
            for r in range(4):
                scattered(passes, (r,))
                if r:
                    dve.wait_ge(ring_dve, passes * RING_DVE + (RING_DVE0 + r))
                    half_stats((r - 1) // 2, (r - 1) % 2)
            dve.wait_ge(ring_dve, passes * RING_DVE + (RING_DVE0 + 4))
            half_stats(1, 1)
            rows_normed(3, 2, [(0, 0), (0, 1), (1, 0)])

        @block.gpsimd
        def _(pool):
            g_ = nc.gpsimd
            chained = [0]

            def link(ins):
                chained[0] += 1
                ins.then_inc(pool_chain, 1)
                pool.wait_ge(pool_chain, chained[0])

            def select(t, pattern, base_, mult, op, fill):
                link(g_.affine_select(out=t, in_=t, compare_op=op, fill=fill, base=base_, pattern=pattern, channel_multiplier=mult))

            for t, value in ((ID, 0.0), (SI, 1.0), (LS, 1.0), (BD, 1.0), (LV, 1.0), (BO, 1.0), (NTRI, -1.0), (NONE, -1.0),
                             (ONE, 1.0), (EC, -0.5), (EPS, GN_EPS)):
                g_.memset(t[tuple([slice(None)] * len(t.shape))], value)
            link(g_.iota(IO[:, :], [[1, P]], base=0, channel_multiplier=0, allow_small_or_imprecise_dtypes=True))
            select(ID[:, :], [[-1, P]], 0, 1, ALU.not_equal, 1.0)
            select(SI[:, 0, :], [[1, P]], 0, -1, ALU.is_gt, 0.0)
            select(SI[:, 1, :], [[1, P]], 0, -1, ALU.is_ge, 0.0)
            select(LS[:, :], [[-1, P]], 0, 1, ALU.is_gt, 0.0)
            bd = BD[:, :].rearrange("p (b c) -> p b c", c=16)
            select(bd, [[-16, 8], [0, 16]], 0, 1, ALU.is_ge, 0.0)
            select(bd, [[16, 8], [0, 16]], 15, -1, ALU.is_ge, 0.0)
            bo = BO[:, :].rearrange("p (b c) -> p b c", c=HD)
            select(bo, [[-HD, 2], [0, HD]], 0, 1, ALU.is_ge, 0.0)
            select(bo, [[HD, 2], [0, HD]], HD - 1, -1, ALU.is_ge, 0.0)
            for lev in range(3):
                w = 16 << lev
                nb = P // (2 * w)
                lv = LV[:, lev, :].rearrange("p (b z c) -> p b z c", z=2, c=w)
                select(lv, [[0, nb], [-1, 2], [0, w]], 0, 0, ALU.is_ge, 0.0)
                select(lv, [[-2 * w, nb], [0, 2], [0, w]], -w, 1, ALU.is_ge, 0.0)
                select(lv, [[2 * w, nb], [0, 2], [0, w]], 2 * w - 1, -1, ALU.is_ge, 0.0)
            g_.affine_select(out=NTRI[:, :], in_=NTRI[:, :], compare_op=ALU.is_ge, fill=0.0, base=0, pattern=[[-1, P]],
                             channel_multiplier=1).then_inc(consts_ready, 1)
            pool.wait_ge(consts_ready, 1)

            pool.wait_ge(cols_ready, 1)
            for i in range(TILES):
                pool.wait_ge(a_dve, A_DVE[8 + i // 2])
                a2 = AR[:, i, :, 0, :]
                link(g_.tensor_scalar(a2, KK[:, i, :].rearrange("p (c t) -> p c t", c=NT), col(VEC + 12 + i), None, ALU.mult))
                if i >= 2:
                    wait_ready(pool, "norm", i - 2)
                g_.tensor_tensor(SQ[:, i % 2, :].rearrange("p (c t) -> p c t", c=NT), a2, a2, ALU.mult).then_inc(square_ready, 1)

            for g in range(NG):
                for l in range(4):
                    L = lanes[l]
                    PX = L["PX"]
                    pool.wait_ge(lane_dve[l], DVE_N * g + 1)
                    g_.tensor_tensor(PX[:, 1, :], L["MR"][:, 0, :], BD[:, :], ALU.mult).then_inc(lane_pool[l], 1)
                    pool.wait_ge(lane_dve[l], DVE_N * g + 3)
                    g_.tensor_tensor(PX[:, 0, :], L["AL"][:, :], BD[:, :], ALU.mult).then_inc(lane_pool[l], 1)
                    pool.wait_ge(lane_pool[l], POOL_N * g + 2)
                    g_.tensor_tensor(PX[:, 2, :], PX[:, 1, :], ID[:, :], ALU.add).then_inc(lane_pool[l], 1)
                for l in range(4):
                    L = lanes[l]
                    g_.tensor_tensor(L["LT"][:, :, :], L["AL"][:, :].rearrange("p (o c) -> p o c", o=1).broadcast_to([P, 3, P]),
                                     LV[:, :, :], ALU.mult).then_inc(lane_pool[l], 1)

            for i in range(TILES):
                wait_emptied(pool, "yt", i)
                g_.tensor_tensor(YT[:, i, :], YT[:, i, :], V[:, i, :], ALU.add).then_inc(yt_bonus, 1)

            def rstd(idx):
                pool.wait_ge(stats_ready, NT * (idx + 1))
                link(g_.tensor_scalar(RS[:, :], MV[:, :, 1], LN_EPS, None, ALU.add))
                link(g_.tensor_tensor(RS[:, :], RS[:, :], EC[:, :], ALU.pow))
                link(g_.tensor_scalar(NM[:, :], MV[:, :, 0], -1.0, None, ALU.mult))
                g_.tensor_tensor(NM[:, :], NM[:, :], RS[:, :], ALU.mult).then_inc(rstd_ready, 1)

            def affine(idx):
                rstd(idx)
                pool.wait_ge(rows_in, 32 * (idx + 1))
                pool.wait_ge(xn_act, idx + 1)
                part = X[:, 1, HALF:D]
                link(g_.tensor_tensor(part, part, GB[:, 0, HALF:D], ALU.mult))
                g_.tensor_tensor(part, part, GB[:, 1, HALF:D], ALU.add).then_inc(x_ready, 1)

            affine(0)
            affine(1)
            for s in range(HEADS + 1):
                if s < HEADS:
                    pool.wait_ge(stick_sp, s + 1)
                    t = SP[:, s % 3, 0:3:2, :]
                    g_.affine_select(out=t, in_=t, compare_op=ALU.is_gt, fill=0.0, base=0, pattern=[[0, 2], [1, P]],
                                     channel_multiplier=-1).then_inc(stick_masked, 1)
                if s:
                    wait_emptied(pool, "z", s - 1)
                    t = WT[:, (s - 1) % 2, 0:3:2, :]
                    g_.affine_select(out=t, in_=t, compare_op=ALU.is_gt, fill=0.0, base=0, pattern=[[0, 2], [1, P]],
                                     channel_multiplier=-1).then_inc(stick_w, 1)
            affine(2)
            g_.memset(CWC[:, :], 0.0)
            link(g_.memset(DTC[:, :, :].bitcast(F32), 0.0))
            g_.memset(OH[:, :, :].bitcast(F32), 0.0).then_inc(cur_ready, 1)

            def current(p):
                pool.wait_ge(ring2_ready, ring_ready(p, 3))
                pool.wait_ge(*ring_count(p - 1, 9))
                g_.tensor_tensor(DTC[:, :, :], DTN[:, :, :].bitcast(F32),
                                 ONE[:, :].rearrange("p (o c) -> p o c", o=1).broadcast_to([P, NT, P]), ALU.mult)
                g_.tensor_copy(CWC[:, :], CWN[:, :]).then_inc(cur_ready, 1)

            with pool.Fori(0, EXPERTS) as p:
                current(p)
            pool.wait_ge(route_ready, 1)
            n_extra = pool.value_load(NUI[0:1, 0:1], min_val=0, max_val=EXTRA)
            for j in range(EXTRA):
                with pool.If(n_extra > j):
                    current(EXPERTS + j)
            affine(3)


_INS = ["x", "mem", "a_w_in_first", "a_mu_first", "a_vec", "a_w_up", "a_a_up", "a_g_up", "a_r_k", "b_w_in",
        "w_kv_shared", "mem_kv", "w_o", "ln", "ffn_gate_up", "ffn_down", "router", "exp_gate_up", "exp_down"]


def kernel(**inputs):
    import numpy as np
    import concourse.bacc as bacc
    from concourse.bass_utils import run_bass_kernel_spmd

    nc = bacc.Bacc("TRN2", target_bir_lowering=False, num_devices=1)
    arrays, args = {}, []
    for name in _INS:
        a = np.ascontiguousarray(inputs[name])
        arrays[f"in_{name}"] = a
        args.append(nc.dram_tensor(f"in_{name}", a.shape, mybir.dt.from_np(a.dtype), kind="ExternalInput").ap())
    out = nc.dram_tensor("out", (1, T, D), F32, kind="ExternalOutput").ap()
    program(nc, *args, out)
    r = run_bass_kernel_spmd(nc, [arrays], core_ids=[0])
    return r.results[0]["out"]
```

```python
from contextlib import ExitStack

import concourse.bass as bass
from concourse import mybir

F32 = mybir.dt.float32
F32R = mybir.dt.float32r
I32 = mybir.dt.int32
U32 = mybir.dt.uint32
ALU = mybir.AluOpType
ACT = mybir.ActivationFunctionType
AX_X = mybir.AxisListType.X

P = 128
T = 256
D = 1024
KT = D // P
HALF = D // 2
NT = T // P
HEADS = 12
HD = 64
MIX = HEADS * HD
TILES = MIX // P
MEMH = 4
FF = 2816
FT = FF // P
EXPERTS = 8
EXTRA = 3
ALPHA = 4 ** 0.25
LN_EPS = 1e-5
GN_EPS = 64e-5
BETA = 0.6065306597126334
SCALE = HD ** -0.5

PIECE = 1024
PIECES = 6
SLOT = 3 * PIECE
SLOTS = 8
SEMS = 8


class Slab:

    def __init__(self, kind, loads, offset, size):
        self.kind, self.loads, self.offset, self.size = kind, loads, offset, size
        self.waits = 0
        self.first = None
        self.down = None


def plan_front(nslabs_before_ffn, nslabs_after_ffn):
    slabs = [Slab("A", None, 2 * PIECE * (n % 3), 2 * PIECE) for n in range(nslabs_before_ffn)]
    slabs += [Slab("B", None, SLOT * (n % 6), SLOT) for n in range(FT)]
    slabs += [Slab("A", None, SLOT * ((FT + n) % 6), 2 * PIECE) for n in range(nslabs_after_ffn)]
    pieces = []
    for n, s in enumerate(slabs):
        s.first = len(pieces)
        pieces += [(n, 0), (n, 1)]
        if s.kind == "B" and n > nslabs_before_ffn:
            slabs[n - 1].down = len(pieces)
            pieces.append((n - 1, 2))
        if s.kind == "B" and n == nslabs_before_ffn + FT - 1:
            s.down = len(pieces)
            pieces.append((n, 2))
    for n, s in enumerate(slabs):
        last = [m for m in range(n) if slabs[m].offset < s.offset + s.size and s.offset < slabs[m].offset + slabs[m].size]
        s.waits = max([max(slabs[m].first + 1, slabs[m].down or 0) + 1 for m in last], default=0)
    return slabs, pieces


def plan_pass():
    pieces = []
    for j in range(FT):
        pieces += [(j, 0), (j, 1)]
        if j >= 2:
            pieces.append((j - 2, 2))
    return pieces + [(FT - 2, 2), (FT - 1, 2)]


MOE_SLOT = [j % SLOTS for j in range(FT)]


def program(nc, x, mem, a_w_in_first, a_mu_first, a_vec, a_w_up, a_a_up, a_g_up, a_r_k, b_w_in,
            w_kv_shared, mem_kv, w_o, ln, ffn_gate_up, ffn_down, router, exp_gate_up, exp_down, out):
    with ExitStack() as ctx:
        def sem(name):
            return ctx.enter_context(nc.semaphore(name))

        base = nc.sbuf_base
        end = nc.sbuf_usable_end
        ctx.enter_context(nc.sbuf_tensor("arena", [P, (end - base) // 4 - 16], F32))
        base = (base + 31) // 32 * 32

        class Region:

            def __init__(self, at, limit):
                self.at, self.limit = at, limit

            def __call__(self, name, shape, dt=F32):
                n = 4
                for s in shape[1:]:
                    n *= s
                t = nc.alloc_sbuf_tensor_at(name, shape, dt, offset=self.at)
                self.at += (n + 31) // 32 * 32
                assert self.at <= self.limit, (name, self.at - self.limit)
                return t

        main = Region(base, end - 64)
        RAW = main("raw", [P, SLOTS * SLOT])
        WH = main("w_hi", [P, PIECES, PIECE], F32R)
        WL = main("w_lo", [P, PIECES, PIECE], F32R)
        X = main("x_tok", [P, NT, D])
        th_at = main.at
        TH = main("operand_hi", [P, KT, T], F32R)
        TL = main("operand_lo", [P, KT, T], F32R)
        gb_at = main.at
        GB = main("ln_rows", [P, 2, D])
        ID = main("ident", [P, P])
        SI = main("mask_after_upto", [P, 2, P])
        masks_at = main.at
        LS = main("mask_before", [P, P])
        BD = main("mask_blocks16", [P, 2, P])
        LV = main("mask_levels", [P, 3, P])
        BO = main("ones_per_head", [P, P])
        masks_end = main.at
        NTRI = main("minus_suffix", [P, P])
        NONE = main("minus_ones", [P, P])
        IO = main("iota_row", [P, P])
        COLS = main("cols", [P, P])
        OMMU = main("one_minus_mu", [P, 20])
        OMKA = main("one_minus_ka", [P, 6])
        BN = main("bn", [P, NT, 4, 6])
        MV = main("mean_var", [P, NT, 2])
        RS = main("rstd", [P, NT])
        NM = main("minus_mean_rstd", [P, NT])
        EC = main("pow_exponent", [P, NT])
        SMX = main("smax", [P, MEMH, NT])
        SSM = main("ssum", [P, MEMH, NT])
        SRI = main("srecip", [P, MEMH, NT])
        EPS = main("eps", [P, 1])
        ONE = main("ones", [P, P])
        BM = main("mid", [P, 2, TILES, NT])
        WM = main("w_mid", [P, TILES])
        SC = main("state_scale", [P, TILES])
        mk_at = main.at
        MK = main("mem_keys", [P, 2, 2, T])
        MVA = main("mem_values", [P, 2, NT, T])
        free_at = main.at
        limit = end - 64

        l0 = Region(base + 4 * 2 * SLOT, base + 4 * SLOTS * SLOT)
        AR = l0("a_r", [P, TILES, NT, 2, P])
        BT = l0("b_scaled", [P, TILES, T])
        KK = l0("k_scaled", [P, TILES, T])
        V = l0("v_chan", [P, TILES, T])
        G = l0("gate", [P, TILES, T])
        CS = l0("decay_sum", [P, TILES, NT, P + 1])
        vt_at = l0.at
        VT = l0("v_tok", [P, NT, MIX])
        BKT = l0("bk_tok", [P, TILES, 2, P])
        Y = l0("y_tok", [P, NT, MIX])
        y_at = l0.at - 4 * NT * MIX
        S0 = l0("state", [P, TILES, HD])
        WUP = l0("wa_up", [P, MIX])
        GUP = l0("g_up", [P, MIX])
        WD = l0("wd_ad", [P, T])
        GD = l0("gd", [P, T])
        before_y = Region(y_at, y_at + 4 * NT * MIX)
        SPR = before_y("spread_heads", [HEADS, TILES, P])
        IND = before_y("head_of_channel", [P, TILES, HEADS])
        RN = before_y("rnorm", [HEADS, T])
        memr = Region(vt_at, base + 4 * SLOTS * SLOT)
        MTH = memr("mem_hi", [P, KT, T], F32R)
        MTL = memr("mem_lo", [P, KT, T], F32R)
        small = Region(free_at, limit)
        QM = small("q_mem", [P, 2, T])
        lane_at = small.at
        ROWS = nc.alloc_sbuf_tensor_at("rows", [P, P], F32, offset=lane_at)
        EW = small("decay_to", [P, 2, NT, P + 1])
        EI = small("decay_from", [P, 2, NT, P])
        SQ = small("square", [P, 2, T])
        FM = small("k_factor", [P, 2, T])
        RK = small("rk", [P, 2, T])
        YT = nc.alloc_sbuf_tensor_at("y_norm_chan", [P, TILES, T], F32, offset=lane_at)
        LANE = 4 * (13 * P)
        gn = Region(th_at + 2 * LANE, gb_at)
        YSQ = gn("y_square", [P, 4 * HD])
        GNS = gn("gn_stats", [P, 4, 2 * TILES * NT])

        lanes = []
        for l in range(4):
            r = Region(th_at + LANE * l, limit) if l < 2 else Region(lane_at + LANE * (l - 2), limit)
            lanes.append(dict(
                MR=r(f"mr{l}", [P, 2, P]), KR=r(f"kr{l}", [P, 2, P]), AL=r(f"al{l}", [P, P]),
                PX=r(f"px{l}", [P, 4, P]), LT=r(f"lt{l}", [P, 3, P]), Q1=r(f"q1{l}", [P, HD]), SA=r(f"sa{l}", [P, HD])))

        ma = Region(gb_at, gb_at + 8192)
        PR = ma("probs", [P, 2, NT, T])
        PT = ma("probs_t", [P, 2, NT, T])

        ff = Region(free_at, limit)
        FS = ff("ffn_silu", [P, NT, P])
        FH = ff("ffn_h", [P, NT, P])
        FHH = ff("ffn_ht_hi", [P, 2, T], F32R)
        FHL = ff("ffn_ht_lo", [P, 2, T], F32R)

        l1 = Region(base + 4 * 6 * SLOT, base + 4 * SLOTS * SLOT)
        KC = l1("k_chan", [P, TILES, T])
        VK = l1("vk_tok", [P, NT, MIX])
        QC = l1("q_chan", [P, TILES, T])
        QM1 = l1("q_mem1", [P, 2, T])
        l1t = Region(free_at, limit)
        MO = l1t("mem_out", [P, 2, T])
        SPA = l1t("softplus_a", [P, 2, 3, P])
        SP = l1t("softplus", [P, 3, 3, P])
        WT = l1t("weights_t", [P, 2, 3, P])

        me = Region(mk_at, limit)
        OH = me("out_hi", [P, 2, 512], F32R)
        OL = me("out_lo", [P, 2, 512], F32R)
        XGH = me("gathered_hi", [P, KT, P], F32R)
        XGL = me("gathered_lo", [P, KT, P], F32R)
        ES = me("exp_silu", [P, P])
        EH = me("exp_h", [P, P])
        EHH = me("exp_ht_hi", [P, 2, P], F32R)
        EHL = me("exp_ht_lo", [P, 2, P], F32R)
        DI = me("dispatch", [P, NT, P], F32R)
        DTN = me("dispatch_t_next", [P, NT, P], F32R)
        DTC = me("dispatch_t", [P, NT, P], F32R)
        NP = EXPERTS + EXTRA + 1
        RKP = me("rank_of_pass", [P, NT, NP])
        SLP = me("selected_of_pass", [P, NT, NP])
        CBP = me("weight_of_pass", [P, NT, NP])
        NUI = me("extras_int", [P, 4], I32)
        CPC = me("combine_of_slot_tok", [P, NT])
        CWN = me("slot_weight_next", [P, 1])
        CWC = me("slot_weight", [P, 1])
        ro = Region(me.at, limit)
        LG = ro("logits", [P, NT, 8])
        MX8 = ro("top8", [P, NT, 8])
        IX8 = ro("top8_index", [P, NT, 8], U32)
        IXF = ro("top_index", [P, NT, 8])
        W12 = ro("top_weights", [P, NT, 4])
        OH1 = ro("one_hot1", [P, NT, 8])
        OH2 = ro("one_hot2", [P, NT, 8])
        SEL = ro("selected", [P, NT, 8])
        CMB = ro("combine", [P, NT, 8])
        RK8 = ro("rank", [P, NT, 8])
        OVR = ro("over", [P, 8])
        POS = ro("over_position", [P, 8])
        ro = Region(masks_at, masks_end)
        LGT = ro("logits_t", [EXPERTS, T])
        EXJ = ro("extra_is", [P, EXTRA, 8])
        PRD = ro("extra_products", [P, EXTRA, 3, NT, 8])
        PRE = ro("extra_index_products", [P, EXTRA, 8])
        ROW8 = IO[:, 0:EXPERTS]
        NUM = ro("extras", [P, 4])
        RTH = ro("router_raw", [P, KT, 8])
        RHI = ro("router_hi", [P, KT, 8], F32R)
        RLO = ro("router_lo", [P, KT, 8], F32R)

        bank = [ctx.enter_context(nc.psum_tensor(f"bank{b}", [P, 512], F32)) for b in range(8)]

        small_in, up_in, ident_ready = sem("small_in"), sem("up_in"), sem("ident_ready")
        mem_in, x_in = sem("mem_in"), sem("x_in")
        rows_in = sem("rows_in")
        router_in = sem("router_in")
        raw_in = [sem(f"raw_in{s}") for s in range(SEMS)]
        down_in = [sem(f"down_in{s}") for s in range(SLOTS)]
        hi_done, lo_done, piece_used = sem("hi_done"), sem("lo_done"), sem("piece_used")
        consts_ready, cols_ready = sem("consts_ready"), sem("cols_ready")
        misc_ready, misc_act, misc_dve = sem("misc_ready"), sem("misc_act"), sem("misc_dve")
        a_act, a_dve = sem("a_act"), sem("a_dve")
        act_chain, dve_chain, pool_chain = sem("act_chain"), sem("dve_chain"), sem("pool_chain")
        lora_in_ready = sem("lora_in_ready")
        decay_ready, exp_ready, exp_used = sem("decay_ready"), sem("exp_ready"), sem("exp_used")
        bk_scaled, k_ready = sem("bk_scaled"), sem("k_ready")
        square_ready, square_used, norm_sqrt = sem("square_ready"), sem("square_used"), sem("norm_sqrt")
        rnorm_ready, heads_ready, rk_ready = sem("rnorm_ready"), sem("heads_ready"), sem("rk_ready")
        lane_mm = [sem(f"lane_mm{l}") for l in range(4)]
        lane_act = [sem(f"lane_act{l}") for l in range(4)]
        lane_dve = [sem(f"lane_dve{l}") for l in range(4)]
        lane_pool = [sem(f"lane_pool{l}") for l in range(4)]
        state_ready = sem("state_ready")
        y_sqrt, y_ready, yt_bonus, yt_gated = sem("y_sqrt"), sem("y_ready"), sem("yt_bonus"), sem("yt_gated")
        y_var = sem("y_var")
        smax_ready, probs_ready = sem("smax_ready"), sem("probs_ready")
        attn_hi = sem("attn_hi")
        stats_ready, rstd_ready, xn_act, x_parts = sem("stats_ready"), sem("rstd_ready"), sem("xn_act"), sem("x_parts_ready")
        logits_t_ready, logits_t_copied = sem("logits_t_ready"), sem("logits_t_copied")
        x_ready = sem("x_ready")
        tr_hi = sem("tr_hi")
        silu_ready, h_ready = sem("silu_ready"), sem("h_ready")
        ht_ready, ht_hi, ht_lo = sem("ht_ready"), sem("ht_hi"), sem("ht_lo")
        ffn_tile0, ffn_out = sem("ffn_tile0"), sem("ffn_out")
        stick_abs, stick_ln, stick_sp, stick_masked = sem("stick_abs"), sem("stick_ln"), sem("stick_sp"), sem("stick_masked")
        cs_ready, stick_w = sem("cs_ready"), sem("stick_w")
        mem_out_hi, mem_out_lo = sem("mem_out_hi"), sem("mem_out_lo")
        x2_hi, x2_split = sem("x2_hi"), sem("x2_split")
        y_start = sem("y_start")
        top_ready, route_ready = sem("top_ready"), sem("route_ready")
        router_hi, router_split = sem("router_hi"), sem("router_split")
        es_ready, eh_ready = sem("expert_silu_ready"), sem("expert_h_ready")
        et_ready, eth_hi, eth_lo = sem("expert_ht_ready"), sem("expert_ht_hi"), sem("expert_ht_lo")
        disp_ready, ring2_ready = sem("dispatch_ready"), sem("pair_ready")
        out_hi_s, out_lo_s = sem("out_hi_ready"), sem("out_lo_ready")
        ring_act, ring_dve = sem("ring_emptied_act"), sem("ring_emptied_dve")
        cur_ready = sem("current_ready")
        top_diff, top_exp = sem("top_diff"), sem("top_exp")
        rank_ready, logits_ready = sem("rank_ready"), sem("logits_ready")
        cat_hi, cat_ready = sem("cat_hi"), sem("cat_ready")
        stored = sem("stored")

        A_BEFORE, A_AFTER = 19, 14
        slabs, pieces = plan_front(A_BEFORE, A_AFTER)
        NF = len(pieces)
        A_IDX = list(range(A_BEFORE)) + list(range(A_BEFORE + FT, len(slabs)))
        B0 = A_BEFORE
        W_ORDER = [9, 10, 3, 4, 5, 0, 1, 2, 6, 7, 8]

        def cols256(w, c):
            return w.rearrange("(k p) c -> p k c", p=P)[:, :, 256 * c:256 * c + 256]

        srcs = [cols256(mem_kv[0], 0), cols256(mem_kv[0], 1), cols256(mem_kv[1], 0), cols256(mem_kv[1], 1)]
        srcs += [cols256(a_w_in_first, c) for c in W_ORDER]
        srcs += [cols256(w_o[0], c) for c in range(4)]
        srcs += [cols256(b_w_in[0], 3)]
        srcs += [cols256(w_kv_shared, c) for c in range(6)]
        srcs += [cols256(b_w_in[0], c) for c in range(3)]
        srcs += [cols256(w_o[1], c) for c in range(4)]

        def raw_a(off):
            return RAW[:, off:off + 2 * PIECE].rearrange("p (k c) -> p k c", k=KT)

        def raw_gu(off):
            return RAW[:, off:off + 2 * PIECE].rearrange("p (k g c) -> p k g c", k=KT, g=2)

        def gate_up(w):
            return w.rearrange("(k p) (g c) -> p k g c", p=P, g=2)

        for n, s in enumerate(A_IDX):
            slabs[s].loads = [(raw_a(slabs[s].offset), srcs[n])]
        for f in range(FT):
            s = slabs[B0 + f]
            w = gate_up(ffn_gate_up[0])
            s.loads = [(raw_gu(s.offset)[:, :, g, :], w[:, :, g, P * f:P * f + P]) for g in range(2)]
            s.loads.append((RAW[:, s.offset + 2 * PIECE:s.offset + SLOT], ffn_down[0, P * f:P * f + P, :]))
        sem_count = [0] * SEMS
        for n, s in enumerate(slabs):
            sem_count[n % SEMS] += 16 * len(s.loads)
            s.sem, s.count = raw_in[n % SEMS], sem_count[n % SEMS]
        MOE_BASE = list(sem_count)
        PER_PASS = [MOE_SLOT.count(s) for s in range(SLOTS)]
        pass_pieces = plan_pass()
        PP = len(pass_pieces)
        DOWN_AT = {j: pass_pieces.index((j, 2)) for j in range(FT)}
        GU_AT = {j: pass_pieces.index((j, 0)) for j in range(FT)}
        last_use = {}
        for n, s in enumerate(slabs):
            for slot in range(SLOTS):
                if s.offset < SLOT * (slot + 1) and SLOT * slot < s.offset + s.size:
                    last_use[slot] = max(last_use.get(slot, 0), (s.down or s.first + 1) + 1)

        MEM0, MEM1 = 10, 21

        A_KIND = ["act"] * 4 + ["both", "act"] + ["both"] * 9 + ["dve"] * 4 + ["act"] * 10 + ["dve"] * 4
        A_ACT = [sum(k in ("act", "both") for k in A_KIND[:n + 1]) for n in range(len(A_KIND))]
        A_DVE = [sum(k in ("dve", "both") for k in A_KIND[:n + 1]) for n in range(len(A_KIND))]

        uses = [("cols", 0, "dve")]
        uses += [("tr0", q, "dve") for q in range(4)] + [("tr1", q, "dve") for q in range(4)]
        for i in range(TILES):
            uses += [("up", i, "act"), ("gate", i, "act")]
        uses += [("norm", 0, "dve")]

        def mem_step_uses(l, n):
            u = []
            if n < MEMH:
                u += [(f"s{l}", n, "act")]
            if 1 <= n <= MEMH:
                u += [(f"pt{l}", n - 1, "dve")]
            if n >= 3 and n % 2 == 1:
                u += [(f"mo{l}", (n - 3) // 2, "act")]
            return u

        for a in range(MEM0, MEM0 + MEMH + 2):
            uses += mem_step_uses(0, a - MEM0)
            if a == MEM0 + 1:
                uses += [("spread", j, "dve") for j in range(TILES // 2)]
            if a >= MEM0 + 3:
                for kind, who in (("vt", "act"), ("bonus", "dve")):
                    uses += [(kind, i, who) for i in (2 * (a - MEM0 - 3), 2 * (a - MEM0 - 3) + 1)]
        uses += [("bk", i, "act") for i in range(TILES)]
        uses += [("yt", i, "act") for i in range(TILES)]
        uses += [("tr2", q, "dve") for q in range(4)]
        uses += [("tr3", q, "dve") for q in range(4)]
        for n in range(MEMH + 2):
            uses += mem_step_uses(1, n)
        for s in range(HEADS + 3):
            if s < HEADS:
                uses.append(("z", s, "act"))
            if s >= 4 and s % 2 == 0:
                uses.append(("so", (s - 4) // 2, "dve"))
        uses += [("tr4", q, "dve") for q in range(4)]
        USE = {(n, i): u for u, (n, i, _) in enumerate(uses)}

        def use_bank(name, i):
            return bank[2 + USE[name, i] % 6]

        def emptied(u):
            who = uses[u][2]
            return (misc_act if who == "act" else misc_dve), sum(w == who for _, _, w in uses[:u + 1])

        def wait_ready(eng, name, i):
            eng.wait_ge(misc_ready, USE[name, i] + 1)

        def wait_emptied(eng, name, i):
            eng.wait_ge(*emptied(USE[name, i]))

        def wait_bank(eng, name, i):
            u = USE[name, i]
            if u >= 6:
                eng.wait_ge(*emptied(u - 6))

        MU, VEC, RKC = 0, 20, 56

        def col(n):
            return COLS[:, n:n + 1]

        NG = HEADS * NT // 4
        MM_N, ACT_N, DVE_N, POOL_N = 14, 10, 11, 2

        def job(g, l):
            return 4 * (g % 3) + l, g // 3

        def y_of(g):
            at = HD * 4 * (g % 3)
            return Y[:, g // 3, at:at + 4 * HD]

        RING = ["dve"] * 4 + ["act"] * 2 + ["dve"] * 2 + ["act"] * 2
        RING_ACT0, RING_DVE0, RING_ACT, RING_DVE = 4, 2, 4, 6
        RING0 = RING_ACT0 + RING_DVE0

        NONE_BEFORE = -1
        MOE_H0 = 2

        def ring_bank(r):
            return bank[5 + r % 2]

        def ring_count(p, r):
            n = sum(w == RING[r] for w in RING[:r + 1])
            if RING[r] == "act":
                return ring_act, p * RING_ACT + (RING_ACT0 + n)
            return ring_dve, p * RING_DVE + (RING_DVE0 + n)

        def ring_ready(p, r):
            return p * len(RING) + (RING0 + r + 1)

        AHEAD = 6

        def always(step):
            step()

        def last_passes(eng, expert, n_extra):
            def if_more_than(j):
                def follow(step):
                    with eng.If(n_extra > j):
                        step()
                return follow

            expert(EXPERTS - 1, if_more_than(0))
            for j in range(EXTRA):
                with eng.If(n_extra > j):
                    expert(EXPERTS + j, if_more_than(j + 1) if j + 1 < EXTRA else lambda step: None)

        XH = TH[:, :, :].rearrange("p k t -> p (k t)")
        XL = TL[:, :, :].rearrange("p k t -> p (k t)")

        def silu_view(b):
            return b[:, :].rearrange("p (t g c) -> p t g c", t=NT, g=2)

        block = ctx.enter_context(nc.Block())

        PARTS = [(0, 0), (1, 0), (0, 1)]

        def which_ln(idx):
            return idx // 2, 2 * (idx % 2)

        def rows_done(eng, idx):
            eng.wait_ge(x_parts, len(PARTS) * (idx + 1))
            eng.wait_ge(x_ready, idx + 1)

        @block.sync
        def _(sp):
            rows = ROWS[0:62, :]
            sp.dma_start(rows[0:20, :], a_mu_first.rearrange("(a p) -> a p", p=P)).then_inc(small_in, 16)
            sp.dma_start(rows[20:56, :], a_vec[0].rearrange("v (a p) -> (v a) p", p=P)).then_inc(small_in, 16)
            sp.dma_start(rows[56:62, :], a_r_k[0].rearrange("(a h) d -> a (h d)", h=2)).then_inc(small_in, 16)
            sp.dma_start(GB[:, :, :], mem[0].rearrange("(t p) d -> p t d", p=P)).then_inc(mem_in, 16)

            def rows_of(idx):
                l, v = which_ln(idx)
                for r in range(2):
                    sp.dma_start(GB[:, r, :], ln[l, v + r].rearrange("(a d) -> a d", a=1).broadcast_to([P, D]))\
                        .then_inc(rows_in, 16)

            def load(n):
                s = slabs[n]
                if s.waits:
                    sp.wait_ge(lo_done, s.waits)
                for dst, src in s.loads:
                    sp.dma_start(dst, src).then_inc(s.sem, 16)

            for n in range(B0 + 2):
                if n == B0 - 1:
                    wait_emptied(sp, "mo0", 1)
                    rows_of(0)
                load(n)
                if n == 2:
                    sp.dma_start(X[:, :, :], x[0].rearrange("(t p) d -> p t d", p=P)).then_inc(x_in, 16)
                    sp.dma_start(WUP[0:64, :], a_w_up[0]).then_inc(up_in, 16)
                    sp.dma_start(WUP[64:128, :], a_a_up[0]).then_inc(up_in, 16)
                    sp.dma_start(GUP[:, :], a_g_up[0]).then_inc(up_in, 16)
            sp.wait_ge(yt_gated, TILES)
            for n in range(B0 + 2, len(slabs)):
                load(n)
                if n == B0 + 10:
                    rows_done(sp, 0)
                    rows_of(1)
            rows_done(sp, 1)
            wait_emptied(sp, "mo1", 1)
            rows_of(2)
            wait_emptied(sp, "so", TILES - 1)
            sp.dma_start(RTH[:, :, :], router[0].rearrange("(k p) e -> p k e", p=P)).then_inc(router_in, 16)

            def pass_loads(p, e):
                w = exp_gate_up[0].rearrange("e (k p) (g c) -> e p k g c", p=P, g=2)
                for m, part in pass_pieces:
                    if part == 1:
                        continue
                    at, split_pieces = (GU_AT, 2) if part == 0 else (DOWN_AT, 1)
                    s = MOE_SLOT[m]
                    before = [x for x in range(m) if MOE_SLOT[x] == s]
                    if before:
                        sp.wait_ge(lo_done, NF + PP * p + at[before[-1]] + split_pieces)
                    else:
                        last = max(x for x in range(FT) if MOE_SLOT[x] == s)
                        sp.wait_ge(lo_done, NF + PP * (p - 1) + at[last] + split_pieces)
                    off = SLOT * s
                    if part == 0:
                        for g in range(2):
                            sp.dma_start(raw_gu(off)[:, :, g, :], w[e, :, :, g, P * m:P * m + P]).then_inc(raw_in[s], 16)
                    else:
                        sp.dma_start(RAW[:, off + 2 * PIECE:off + SLOT], exp_down[0][e, P * m:P * m + P, :]).then_inc(down_in[s], 16)

            sp.wait_ge(lo_done, max(last_use[s] for s in range(6)))
            with sp.Fori(0, EXPERTS) as e:
                pass_loads(e, e)
            sp.wait_ge(route_ready, 1)
            n_extra = sp.value_load(NUI[0:1, 0:1], min_val=0, max_val=EXTRA)
            for j in range(EXTRA):
                with sp.If(n_extra > j):
                    e = sp.value_load(NUI[0:1, 1 + j:2 + j], min_val=0, max_val=EXPERTS - 1)
                    pass_loads(EXPERTS + j, e)
            rows_done(sp, 2)
            rows_of(3)
            for t in range(NT):
                if t == 0:
                    sp.wait_ge(x_parts, len(PARTS) * 3 + 2)
                else:
                    rows_done(sp, 3)
                sp.dma_start(out[0, P * t:P * t + P, :], X[:, t, :]).then_inc(stored, 16)
            sp.wait_ge(stored, 16 * NT)


        @block.tensor
        def _(pe):
            def mm(out, lhsT, rhs, start=True, stop=True):
                return nc.tensor.matmul(out, lhsT, rhs, start=start, stop=stop, skip_group_check=True)

            def product(out, lh, ll, rh, rl, start, stop):
                mm(out, lh, rh, start, False)
                mm(out, lh, rl, False, False)
                return mm(out, ll, rh, False, stop)

            def transposes(name, src, before=lambda q: None):
                for q in range(4):
                    before(q)
                    wait_bank(pe, name, q)
                    b = use_bank(name, q)
                    for k in range(2):
                        for t in range(NT):
                            last = nc.tensor.transpose(b[:, k * T + t * P:k * T + t * P + P],
                                                       src[:, t, (2 * q + k) * P:(2 * q + k + 1) * P], ID[:, :])
                    last.then_inc(misc_ready, 1)

            def a_slab(a, channels, oh, ol, before=None):
                s = slabs[A_IDX[a]]
                if a >= 2:
                    if A_KIND[a - 2] != "dve":
                        pe.wait_ge(a_act, A_ACT[a - 2])
                    if A_KIND[a - 2] != "act":
                        pe.wait_ge(a_dve, A_DVE[a - 2])
                for pc in range(2):
                    q = s.first + pc
                    pe.wait_ge(lo_done, q + 1)
                    wh = WH[:, q % PIECES, :].rearrange("p (k c) -> p k c", k=4)
                    wl = WL[:, q % PIECES, :].rearrange("p (k c) -> p k c", k=4)
                    for kk in range(4):
                        k = 4 * pc + kk
                        if before:
                            before(k)
                        for m in range(2):
                            o = bank[a % 2][:, T * m:T * m + T]
                            cut = slice(P * m, P * m + P)
                            first = k == 0 and m == 0
                            if channels:
                                last = product(o, wh[:, kk, cut], wl[:, kk, cut], oh[:, k, :], ol[:, k, :],
                                               first, k == KT - 1)
                            else:
                                last = product(o, oh[:, k, cut], ol[:, k, cut], wh[:, kk, :], wl[:, kk, :],
                                               first, k == KT - 1)
                    last.then_inc(piece_used, 1)

            def columns_split(name):
                def before(k):
                    if k % 2 == 0:
                        wait_emptied(pe, name, k // 2)
                return before

            pe.wait_ge(ident_ready, 1)
            pe.wait_ge(small_in, 3 * 16)
            nc.tensor.transpose(use_bank("cols", 0)[:, 0:62], ROWS[0:62, :], ID[0:62, 0:62]).then_inc(misc_ready, 1)
            pe.wait_ge(mem_in, 16)
            transposes("tr0", GB)
            for a in range(4):
                a_slab(a, a % 2 == 0, MTH, MTL, columns_split("tr0") if a == 0 else None)

            pe.wait_ge(x_in, 16)
            transposes("tr1", X)

            def lora(i):
                cut = slice(P * i, P * i + P)
                wait_bank(pe, "up", i)
                b = use_bank("up", i)
                mm(b[:, 0:T], WUP[0:HD, cut], WD[0:HD, :]).then_inc(misc_ready, 1)
                wait_bank(pe, "gate", i)
                mm(use_bank("gate", i)[:, T:2 * T], WUP[HD:P, cut], WD[HD:P, :])
                mm(use_bank("gate", i)[:, 0:T], GUP[:, cut], GD[:, :]).then_inc(misc_ready, 1)

            def norm(i):
                pe.wait_ge(square_ready, i + 1)
                if i == 0:
                    wait_bank(pe, "norm", 0)
                    pe.wait_ge(heads_ready, 1)
                mm(use_bank("norm", 0)[0:HEADS, 0:T], IND[:, i, :], SQ[:, i % 2, :], i == 0, i == TILES - 1)\
                    .then_inc(square_used if i + 1 < TILES else misc_ready, 1)

            def spread(j):
                pe.wait_ge(rnorm_ready, 1)
                wait_bank(pe, "spread", j)
                for m in range(2):
                    last = mm(use_bank("spread", j)[:, T * m:T * m + T], SPR[:, 2 * j + m, :], RN[:, :], m == 0, True)
                last.then_inc(misc_ready, 1)

            def values(i):
                wait_bank(pe, "vt", i)
                b = use_bank("vt", i)
                for c in range(NT):
                    last = nc.tensor.transpose(b[:, P * c:P * c + P], V[:, i, P * c:P * c + P], ID[:, :])
                last.then_inc(misc_ready, 1)

            def bonus(i):
                pe.wait_ge(rk_ready, i + 1)
                pe.wait_ge(consts_ready, 1)
                wait_bank(pe, "bonus", i)
                mm(use_bank("bonus", i)[:, 0:T], BO[:, :], RK[:, i % 2, :]).then_inc(misc_ready, 1)

            def mem_step(l, q, n):
                if n < MEMH:
                    i, hb = n // 2, HD * (n % 2)
                    wait_bank(pe, f"s{l}", n)
                    b = use_bank(f"s{l}", n)
                    for t in range(NT):
                        last = mm(b[:, T * t:T * t + T], q[hb:hb + HD, i, P * t:P * t + P], MK[hb:hb + HD, l, i, :])
                    last.then_inc(misc_ready, 1)
                if 1 <= n <= MEMH:
                    h = n - 1
                    pe.wait_ge(probs_ready, MEMH * l + h + 1)
                    wait_bank(pe, f"pt{l}", h)
                    b = use_bank(f"pt{l}", h)
                    for mt in range(2):
                        for t in range(NT):
                            last = nc.tensor.transpose(b[:, T * mt + P * t:T * mt + P * t + P],
                                                       PR[:, h % 2, t, P * mt:P * mt + P], ID[:, :])
                    last.then_inc(misc_ready, 1)
                if n >= 2:
                    h = n - 2
                    i, hb = h // 2, HD * (h % 2)
                    wait_emptied(pe, f"pt{l}", h)
                    if h % 2 == 0:
                        wait_bank(pe, f"mo{l}", i)
                    b = use_bank(f"mo{l}", i)
                    for mt in range(2):
                        last = mm(b[hb:hb + HD, 0:T], MVA[:, l, mt, HD * h:HD * h + HD], PT[:, h % 2, mt, :],
                                  mt == 0, mt == 1)
                    if h % 2:
                        last.then_inc(misc_ready, 1)

            for a in range(4, 16):
                if a < 15:
                    a_slab(a, True, TH, TL, columns_split("tr1") if a == 4 else None)
                if 5 <= a <= 7:
                    pe.wait_ge(lora_in_ready, 2)
                    pe.wait_ge(up_in, 3 * 16)
                    for i in (2 * a - 10, 2 * a - 9):
                        lora(i)
                if 7 <= a <= 9:
                    for i in (2 * a - 14, 2 * a - 13):
                        norm(i)
                if a >= MEM0:
                    if a == MEM0:
                        pe.wait_ge(a_act, A_ACT[5])
                    mem_step(0, QM, a - MEM0)
                if a == MEM0 + 1:
                    for j in range(TILES // 2):
                        spread(j)
                if a >= MEM0 + 3:
                    pair = (2 * (a - MEM0 - 3), 2 * (a - MEM0 - 3) + 1)
                    pe.wait_ge(a_dve, A_DVE[a - 1])
                    for i in pair:
                        values(i)
                    for i in pair:
                        bonus(i)
            for i in range(TILES):
                pe.wait_ge(bk_scaled, i + 1)
                wait_bank(pe, "bk", i)
                b = use_bank("bk", i)
                nc.tensor.transpose(b[:, 0:P], BT[:, i, 0:P], ID[:, :])
                nc.tensor.transpose(b[:, P:2 * P], KK[:, i, 0:P], ID[:, :]).then_inc(misc_ready, 1)

            wait_emptied(pe, "bk", TILES - 1)
            wait_emptied(pe, "bonus", TILES - 1)
            pe.wait_ge(a_act, A_ACT[14])
            for g in range(NG):
                for step in range(1, MM_N + 1):
                    for l in range(4):
                        h, c = job(g, l)
                        L = lanes[l]
                        i, hb = h // 2, HD * (h % 2)
                        rows = slice(hb, hb + HD)
                        PX = L["PX"]
                        b, other = bank[2 * l + step % 2], bank[2 * l + 1 - step % 2]

                        def act_at(n):
                            pe.wait_ge(lane_act[l], ACT_N * g + n)

                        def dve_at(n):
                            pe.wait_ge(lane_dve[l], DVE_N * g + n)

                        def pool_at(n):
                            pe.wait_ge(lane_pool[l], POOL_N * g + n)

                        if step == 1:
                            if g:
                                act_at(0)
                                dve_at(0)
                            ar = AR[rows, i, c, :, :].rearrange("p a c -> p (a c)")
                            tok = slice(P * c, P * c + P)
                            mm(bank[2 * l][:, 0:P], AR[rows, i, c, 0, :], BT[rows, i, tok])
                            mm(bank[2 * l + 1][:, 0:T], BT[rows, i, tok], ar)
                            last = mm(bank[2 * l + 1][:, T:2 * T], KK[rows, i, tok], ar)
                        elif step == 2:
                            dve_at(3)
                            mm(b[:, 0:P], PX[:, 1, :], PX[:, 0, :])
                            last = mm(b[:, P:2 * P], PX[:, 0, :], PX[:, 1, :])
                        elif step in (3, 4):
                            act_at(step - 2)
                            if step == 3:
                                pool_at(1)
                            dve_at(step + 2)
                            mm(b[:, 0:P], PX[:, 1, :], PX[:, 0, :])
                            if step == 3:
                                mm(b[:, P:2 * P], PX[:, 0, :], PX[:, 1, :])
                            last = mm(other[:, 0:P], PX[:, 0, :], PX[:, 2, :])
                        elif step == 5:
                            act_at(3)
                            dve_at(7)
                            mm(b[:, 0:P], PX[:, 0, :], PX[:, 2, :])
                            if c:
                                pe.wait_ge(state_ready, h + 1)
                            last = mm(other[:, 0:HD], L["KR"][:, 0, :], VT[:, c, HD * h:HD * h + HD], True, c == 0)
                            if c:
                                last = mm(other[:, 0:HD], AR[rows, i, c, 0, :], S0[rows, i, :], False, True)
                        elif step == 6:
                            dve_at(8)
                            act_at(4)
                            last = nc.tensor.transpose(b[:, 0:P], PX[:, 2, :], ID[:, :])
                        elif step in (7, 9, 11):
                            lev = (step - 7) // 2
                            if step == 7:
                                pool_at(2)
                            else:
                                dve_at(8 + lev)
                            last = mm(b[:, 0:P], L["LT"][:, lev, :], PX[:, 2, :])
                        elif step in (8, 10, 12):
                            lev = (step - 8) // 2
                            act_at(6 + lev)
                            last = mm(b[:, 0:P], PX[:, 3, :], PX[:, 0, :])
                            if step < 12:
                                last = mm(b[:, P:2 * P], PX[:, 0, :], PX[:, 3, :])
                        elif step == 13:
                            dve_at(11)
                            last = mm(b[:, 0:HD], PX[:, 2, :], L["Q1"][:, :])
                        else:
                            act_at(9)
                            vt = VT[:, c, HD * h:HD * h + HD]
                            mm(b[:, 0:HD], L["MR"][:, 1, :], L["SA"][:, :], True, False)
                            last = mm(b[:, 0:HD], L["KR"][:, 1, :], vt, False, c == 0)
                            if c:
                                last = mm(b[:, 0:HD], AR[rows, i, c, 1, :], S0[rows, i, :], False, True)
                            else:
                                mm(b[rows, HD:2 * HD], BKT[:, i, 0, rows], L["SA"][:, :], True, False)
                                last = mm(b[rows, HD:2 * HD], BKT[:, i, 1, rows], vt, False, True)
                        last.then_inc(lane_mm[l], 1)
            for l in range(4):
                pe.wait_ge(lane_act[l], ACT_N * NG)

            for i in range(TILES):
                pe.wait_ge(y_ready, NT * 3 - 2 + i // 2)
                wait_bank(pe, "yt", i)
                b = use_bank("yt", i)
                for c in range(NT):
                    last = nc.tensor.transpose(b[:, P * c:P * c + P], Y[:, c, P * i:P * i + P], ID[:, :])
                last.then_inc(misc_ready, 1)
            def cat_made(k):
                if k < TILES:
                    pe.wait_ge(cat_ready, k + 1)
                elif k == TILES:
                    pe.wait_ge(mem_out_lo, 1)

            for a in range(15, 19):
                a_slab(a, False, TH, TL, cat_made if a == 15 else None)

            def normed(idx, name, after=None):
                def parts_made(q):
                    if q == 0:
                        pe.wait_ge(x_parts, len(PARTS) * idx + 2)
                    elif q == 2:
                        rows_done(pe, idx)

                transposes(name, X, parts_made)
                if after:
                    for q in range(4):
                        wait_emptied(pe, name, q)
                        after(q)

            normed(0, "tr2")

            pe.wait_ge(a_dve, A_DVE[18])
            first_columns = columns_split("tr2")
            for f in range(FT + 1):
                if f < FT:
                    s = slabs[B0 + f]
                    if f >= 2:
                        pe.wait_ge(h_ready, f - 1)
                for pc in range(2):
                    if f < FT:
                        q = s.first + pc
                        pe.wait_ge(lo_done, q + 1)
                        wh = WH[:, q % PIECES, :].rearrange("p (k c) -> p k c", k=4)
                        wl = WL[:, q % PIECES, :].rearrange("p (k c) -> p k c", k=4)
                        for kk in range(4):
                            k = 4 * pc + kk
                            if f == 0:
                                first_columns(k)
                            for t in range(NT):
                                cut = slice(P * t, P * t + P)
                                last = product(bank[f % 2][:, T * t:T * t + T], TH[:, k, cut], TL[:, k, cut],
                                               wh[:, kk, :], wl[:, kk, :], k == 0 and t == 0, k == KT - 1)
                        last.then_inc(piece_used, 1)
                    if pc == 0 and f:
                        pe.wait_ge(h_ready, f)
                        if f >= 3:
                            pe.wait_ge(ht_lo, f - 2)
                        b = bank[6 + (f - 1) % 2]
                        for t in range(NT):
                            last = nc.tensor.transpose(b[:, P * t:P * t + P], FH[:, t, :], ID[:, :])
                        last.then_inc(ht_ready, 1)
                if f:
                    pe.wait_ge(ht_lo, f)
                    q = slabs[B0 + f - 1].down
                    pe.wait_ge(lo_done, q + 1)
                    for t in range(NT):
                        cut = slice(P * t, P * t + P)
                        for half in range(2):
                            n = slice(512 * half, 512 * half + 512)
                            last = product(bank[2 + 2 * t + half][:, :], FHH[:, (f - 1) % 2, cut], FHL[:, (f - 1) % 2, cut],
                                           WH[:, q % PIECES, n], WL[:, q % PIECES, n], f == 1, f == FT)
                        if f == FT and t == 0:
                            last.then_inc(ffn_tile0, 1)
                    last.then_inc(piece_used, 1)

            pe.wait_ge(ffn_out, 4)
            normed(1, "tr3")
            for a in range(19, 29):
                a_slab(a, a not in (23, 24, 25), TH, TL, columns_split("tr3") if a == 19 else None)
                if a == MEM1:
                    pe.wait_ge(a_act, A_ACT[19])
                if 0 <= a - MEM1 < MEMH + 2:
                    mem_step(1, QM1, a - MEM1)
            pe.wait_ge(a_act, A_ACT[28])

            for s in range(HEADS + 3):
                if s < HEADS:
                    h = s
                    i, rows = h // 2, slice(HD * (h % 2), HD * (h % 2) + HD)
                    wait_bank(pe, "z", h)
                    b = use_bank("z", h)
                    mm(b[:, 0:T], KC[rows, i, 0:P], QC[rows, i, :], True, False)
                    mm(b[:, T:T + P], KC[rows, i, P:T], QC[rows, i, P:T], False, False).then_inc(misc_ready, 1)
                if 2 <= s < HEADS + 2:
                    h = s - 2
                    b = use_bank("z", h)
                    pe.wait_ge(stick_masked, h + 1)
                    sp_ = SP[:, h % 3, :, :].rearrange("p a c -> p (a c)")
                    mm(b[:, 0:T], NTRI[:, :], sp_[:, 0:T], False, False)
                    mm(b[:, P:T], NONE[:, :], sp_[:, T:T + P], False, False)
                    mm(b[:, T:T + P], NTRI[:, :], sp_[:, T:T + P], False, True).then_inc(cs_ready, 1)
                if s >= 3:
                    h = s - 3
                    i, rows = h // 2, slice(HD * (h % 2), HD * (h % 2) + HD)
                    if h % 2 == 0:
                        wait_bank(pe, "so", i)
                    b = use_bank("so", i)
                    pe.wait_ge(stick_w, h + 1)
                    wt = WT[:, h % 2, :, :].rearrange("p a c -> p (a c)")
                    mm(b[rows, 0:T], VK[:, 0, HD * h:HD * h + HD], wt[:, 0:T], True, False)
                    last = mm(b[rows, P:T], VK[:, 1, HD * h:HD * h + HD], wt[:, T:T + P], False, True)
                    if h % 2:
                        last.then_inc(misc_ready, 1)
            wait_emptied(pe, "so", TILES - 1)
            pe.wait_ge(mem_out_lo, 2)
            for a in range(29, 33):
                a_slab(a, False, TH, TL)
            pe.wait_ge(a_dve, A_DVE[32])

            def logits(q):
                if q == 0:
                    pe.wait_ge(router_split, 1)
                for k in (2 * q, 2 * q + 1):
                    last = product(bank[0][0:EXPERTS, 0:T], RHI[:, k, :], RLO[:, k, :], TH[:, k, :], TL[:, k, :],
                                   k == 0, k == KT - 1)
                if q == 3:
                    last.then_inc(logits_t_ready, 1)

            normed(2, "tr4", logits)
            pe.wait_ge(logits_t_copied, 1)
            for t in range(NT):
                last = nc.tensor.transpose(bank[1][:, EXPERTS * t:EXPERTS * t + EXPERTS], LGT[:, P * t:P * t + P],
                                           ID[0:EXPERTS, 0:EXPERTS])
            last.then_inc(logits_ready, 1)

            pe.wait_ge(top_ready, 1)
            mm(bank[0][:, 0:16], SI[:, 0, :], SEL[:, :, :].rearrange("p t e -> p (t e)"), True, False)
            mm(bank[0][:, 8:16], ONE[:, :], SEL[:, 0, :], False, True)
            mm(bank[0][:, 16:24], ONE[:, :], SEL[:, 0, :], False, False)
            mm(bank[0][:, 16:24], ONE[:, :], SEL[:, 1, :], False, True).then_inc(rank_ready, 1)

            def gather(p, uses):
                for r in uses:
                    if p is NONE_BEFORE and r == 6:
                        pe.wait_ge(x2_split, 1)
                    src = XH if r < 6 else XL
                    if r >= 6 or p is not NONE_BEFORE:
                        pe.wait_ge(*ring_count(p, r - 2))
                    b = ring_bank(r)
                    for d in range(4):
                        for t in range(NT):
                            at = D * t + P * (4 * (r % 2) + d)
                            last = mm(b[:, P * d:P * d + P], src[:, at:at + P], DI[:, t, :], d == 0 and t == 0, t == NT - 1)
                    last.then_inc(ring2_ready, 1)

            def gather_slots(p):
                pe.wait_ge(*ring_count(p, 6))
                for t in range(NT):
                    last = nc.tensor.transpose(ring_bank(8)[:, P * t:P * t + P], DI[:, t, :].bitcast(F32), ID[:, :])
                last.then_inc(ring2_ready, 1)
                pe.wait_ge(*ring_count(p, 7))
                for t in range(NT):
                    last = mm(ring_bank(9)[:, 0:1], DI[:, t, :].bitcast(F32), CPC[:, t:t + 1], t == 0, t == NT - 1)
                last.then_inc(ring2_ready, 1)

            def scatter(p, uses):
                pe.wait_ge(out_lo_s, 2 * p + 2)
                for r in uses:
                    t, half = r // 2, r % 2
                    if r < 2:
                        pe.wait_ge(*ring_count(p - 1, 8 + r))
                    else:
                        pe.wait_ge(*ring_count(p, r - 2))
                    mm(ring_bank(r)[:, :], DTC[:, t, :], OH[:, half, :], True, False)
                    mm(ring_bank(r)[:, :], DTC[:, t, :], OL[:, half, :], False, True).then_inc(ring2_ready, 1)

            def expert(p):
                for j in range(FT + 2):
                    if j < FT:
                        pe.wait_ge(eh_ready, p * FT + (j - 1 + MOE_H0))
                        if j == 0:
                            pe.wait_ge(*ring_count(p - 1, 5))
                            pe.wait_ge(*ring_count(p - 1, 7))
                    for pc in range(2):
                        if j < FT:
                            r = GU_AT[j] + pc
                            pe.wait_ge(lo_done, p * PP + (NF + r + 1))
                            wh = WH[:, r % PIECES, :].rearrange("p (k c) -> p k c", k=4)
                            wl = WL[:, r % PIECES, :].rearrange("p (k c) -> p k c", k=4)
                            for kk in range(4):
                                k = 4 * pc + kk
                                last = product(bank[j % 2][:, 0:T], XGH[:, k, :], XGL[:, k, :], wh[:, kk, :], wl[:, kk, :],
                                               k == 0, k == KT - 1)
                            last.then_inc(piece_used, 1)
                        if pc == 0 and 1 <= j <= FT:
                            if j == FT:
                                pe.wait_ge(disp_ready, p * 3 + 6)
                                pe.wait_ge(cur_ready, p + 2)
                                gather(p, (4, 5))
                            pe.wait_ge(eh_ready, p * FT + (j + MOE_H0))
                            pe.wait_ge(eth_lo, p * FT + (j - 2 + MOE_H0))
                            nc.tensor.transpose(bank[4 + 3 * ((j - 1) % 2)][:, 0:P], EH[:, :], ID[:, :]).then_inc(et_ready, 1)
                    if j in (1, 2):
                        scatter(p, (0, 1) if j == 1 else (2, 3))
                    if j >= 2:
                        pe.wait_ge(eth_lo, p * FT + (j - 1 + MOE_H0))
                        r = DOWN_AT[j - 2]
                        pe.wait_ge(lo_done, p * PP + (NF + r + 1))
                        for half in range(2):
                            n = slice(512 * half, 512 * half + 512)
                            last = product(bank[2 + half][:, :], EHH[:, j % 2, :], EHL[:, j % 2, :],
                                           WH[:, r % PIECES, n], WL[:, r % PIECES, n], j == 2, j == FT + 1)
                        last.then_inc(piece_used, 1)
                    if j == FT:
                        gather(p, (6, 7))
                gather_slots(p)

            pe.wait_ge(x2_hi, 1)
            pe.wait_ge(disp_ready, 3)
            gather(NONE_BEFORE, (4, 5, 6, 7))
            gather_slots(NONE_BEFORE)
            with pe.Fori(0, EXPERTS) as p:
                expert(p)
            pe.wait_ge(route_ready, 1)
            n_extra = pe.value_load(NUI[0:1, 0:1], min_val=0, max_val=EXTRA)
            for j in range(EXTRA):
                with pe.If(n_extra > j):
                    expert(EXPERTS + j)
            scatter(n_extra + EXPERTS, (0, 1, 2, 3))

        @block.scalar
        def _(act):
            def copy(out, in_):
                return nc.scalar.activation(out, in_, ACT.Copy)

            chained = [0]

            def link(ins):
                chained[0] += 1
                ins.then_inc(act_chain, 1)
                act.wait_ge(act_chain, chained[0])

            split = [0]

            def split_to(q_end):
                for q in range(split[0], min(q_end, NF)):
                    n, pc = pieces[q]
                    s = slabs[n]
                    act.wait_ge(s.sem, s.count)
                    if q >= PIECES:
                        act.wait_ge(piece_used, q - PIECES + 1)
                    at = s.offset + PIECE * pc
                    copy(WH[:, q % PIECES, :], RAW[:, at:at + PIECE]).then_inc(hi_done, 1)
                split[0] = max(split[0], q_end)

            def a_filled(a):
                s = slabs[A_IDX[a]]
                split_to(s.first + PIECES)
                act.wait_ge(piece_used, s.first + 2)
                return bank[a % 2]

            def plain_hi(name, dst):
                for q in range(4):
                    wait_ready(act, name, q)
                    copy(dst[:, 2 * q:2 * q + 2, :].rearrange("p k t -> p (k t)"), use_bank(name, q)[:, :]).then_inc(tr_hi, 1)

            plain_hi("tr0", MTH)
            split_to(PIECES)
            for a in range(4):
                b = a_filled(a)
                dst = (MK if a % 2 == 0 else MVA)[:, a // 2, :, :].rearrange("p a c -> p (a c)")
                copy(dst, b[:, :]).then_inc(a_act, 1)
            plain_hi("tr1", TH)
            act.wait_ge(cols_ready, 1)

            def lora(i):
                wait_ready(act, "up", i)
                b = use_bank("up", i)
                nc.scalar.activation(CS[:, i, :, 1:P + 1], b[:, 0:T].rearrange("p (c t) -> p c t", c=NT), ACT.Sigmoid,
                                     bias=col(VEC + i)).then_inc(misc_act, 1)
                wait_ready(act, "gate", i)
                nc.scalar.activation(BT[:, i, :], use_bank("gate", i)[:, T:2 * T], ACT.Sigmoid, bias=col(VEC + 6 + i))
                copy(G[:, i, :], use_bank("gate", i)[:, 0:T]).then_inc(misc_act, 1)

            def exps(i):
                if i >= 2:
                    act.wait_ge(exp_used, i - 1)
                    act.wait_ge(bk_scaled, i - 1)
                for c in range(NT):
                    nc.scalar.activation(EW[:, i % 2, c, :], CS[:, i, c, :], ACT.Exp, scale=-BETA, bias=BM[:, 0, i, c:c + 1])
                    nc.scalar.activation(EI[:, i % 2, c, :], CS[:, i, c, 1:P + 1], ACT.Exp, scale=BETA, bias=BM[:, 1, i, c:c + 1])
                nc.scalar.activation(WM[:, i:i + 1], BM[:, 0, i, 1:2], ACT.Exp, scale=-1.0).then_inc(exp_ready, 1)

            def values(i):
                wait_ready(act, "vt", i)
                copy(VT[:, :, P * i:P * i + P], use_bank("vt", i)[:, 0:T].rearrange("p (c t) -> p c t", c=NT)).then_inc(misc_act, 1)

            def mem_step(l, n, out):
                if n < MEMH:
                    act.wait_ge(smax_ready, MEMH * l + n + 1)
                    if n >= 2:
                        wait_ready(act, f"pt{l}", n - 2)
                    b = use_bank(f"s{l}", n)
                    for t in range(NT):
                        last = nc.scalar.activation(PR[:, n % 2, t, :], b[:, T * t:T * t + T], ACT.Exp,
                                                    bias=SMX[:, n, t:t + 1], accum_out=SSM[:, n, t:t + 1])
                    last.then_inc(misc_act, 1)
                if n >= 3 and n % 2 == 1:
                    i = (n - 3) // 2
                    wait_ready(act, f"mo{l}", i)
                    copy(out[:, i, :], use_bank(f"mo{l}", i)[:, 0:T]).then_inc(misc_act, 1)

            for a in range(4, 15):
                b = a_filled(a)
                w = W_ORDER[a - 4]
                if w == 10:
                    last = nc.scalar.activation(QM[:, :, :].rearrange("p a c -> p (a c)"), b[:, :], ACT.Copy, scale=SCALE)
                else:
                    for m in range(2):
                        tile = 2 * w + m
                        src = b[:, T * m:T * m + T]
                        if tile < 6:
                            dst = AR[:, tile, :, 1, :]
                            src = src.rearrange("p (c t) -> p c t", c=NT)
                        else:
                            dst = [KK, V][tile // 6 - 1][:, tile % 6, :] if tile < 18 else [WD, GD][tile - 18][:, :]
                        last = nc.scalar.activation(dst, src, ACT.Identity, scale=OMMU[:, tile:tile + 1])
                last.then_inc(a_act, 1)
                if a == 4:
                    act.wait_ge(a_dve, 1)
                    nc.scalar.activation(WD[0:HD, :], WD[0:HD, :], ACT.Tanh).then_inc(lora_in_ready, 1)
                    nc.scalar.activation(GD[:, :], GD[:, :], ACT.Sigmoid).then_inc(lora_in_ready, 1)
                if 5 <= a <= 7:
                    for i in (2 * a - 10, 2 * a - 9):
                        lora(i)
                if a == MEM0:
                    wait_emptied(act, "norm", 0)
                    nc.scalar.activation(RN[:, :], RN[:, :], ACT.Sqrt).then_inc(norm_sqrt, 1)
                if a >= MEM0:
                    mem_step(0, a - MEM0, QM)
                if a == MEM0 + 1:
                    act.wait_ge(decay_ready, 1)
                    exps(0)
                    exps(1)
                if a >= MEM0 + 3:
                    pair = (2 * (a - MEM0 - 3), 2 * (a - MEM0 - 3) + 1)
                    for i in pair:
                        values(i)
                    for i in pair:
                        exps(i + 2)
            mem_step(0, MEMH + 1, QM)
            values(TILES - 2)
            values(TILES - 1)
            for i in range(TILES):
                wait_ready(act, "bk", i)
                copy(BKT[:, i, :, :].rearrange("p a c -> p (a c)"), use_bank("bk", i)[:, 0:T]).then_inc(misc_act, 1)
            split_to(slabs[A_IDX[15]].first + PIECES)

            LANE_COPY = {2: 1, 3: 2, 4: 3, 5: 4, 6: 5, 7: 6, 9: 7, 11: 8, 13: 9, 14: 10}
            def squares(g):
                act.wait_ge(y_var, 2 * g + 1)
                nc.scalar.activation(YSQ[:, :], y_of(g), ACT.Square).then_inc(y_sqrt, 1)

            def deviations(g):
                act.wait_ge(y_var, 2 * g + 2)
                nc.scalar.activation(GNS[:, 2, 4 * g:4 * g + 4], GNS[:, 1, 4 * g:4 * g + 4], ACT.Sqrt, scale=1.0 / HD,
                                     bias=EPS[:, 0:1]).then_inc(y_sqrt, 1)

            for g in range(NG):
                for step in LANE_COPY:
                    if g and step == 4:
                        squares(g - 1)
                    if g and step == 7:
                        deviations(g - 1)
                    for l in range(4):
                        h, c = job(g, l)
                        L = lanes[l]
                        i, hb = h // 2, HD * (h % 2)
                        rows = slice(hb, hb + HD)
                        PX = L["PX"]
                        b = bank[2 * l + step % 2]
                        act.wait_ge(lane_mm[l], MM_N * g + step)
                        if step == 2:
                            act.wait_ge(lane_pool[l], POOL_N * g + 1)
                        if step <= 3:
                            last = copy(PX[:, 0:2, :].rearrange("p a c -> p (a c)"), b[:, 0:T])
                        elif step == 4:
                            last = copy(PX[:, 0, :], b[:, 0:P])
                        elif step == 5:
                            last = copy(L["Q1"][:, :], bank[2 * l][:, 0:HD])
                        elif step == 6:
                            last = copy(PX[:, 3, :], b[:, 0:P])
                        elif step <= 11:
                            last = copy(PX[:, 0, :], b[:, 0:P])
                        elif step == 13:
                            last = copy(L["SA"][:, :], b[:, 0:HD])
                        else:
                            if c == 0:
                                nc.scalar.activation(S0[rows, i, :], b[rows, HD:2 * HD], ACT.Identity,
                                                     scale=SC[rows, i:i + 1]).then_inc(state_ready, 1)
                            last = copy(Y[:, c, HD * h:HD * h + HD], b[:, 0:HD])
                        last.then_inc(lane_act[l], 1)

            squares(NG - 1)
            deviations(NG - 1)
            copy(TH[:, TILES:KT, :], QM[:, :, :]).then_inc(mem_out_hi, 1)
            for i in range(TILES + 2):
                if i < TILES:
                    wait_ready(act, "yt", i)
                    nc.scalar.activation(YT[:, i, :], use_bank("yt", i)[:, 0:T], ACT.Identity,
                                         scale=col(VEC + 24 + i), bias=col(VEC + 30 + i)).then_inc(misc_act, 1)
                if i >= 2:
                    act.wait_ge(yt_gated, i - 1)
                    copy(TH[:, i - 2, :], YT[:, i - 2, :]).then_inc(cat_hi, 1)

            def normed(idx, name):
                act.wait_ge(rstd_ready, idx + 1)
                part = X[:, 1, HALF:D]
                nc.scalar.activation(part, part, ACT.Identity, scale=RS[:, 1:2], bias=NM[:, 1:2]).then_inc(xn_act, 1)
                if name:
                    plain_hi(name, TH)

            split_to(slabs[A_IDX[18]].first + PIECES)
            normed(0, "tr2")

            for f in range(FT + 1):
                if f < FT:
                    split_to(slabs[B0 + f].first + PIECES)
                if f:
                    act.wait_ge(ht_ready, f)
                    if f >= 3:
                        act.wait_ge(piece_used, slabs[B0 + f - 3].down + 1)
                    copy(FHH[:, (f - 1) % 2, :], bank[6 + (f - 1) % 2][:, 0:T]).then_inc(ht_hi, 1)
                if f < FT:
                    act.wait_ge(piece_used, slabs[B0 + f].first + 2)
                    if f:
                        act.wait_ge(h_ready, f)
                    nc.scalar.activation(FS[:, :, :], silu_view(bank[f % 2])[:, :, 0, :], ACT.Silu).then_inc(silu_ready, 1)
            split_to(slabs[A_IDX[19]].first + PIECES)
            normed(1, "tr3")
            for a in range(19, 29):
                b = a_filled(a)
                c = (a - 20) % 3
                if a == 19:
                    dst = QM1[:, :, :].rearrange("p a c -> p (a c)")
                elif 23 <= a < 26:
                    dst = VK[:, :, T * c:T * c + T]
                else:
                    dst = (KC if a < 23 else QC)[:, 2 * c:2 * c + 2, :].rearrange("p a c -> p (a c)")
                src = b[:, :].rearrange("p (t c) -> p t c", t=NT) if 23 <= a < 26 else b[:, :]
                nc.scalar.activation(dst, src, ACT.Copy, scale=SCALE if a == 19 or a >= 26 else 1.0).then_inc(a_act, 1)
                if a == MEM1:
                    rows_done(act, 1)
                    nc.scalar.preload_act_table_set("natural_log_exp_and_others")
                if 0 <= a - MEM1 < MEMH + 2:
                    mem_step(1, a - MEM1, MO)
            wait_emptied(act, "mo1", 1)
            copy(TH[:, TILES:KT, :], MO[:, :, :]).then_inc(mem_out_hi, 1)

            for s in range(HEADS + 4):
                if s == 2:
                    split_to(slabs[A_IDX[29]].first + PIECES)
                if s < HEADS:
                    wait_ready(act, "z", s)
                    e = SPA[:, s % 2, :, :].rearrange("p a c -> p (a c)")
                    if s >= 2:
                        act.wait_ge(stick_sp, s - 1)
                    nc.scalar.activation(e, use_bank("z", s)[:, 0:3 * P], ACT.Abs).then_inc(stick_abs, 1)
                if 2 <= s < HEADS + 2:
                    h = s - 2
                    act.wait_ge(cs_ready, h + 1)
                    nc.scalar.activation(WT[:, h % 2, :, :].rearrange("p a c -> p (a c)"), use_bank("z", h)[:, 0:3 * P],
                                         ACT.Exp).then_inc(misc_act, 1)
                if s >= 5 and s % 2 == 1:
                    i = (s - 5) // 2
                    wait_ready(act, "so", i)
                    copy(TH[:, i, :], use_bank("so", i)[:, 0:T]).then_inc(attn_hi, 1)
                if s < HEADS:
                    act.wait_ge(stick_abs, s + 1)
                    link(nc.scalar.activation(e, e, ACT.Exp, scale=-1.0))
                    nc.scalar.activation(e, e, ACT.Ln, bias=1.0).then_inc(stick_ln, 1)
            for a in range(29, 33):
                split_to(slabs[A_IDX[a]].first + PIECES)
            act.wait_ge(router_in, 16)
            copy(RHI[:, :, :], RTH[:, :, :]).then_inc(router_hi, 1)
            normed(2, "tr4")

            act.wait_ge(logits_t_ready, 1)
            rows_done(act, 2)
            copy(XH, X[:, :, :].rearrange("p t d -> p (t d)")).then_inc(x2_hi, 1)
            act.wait_ge(top_diff, 1)
            for t in range(NT):
                last = nc.scalar.activation(W12[:, t, 0:1], W12[:, t, 3:4], ACT.Exp)
            last.then_inc(top_exp, 1)

            def gathered(p):
                for r in (4, 5):
                    act.wait_ge(ring2_ready, ring_ready(p, r))
                    half = r % 2
                    copy(XGH[:, 4 * half:4 * half + 4, :].rearrange("p a c -> p (a c)"), ring_bank(r)[:, :]).then_inc(ring_act, 1)

            def gathered_slots(p):
                act.wait_ge(ring2_ready, ring_ready(p, 8))
                copy(DTN[:, :, :].rearrange("p a c -> p (a c)"), ring_bank(8)[:, 0:T]).then_inc(ring_act, 1)
                act.wait_ge(ring2_ready, ring_ready(p, 9))
                copy(CWN[:, :], ring_bank(9)[:, 0:1]).then_inc(ring_act, 1)

            def out_hi(p):
                for half in range(2):
                    nc.scalar.activation(OH[:, half, :], bank[2 + half][:, :], ACT.Copy, scale=CWC[:, 0:1]).then_inc(out_hi_s, 1)

            def hi_parts(p, first, end):
                for r in range(first, end):
                    m, pc = pass_pieces[r]
                    s = MOE_SLOT[m]
                    times = sum(MOE_SLOT[x] == s for x in range(m + 1))
                    if pc == 0:
                        act.wait_ge(raw_in[s], p * (32 * PER_PASS[s]) + (MOE_BASE[s] + 32 * times))
                    elif pc == 2:
                        act.wait_ge(down_in[s], p * (16 * PER_PASS[s]) + 16 * times)
                    act.wait_ge(piece_used, p * PP + (NF + r - PIECES + 1))
                    at = SLOT * s + PIECE * pc
                    copy(WH[:, r % PIECES, :], RAW[:, at:at + PIECE]).then_inc(hi_done, 1)

            def expert(p, follow):
                done = AHEAD
                nc.scalar.preload_act_table(ACT.Silu)
                for j in range(FT + 1):
                    upto = min(GU_AT[min(j, FT - 1)] + PIECES, PP)
                    hi_parts(p, done, upto)
                    done = max(done, upto)
                    if j == FT - 1:
                        follow(lambda: hi_parts(p + 1, 0, 1))
                    if j == FT:
                        follow(lambda: hi_parts(p + 1, 1, 3))
                        gathered(p)
                    if j:
                        act.wait_ge(et_ready, p * FT + j)
                        copy(EHH[:, (j - 1) % 2, :], bank[4 + 3 * ((j - 1) % 2)][:, 0:P]).then_inc(eth_hi, 1)
                    if j < FT:
                        act.wait_ge(piece_used, p * PP + (NF + GU_AT[j] + 2))
                        act.wait_ge(eh_ready, p * FT + (j + MOE_H0))
                        nc.scalar.activation(ES[:, :], bank[j % 2][:, 0:P], ACT.Silu).then_inc(es_ready, 1)
                    if j == 0:
                        act.wait_ge(piece_used, p * PP + NF)
                        act.wait_ge(cur_ready, p + 1)
                        out_hi(p)
                follow(lambda: hi_parts(p + 1, 3, 5))
                gathered_slots(p)
                follow(lambda: hi_parts(p + 1, 5, AHEAD))

            hi_parts(0, 0, 3)
            gathered(NONE_BEFORE)
            gathered_slots(NONE_BEFORE)
            hi_parts(0, 3, AHEAD)
            with act.Fori(0, EXPERTS - 1) as p:
                expert(p, always)
            act.wait_ge(route_ready, 1)
            n_extra = act.value_load(NUI[0:1, 0:1], min_val=0, max_val=EXTRA)
            last_passes(act, expert, n_extra)
            act.wait_ge(piece_used, (n_extra + EXPERTS) * PP + NF)
            act.wait_ge(cur_ready, n_extra + (EXPERTS + 1))
            out_hi(0)
            act.wait_ge(rstd_ready, 4)
            normed(3, None)

        @block.vector
        def _(dve):
            v = nc.vector
            chained = [0]

            def chain(ins):
                chained[0] += 1
                return ins.then_inc(dve_chain, 1)

            def settle():
                dve.wait_ge(dve_chain, chained[0])

            split = [0]

            def split_to(q_end):
                for q in range(split[0], min(q_end, NF)):
                    n, pc = pieces[q]
                    dve.wait_ge(hi_done, q + 1)
                    at = slabs[n].offset + PIECE * pc
                    v.tensor_tensor(WL[:, q % PIECES, :], RAW[:, at:at + PIECE], WH[:, q % PIECES, :].bitcast(F32),
                                    ALU.subtract).then_inc(lo_done, 1)
                split[0] = max(split[0], q_end)

            def low(out, full, hi):
                return v.tensor_tensor(out, full, hi.bitcast(F32), ALU.subtract)

            def plain_lo(name, hi, lo, base_count):
                for q in range(4):
                    dve.wait_ge(tr_hi, base_count + q + 1)
                    flat = lambda t: t[:, 2 * q:2 * q + 2, :].rearrange("p k t -> p (k t)")
                    low(flat(lo), use_bank(name, q)[:, :], flat(hi)).then_inc(misc_dve, 1)

            chain(v.memset(CS[:, :, :, 0:1], 0.0))
            wait_ready(dve, "cols", 0)
            v.tensor_copy(COLS[:, 0:62], use_bank("cols", 0)[:, 0:62]).then_inc(misc_dve, 1)
            dve.wait_ge(misc_dve, 1)
            v.tensor_scalar(OMMU[:, :], COLS[:, MU:MU + 20], -1.0, 1.0, ALU.mult, ALU.add)
            v.tensor_scalar(OMKA[:, :], COLS[:, VEC + 18:VEC + 24], -1.0, 1.0, ALU.mult, ALU.add).then_inc(cols_ready, 1)
            plain_lo("tr0", MTH, MTL, 0)
            for a in range(4):
                split_to(slabs[A_IDX[a]].first + PIECES)
            plain_lo("tr1", TH, TL, 4)

            def mixed(a, b):
                w = W_ORDER[a - 4]
                dve.wait_ge(a_act, A_ACT[a])
                for m in range(2):
                    tile = 2 * w + m
                    mu = col(MU + tile)
                    src = b[:, T * m:T * m + T]
                    if tile < 6:
                        dst = AR[:, tile, :, 1, :]
                        v.scalar_tensor_tensor(dst[:, 0, 1:P], src[:, 0:P - 1], mu, dst[:, 0, 1:P], ALU.mult, ALU.add)
                        last = v.scalar_tensor_tensor(dst[:, 1, :], src[:, P - 1:T - 1], mu, dst[:, 1, :], ALU.mult, ALU.add)
                    else:
                        dst = [KK, V][tile // 6 - 1][:, tile % 6, :] if tile < 18 else [WD, GD][tile - 18][:, :]
                        last = v.scalar_tensor_tensor(dst[:, 1:T], src[:, 0:T - 1], mu, dst[:, 1:T], ALU.mult, ALU.add)
                last.then_inc(a_dve, 1)

            def mem_step(l, n):
                if n < MEMH:
                    wait_ready(dve, f"s{l}", n)
                    b = use_bank(f"s{l}", n)
                    chain(v.tensor_reduce(SMX[:, n, :], b[:, :].rearrange("p (t m) -> p t m", t=NT), AX_X, ALU.max))
                    settle()
                    v.tensor_scalar(SMX[:, n, :], SMX[:, n, :], -1.0, None, ALU.mult).then_inc(smax_ready, 1)
                if 1 <= n <= MEMH:
                    h = n - 1
                    wait_ready(dve, f"pt{l}", h)
                    v.tensor_copy(PT[:, h % 2, :, :].rearrange("p a c -> p (a c)"), use_bank(f"pt{l}", h)[:, :]).then_inc(misc_dve, 1)
                if n < MEMH:
                    wait_emptied(dve, f"s{l}", n)
                    chain(v.reciprocal(SRI[:, n, :], SSM[:, n, :]))
                    settle()
                    for t in range(NT):
                        last = v.tensor_scalar(PR[:, n % 2, t, :], PR[:, n % 2, t, :], SRI[:, n, t:t + 1], None, ALU.mult)
                    last.then_inc(probs_ready, 1)

            def chunks(t):
                return t.rearrange("p (c t) -> p c t", c=NT)

            def products(i):
                dve.wait_ge(k_ready, i + 1)
                dve.wait_ge(exp_ready, i + 1)
                settle()
                if i >= 2:
                    wait_ready(dve, "bonus", i - 2)
                v.scalar_tensor_tensor(chunks(RK[:, i % 2, :]), AR[:, i, :, 1, :], col(RKC + i), chunks(KK[:, i, :]),
                                       ALU.mult, ALU.mult).then_inc(rk_ready, 1)
                chain(v.tensor_tensor(chunks(BT[:, i, :]), chunks(BT[:, i, :]), AR[:, i, :, 0, :], ALU.mult))
                chain(v.tensor_tensor(SC[:, i:i + 1], EW[:, i % 2, 0, P:P + 1], WM[:, i:i + 1], ALU.mult))
                settle()
                dve.wait_ge(rk_ready, i + 1)
                chain(v.tensor_tensor(AR[:, i, :, 1, :], AR[:, i, :, 1, :], EW[:, i % 2, :, 1:P + 1], ALU.mult))
                v.scalar_tensor_tensor(AR[:, i, :, 0, :], AR[:, i, :, 0, :], -1.0, EW[:, i % 2, :, 0:P], ALU.mult, ALU.mult)\
                    .then_inc(exp_used, 1)

            def bonus(i):
                wait_ready(dve, "bonus", i)
                wait_emptied(dve, "vt", i)
                v.tensor_tensor(V[:, i, :], V[:, i, :], use_bank("bonus", i)[:, 0:T], ALU.mult).then_inc(misc_dve, 1)

            for a in range(4, 15):
                split_to(slabs[A_IDX[a]].first + PIECES)
                if W_ORDER[a - 4] != 10:
                    mixed(a, bank[a % 2])
                if a == 8:
                    settle()
                    for i in range(TILES):
                        wait_emptied(dve, "up", i)
                        for c in range(NT):
                            s_ = CS[:, i, c, 1:P + 1]
                            chain(v.tensor_tensor_scan(s_, ONE[:, :], s_, 0.0, ALU.mult, ALU.add))
                    settle()
                    chain(v.tensor_scalar(BM[:, 0, :, :], CS[:, :, :, P // 2], BETA, None, ALU.mult))
                    v.tensor_scalar(BM[:, 1, :, :], CS[:, :, :, P // 2], -BETA, None, ALU.mult).then_inc(decay_ready, 1)
                if a == MEM0 - 1:
                    wait_ready(dve, "norm", 0)
                    v.tensor_scalar(RN[:, :], use_bank("norm", 0)[0:HEADS, 0:T], 1e-24, None, ALU.max).then_inc(misc_dve, 1)
                if a >= MEM0:
                    mem_step(0, a - MEM0)
                if a == MEM0:
                    dve.wait_ge(norm_sqrt, 1)
                    v.reciprocal(RN[:, :], RN[:, :]).then_inc(rnorm_ready, 1)
                if a == MEM0 + 1:
                    for i in range(TILES):
                        wait_ready(dve, "spread", i // 2)
                        ins = v.tensor_tensor(AR[:, i, :, 0, :], AR[:, i, :, 0, :],
                                              chunks(use_bank("spread", i // 2)[:, T * (i % 2):T * (i % 2) + T]), ALU.mult)
                        if i % 2:
                            ins.then_inc(misc_dve, 1)
                        else:
                            chain(ins)
                if a >= MEM0 + 2:
                    wait_emptied(dve, "spread", TILES // 2 - 1)
                    i = 2 * (a - MEM0 - 2)
                    if i:
                        bonus(i - 2)
                        bonus(i - 1)
                    products(i)
                    products(i + 1)
            bonus(TILES - 2)
            bonus(TILES - 1)
            split_to(slabs[A_IDX[15]].first + PIECES)

            def heads_of(t):
                return t.rearrange("p (h d) -> p h d", d=HD)

            def stat(n, g):
                return GNS[:, n, 4 * g:4 * g + 4]

            def spread(n, g):
                return stat(n, g).rearrange("p (h o) -> p h o", o=1).broadcast_to([P, 4, HD])

            def centred(g):
                for l in range(4):
                    dve.wait_ge(lane_act[l], ACT_N * (g + 1))
                chain(v.tensor_reduce(stat(0, g), heads_of(y_of(g)), AX_X, ALU.add))
                settle()
                chain(v.tensor_scalar(stat(0, g), stat(0, g), -1.0 / HD, None, ALU.mult))
                settle()
                v.tensor_tensor(heads_of(y_of(g)), heads_of(y_of(g)), spread(0, g), ALU.add).then_inc(y_var, 1)

            def variances(g):
                dve.wait_ge(y_sqrt, 2 * g + 1)
                v.tensor_reduce(stat(1, g), heads_of(YSQ[:, :]), AX_X, ALU.add).then_inc(y_var, 1)

            def over_deviation(g):
                dve.wait_ge(y_sqrt, 2 * g + 2)
                chain(v.reciprocal(stat(3, g), stat(2, g)))
                settle()
                v.tensor_tensor(heads_of(y_of(g)), heads_of(y_of(g)), spread(3, g), ALU.mult).then_inc(y_ready, 1)

            for g in range(NG):
                for step in (1, 3, 4, 5, 8, 10, 12):
                    if g and step == 3:
                        centred(g - 1)
                    if g and step == 5:
                        variances(g - 1)
                    if g and step == 10:
                        over_deviation(g - 1)
                    for l in range(4):
                        L = lanes[l]
                        PX = L["PX"]
                        b = bank[2 * l + step % 2]
                        dve.wait_ge(lane_mm[l], MM_N * g + step)
                        if step == 1:
                            if g:
                                dve.wait_ge(lane_pool[l], POOL_N * g)
                            si = SI[:, :, :].rearrange("p a c -> p (a c)")
                            flat = lambda t: t[:, :, :].rearrange("p a c -> p (a c)")
                            v.tensor_tensor(PX[:, 0, :], bank[2 * l][:, 0:P], BD[:, 0, :], ALU.mult).then_inc(lane_dve[l], 1)
                            v.tensor_tensor(L["AL"][:, :], bank[2 * l][:, 0:P], LS[:, :], ALU.mult).then_inc(lane_dve[l], 1)
                            v.tensor_tensor(PX[:, 1, :], bank[2 * l + 1][:, 0:P], BD[:, 1, :], ALU.mult).then_inc(lane_dve[l], 1)
                            v.tensor_tensor(flat(L["MR"]), bank[2 * l + 1][:, 0:T], si, ALU.mult).then_inc(lane_dve[l], 1)
                            v.tensor_tensor(flat(L["KR"]), bank[2 * l + 1][:, T:2 * T], si, ALU.mult).then_inc(lane_dve[l], 1)
                        elif step in (3, 4):
                            v.tensor_tensor(PX[:, 2, :], PX[:, 2, :], bank[2 * l + 1 - step % 2][:, 0:P], ALU.add).then_inc(lane_dve[l], 1)
                        elif step in (5, 12):
                            v.tensor_tensor(PX[:, 2, :], PX[:, 2, :], b[:, 0:P], ALU.add).then_inc(lane_dve[l], 1)
                        else:
                            xx = PX[:, 2:4, :].rearrange("p a c -> p (a c)")
                            v.tensor_tensor(xx, xx, b[:, 0:T], ALU.add).then_inc(lane_dve[l], 1)

            centred(NG - 1)
            variances(NG - 1)
            over_deviation(NG - 1)
            dve.wait_ge(y_ready, NG)
            dve.wait_ge(mem_out_hi, 1)
            low(TL[:, TILES:KT, :], QM[:, :, :], TH[:, TILES:KT, :]).then_inc(mem_out_lo, 1)
            for i in range(TILES + 2):
                if i < TILES:
                    dve.wait_ge(yt_bonus, i + 1)
                    v.tensor_tensor(YT[:, i, :], YT[:, i, :], G[:, i, :], ALU.mult).then_inc(yt_gated, 1)
                if i >= 2:
                    dve.wait_ge(cat_hi, i - 1)
                    low(TL[:, i - 2, :], YT[:, i - 2, :], TH[:, i - 2, :]).then_inc(cat_ready, 1)

            def residual(a):
                if a not in (18, 32):
                    split_to(slabs[A_IDX[a]].first + PIECES)
                dve.wait_ge(piece_used, slabs[A_IDX[a]].first + 2)
                cut = slice(T * ((a - 15) % 14), T * ((a - 15) % 14) + T)
                v.scalar_tensor_tensor(X[:, :, cut], X[:, :, cut], ALPHA, bank[a % 2][:, :].rearrange("p (t c) -> p t c", t=NT),
                                       ALU.mult, ALU.add).then_inc(a_dve, 1)
                dve.wait_ge(a_dve, A_DVE[a])
                for t in range(NT):
                    chain(v.bn_stats(BN[:, t, (a - 15) % 14, :], X[:, t, cut]))

            def half_stats(t, half):
                chain(v.bn_stats(BN[:, t, half, :], X[:, t, HALF * half:HALF * half + HALF]))

            def rows_normed(idx, chunks, parts=PARTS):
                settle()
                for t in range(NT):
                    v.bn_aggr(MV[:, t, :], BN[:, t, 0:chunks, :]).then_inc(stats_ready, 1)
                dve.wait_ge(stats_ready, NT * (idx + 1))
                dve.wait_ge(rows_in, 32 * (idx + 1))

                def part(t, half):
                    return X[:, t, HALF * half:HALF * half + HALF]

                for group in (parts[0:2], parts[2:3]):
                    for t, half in group:
                        chain(v.scalar_tensor_tensor(part(t, half), part(t, half), MV[:, t, 0:1],
                                                     GB[:, 0, HALF * half:HALF * half + HALF], ALU.subtract, ALU.mult))
                    settle()
                    dve.wait_ge(rstd_ready, idx + 1)
                    for t, half in group:
                        v.scalar_tensor_tensor(part(t, half), part(t, half), RS[:, t:t + 1],
                                               GB[:, 1, HALF * half:HALF * half + HALF], ALU.mult, ALU.add).then_inc(x_parts, 1)

            for a in range(15, 19):
                residual(a)
            rows_normed(0, 4)
            plain_lo("tr2", TH, TL, 8)

            for f in range(FT + 1):
                if f < FT:
                    split_to(slabs[B0 + f].first + PIECES)
                if f:
                    dve.wait_ge(ht_hi, f)
                    low(FHL[:, (f - 1) % 2, :], bank[6 + (f - 1) % 2][:, 0:T], FHH[:, (f - 1) % 2, :]).then_inc(ht_lo, 1)
                if f < FT:
                    dve.wait_ge(silu_ready, f + 1)
                    if f:
                        dve.wait_ge(ht_ready, f)
                    v.tensor_tensor(FH[:, :, :], FS[:, :, :], silu_view(bank[f % 2])[:, :, 1, :], ALU.mult).then_inc(h_ready, 1)
            split_to(slabs[A_IDX[19]].first + 2)
            rows_done(dve, 0)
            for t in range(NT):
                if t == 0:
                    dve.wait_ge(ffn_tile0, 1)
                else:
                    dve.wait_ge(piece_used, slabs[B0 + FT - 1].down + 1)
                for half in range(2):
                    n = slice(512 * half, 512 * half + 512)
                    v.scalar_tensor_tensor(X[:, t, n], X[:, t, n], ALPHA, bank[2 + 2 * t + half][:, :],
                                           ALU.mult, ALU.add).then_inc(ffn_out, 1)
                    if t or half:
                        dve.wait_ge(ffn_out, 2 * t + half)
                        half_stats((2 * t + half - 1) // 2, (half + 1) % 2)
            dve.wait_ge(ffn_out, 4)
            half_stats(1, 1)
            rows_normed(1, 2)
            plain_lo("tr3", TH, TL, 12)
            for a in range(19, 29):
                split_to(slabs[A_IDX[a]].first + PIECES)
                if a == MEM1:
                    rows_done(dve, 1)
                if 0 <= a - MEM1 < MEMH + 2:
                    mem_step(1, a - MEM1)
            dve.wait_ge(mem_out_hi, 2)
            low(TL[:, TILES:KT, :], MO[:, :, :], TH[:, TILES:KT, :]).then_inc(mem_out_lo, 1)

            flat3 = lambda t: t.rearrange("p a c -> p (a c)")
            for s in range(HEADS + 5):
                if s == 4:
                    split_to(slabs[A_IDX[29]].first + PIECES)
                if 1 <= s <= HEADS:
                    h = s - 1
                    dve.wait_ge(stick_ln, h + 1)
                    if h >= 3:
                        dve.wait_ge(cs_ready, h - 2)
                    v.scalar_tensor_tensor(flat3(SP[:, h % 3, :, :]), use_bank("z", h)[:, 0:3 * P], 0.0,
                                           flat3(SPA[:, h % 2, :, :]), ALU.max, ALU.add).then_inc(stick_sp, 1)
                if s >= 6 and s % 2 == 0:
                    i = (s - 6) // 2
                    dve.wait_ge(attn_hi, i + 1)
                    low(TL[:, i, :], use_bank("so", i)[:, 0:T], TH[:, i, :]).then_inc(misc_dve, 1)
            for a in range(29, 33):
                residual(a)
            rows_normed(2, 4)
            dve.wait_ge(router_hi, 1)
            low(RLO[:, :, :], RTH[:, :, :], RHI[:, :, :]).then_inc(router_split, 1)
            plain_lo("tr4", TH, TL, 16)
            for n in range(MOE_H0):
                v.memset(EH[:, HD * n:HD * n + HD], 0.0).then_inc(eh_ready, 1)
                v.memset(EHL[:, n, :].bitcast(F32), 0.0).then_inc(eth_lo, 1)

            dve.wait_ge(logits_t_ready, 1)
            v.tensor_copy(LGT[:, :], bank[0][0:EXPERTS, 0:T]).then_inc(logits_t_copied, 1)
            dve.wait_ge(logits_ready, 1)
            chain(v.tensor_copy(LG[:, :, :].rearrange("p t e -> p (t e)"), bank[1][:, 0:16]))
            settle()
            for t in range(NT):
                chain(v.max(MX8[:, t, :], LG[:, t, :]))
            settle()
            for t in range(NT):
                chain(v.max_index(IX8[:, t, :], MX8[:, t, :], LG[:, t, :]))
                last = chain(v.tensor_tensor(W12[:, t, 3:4], MX8[:, t, 1:2], MX8[:, t, 0:1], ALU.subtract))
            settle()
            v.tensor_copy(IXF[:, :, :], IX8[:, :, :]).then_inc(top_diff, 1)
            dve.wait_ge(top_diff, 1)
            for t in range(NT):
                chain(v.tensor_scalar(OH1[:, t, :], ROW8, IXF[:, t, 0:1], None, ALU.is_equal))
                chain(v.tensor_scalar(OH2[:, t, :], ROW8, IXF[:, t, 1:2], None, ALU.is_equal))
            settle()
            v.tensor_tensor(SEL[:, :, :], OH1[:, :, :], OH2[:, :, :], ALU.add).then_inc(top_ready, 1)
            dve.wait_ge(top_exp, 1)
            chain(v.tensor_scalar(W12[:, :, 1:2], W12[:, :, 0:1], 1.0, None, ALU.add))
            settle()
            chain(v.reciprocal(W12[:, :, 1:2], W12[:, :, 1:2]))
            settle()
            chain(v.tensor_tensor(W12[:, :, 2:3], W12[:, :, 1:2], W12[:, :, 0:1], ALU.mult))
            settle()
            for t in range(NT):
                chain(v.tensor_scalar(OH1[:, t, :], OH1[:, t, :], W12[:, t, 1:2], None, ALU.mult))
            settle()
            for t in range(NT):
                chain(v.scalar_tensor_tensor(CMB[:, t, :], OH2[:, t, :], W12[:, t, 2:3], OH1[:, t, :], ALU.mult, ALU.add))
            dve.wait_ge(rank_ready, 1)
            chain(v.tensor_copy(RK8[:, :, :].rearrange("p t e -> p (t e)"), bank[0][:, 0:16]))
            chain(v.tensor_scalar(OVR[:, :], bank[0][:, 16:24], float(P), None, ALU.is_gt))
            settle()
            for n, dst in enumerate((RKP, SLP, CBP)):
                chain(v.tensor_copy(dst[:, :, 0:EXPERTS], (RK8, SEL, CMB)[n][:, :, :]))
                chain(v.memset(dst[:, :, NP - 1:NP], 0.0))
            settle()

            def dispatch(p):
                one = bass.ds(p, 1) if not isinstance(p, int) else slice(p, p + 1)
                for t in range(NT):
                    v.tensor_scalar(DI[:, t, :], IO[:, :], RKP[:, t, one], SLP[:, t, one], ALU.is_equal, ALU.mult)\
                        .then_inc(disp_ready, 1)
                v.tensor_copy(CPC[:, :], CBP[:, :, one].rearrange("p t o -> p (t o)")).then_inc(disp_ready, 1)

            dispatch(0)
            dve.wait_ge(x2_hi, 1)
            low(XL, X[:, :, :].rearrange("p t d -> p (t d)"), XH).then_inc(x2_split, 1)

            chain(v.tensor_tensor_scan(POS[:, :], ONE[:, 0:8], OVR[:, :], 0.0, ALU.mult, ALU.add))
            chain(v.memset(NUM[:, :], 0.0))
            settle()
            chain(v.tensor_copy(NUM[:, 0:1], POS[:, 7:8]))
            for j in range(EXTRA):
                chain(v.scalar_tensor_tensor(EXJ[:, j, :], POS[:, :], float(j + 1), OVR[:, :], ALU.is_equal, ALU.mult))
            settle()
            for j in range(EXTRA):
                chain(v.tensor_tensor(PRE[:, j, :], EXJ[:, j, :], ROW8, ALU.mult))
                for n, src in enumerate((RK8, SEL, CMB)):
                    for t in range(NT):
                        chain(v.tensor_tensor(PRD[:, j, n, t, :], src[:, t, :], EXJ[:, j, :], ALU.mult))
            settle()
            chain(v.tensor_reduce(NUM[:, 1:4], PRE[:, :, :], AX_X, ALU.add))
            for n, dst in enumerate((RKP, SLP, CBP)):
                for t in range(NT):
                    chain(v.tensor_reduce(dst[:, t, EXPERTS:EXPERTS + EXTRA], PRD[:, :, n, t, :], AX_X, ALU.add))
            settle()
            chain(v.tensor_scalar(RKP[:, :, EXPERTS:NP - 1], RKP[:, :, EXPERTS:NP - 1], -float(P), None, ALU.add))
            v.tensor_copy(NUI[:, :], NUM[:, :]).then_inc(route_ready, 1)
            settle()
            dve.wait_ge(route_ready, 1)
            dve.wait_ge(eh_ready, MOE_H0)
            dve.wait_ge(eth_lo, MOE_H0)

            def gathered(p):
                for r in (6, 7):
                    dve.wait_ge(ring2_ready, ring_ready(p, r))
                    half = r % 2
                    v.tensor_copy(XGL[:, 4 * half:4 * half + 4, :].rearrange("p a c -> p (a c)"), ring_bank(r)[:, :]).then_inc(ring_dve, 1)

            def out_lo(p):
                for half in range(2):
                    dve.wait_ge(out_hi_s, 2 * p + (half + 1))
                    v.scalar_tensor_tensor(OL[:, half, :], bank[2 + half][:, :], CWC[:, 0:1], OH[:, half, :].bitcast(F32),
                                           ALU.mult, ALU.subtract).then_inc(out_lo_s, 1)

            def scattered(p, uses):
                for r in uses:
                    t, half = r // 2, r % 2
                    n = slice(512 * half, 512 * half + 512)
                    dve.wait_ge(ring2_ready, ring_ready(p, r))
                    v.tensor_tensor(X[:, t, n], X[:, t, n], ring_bank(r)[:, :], ALU.add).then_inc(ring_dve, 1)

            def lo_parts(p, first, end):
                for r in range(first, end):
                    m, pc = pass_pieces[r]
                    dve.wait_ge(hi_done, p * PP + (NF + r + 1))
                    at = SLOT * MOE_SLOT[m] + PIECE * pc
                    v.tensor_tensor(WL[:, r % PIECES, :], RAW[:, at:at + PIECE], WH[:, r % PIECES, :].bitcast(F32),
                                    ALU.subtract).then_inc(lo_done, 1)

            def expert(p, follow):
                done = AHEAD
                for j in range(FT + 1):
                    if j in (2, 3):
                        dve.wait_ge(ring_dve, p * RING_DVE + RING_DVE0)
                        scattered(p, (0, 1) if j == 2 else (2, 3))
                    upto = min(GU_AT[min(j, FT - 1)] + PIECES, PP)
                    lo_parts(p, done, upto)
                    done = max(done, upto)
                    if j == FT - 1:
                        follow(lambda: lo_parts(p + 1, 0, 1))
                    if j == FT - 3:
                        dve.wait_ge(ring2_ready, ring_ready(p - 1, 9))
                        dispatch(p + 1)
                    if j == FT:
                        follow(lambda: lo_parts(p + 1, 1, 3))
                    if j:
                        dve.wait_ge(eth_hi, p * FT + j)
                        low(EHL[:, (j - 1) % 2, :], bank[4 + 3 * ((j - 1) % 2)][:, 0:P], EHH[:, (j - 1) % 2, :]).then_inc(eth_lo, 1)
                    if j < FT:
                        dve.wait_ge(es_ready, p * FT + (j + 1))
                        if j:
                            dve.wait_ge(et_ready, p * FT + j)
                        v.tensor_tensor(EH[:, :], ES[:, :], bank[j % 2][:, P:T], ALU.mult).then_inc(eh_ready, 1)
                    if j == 0:
                        out_lo(p)
                follow(lambda: lo_parts(p + 1, 3, 4))
                gathered(p)
                follow(lambda: lo_parts(p + 1, 4, AHEAD))

            gathered(NONE_BEFORE)
            lo_parts(0, 0, 3)
            lo_parts(0, 3, AHEAD)
            dve.wait_ge(y_start, 1)
            with dve.Fori(0, EXPERTS - 1) as p:
                expert(p, always)
            n_extra = dve.value_load(NUI[0:1, 0:1], min_val=0, max_val=EXTRA)
            last_passes(dve, expert, n_extra)
            passes = n_extra + EXPERTS
            out_lo(passes)
            for r in range(4):
                scattered(passes, (r,))
                if r:
                    dve.wait_ge(ring_dve, passes * RING_DVE + (RING_DVE0 + r))
                    half_stats((r - 1) // 2, (r - 1) % 2)
            dve.wait_ge(ring_dve, passes * RING_DVE + (RING_DVE0 + 4))
            half_stats(1, 1)
            rows_normed(3, 2, [(0, 0), (0, 1), (1, 0)])

        @block.gpsimd
        def _(pool):
            g_ = nc.gpsimd
            chained = [0]

            def link(ins):
                chained[0] += 1
                ins.then_inc(pool_chain, 1)
                pool.wait_ge(pool_chain, chained[0])

            def select(t, pattern, base_, mult, op, fill):
                link(g_.affine_select(out=t, in_=t, compare_op=op, fill=fill, base=base_, pattern=pattern, channel_multiplier=mult))

            link(g_.memset(ID[:, :], 0.0))
            g_.affine_select(out=ID[:, :], in_=ID[:, :], compare_op=ALU.not_equal, fill=1.0, base=0, pattern=[[-1, P]],
                             channel_multiplier=1).then_inc(ident_ready, 1)
            for t, value in ((SI, 1.0), (LS, 1.0), (LV, 1.0), (BO, 1.0), (NTRI, -1.0), (NONE, -1.0),
                             (ONE, 1.0), (EC, -0.5), (EPS, GN_EPS)):
                g_.memset(t[tuple([slice(None)] * len(t.shape))], value)
            link(g_.iota(IO[:, :], [[1, P]], base=0, channel_multiplier=0, allow_small_or_imprecise_dtypes=True))
            select(SI[:, 0, :], [[1, P]], 0, -1, ALU.is_gt, 0.0)
            select(SI[:, 1, :], [[1, P]], 0, -1, ALU.is_ge, 0.0)
            select(LS[:, :], [[-1, P]], 0, 1, ALU.is_gt, 0.0)
            link(g_.tensor_copy(BD[:, 0, :], LS[:, :]))
            link(g_.tensor_copy(BD[:, 1, :], SI[:, 0, :]))
            for half in range(2):
                bd = BD[:, half, :].rearrange("p (b c) -> p b c", c=16)
                select(bd, [[-16, 8], [0, 16]], 0, 1, ALU.is_ge, 0.0)
                select(bd, [[16, 8], [0, 16]], 15, -1, ALU.is_ge, 0.0)
            bo = BO[:, :].rearrange("p (b c) -> p b c", c=HD)
            select(bo, [[-HD, 2], [0, HD]], 0, 1, ALU.is_ge, 0.0)
            select(bo, [[HD, 2], [0, HD]], HD - 1, -1, ALU.is_ge, 0.0)
            for lev in range(3):
                w = 16 << lev
                nb = P // (2 * w)
                lv = LV[:, lev, :].rearrange("p (b z c) -> p b z c", z=2, c=w)
                select(lv, [[0, nb], [-1, 2], [0, w]], 0, 0, ALU.is_ge, 0.0)
                select(lv, [[-2 * w, nb], [0, 2], [0, w]], -w, 1, ALU.is_ge, 0.0)
                select(lv, [[2 * w, nb], [0, 2], [0, w]], 2 * w - 1, -1, ALU.is_ge, 0.0)
            g_.affine_select(out=NTRI[:, :], in_=NTRI[:, :], compare_op=ALU.is_ge, fill=0.0, base=0, pattern=[[-1, P]],
                             channel_multiplier=1).then_inc(consts_ready, 1)
            pool.wait_ge(consts_ready, 1)

            pool.wait_ge(a_act, A_ACT[3])
            link(g_.memset(IND[:, :, :], 0.0))
            for half in range(2):
                own = IND[HD * half:HD * half + HD, :, :].rearrange("p i h -> p (i h)")[:, half:TILES * HEADS:HEADS + 2]
                g_.memset(own, 1.0)
            link(g_.memset(SPR[:, :, :], 1.0))
            select(SPR[:, :, :], [[P, TILES], [1, P]], 0, -HD, ALU.is_ge, 0.0)
            g_.affine_select(out=SPR[:, :, :], in_=SPR[:, :, :], compare_op=ALU.is_ge, fill=0.0, base=HD - 1,
                             pattern=[[-P, TILES], [-1, P]], channel_multiplier=HD).then_inc(heads_ready, 1)

            pool.wait_ge(cols_ready, 1)
            for pair in range(TILES // 2):
                pool.wait_ge(a_dve, A_DVE[6 + pair])
                for i in (2 * pair, 2 * pair + 1):
                    a2 = AR[:, i, :, 0, :]
                    link(g_.tensor_scalar(a2, KK[:, i, :].rearrange("p (c t) -> p c t", c=NT), col(VEC + 12 + i), None, ALU.mult))
                    if i >= 2:
                        pool.wait_ge(square_used, i - 1)
                    g_.tensor_tensor(SQ[:, i % 2, :].rearrange("p (c t) -> p c t", c=NT), a2, a2, ALU.mult).then_inc(square_ready, 1)
                for i in (2 * pair, 2 * pair + 1):
                    wait_emptied(pool, "gate", i)
                    if i >= 2:
                        pool.wait_ge(k_ready, i - 1)
                    link(g_.tensor_scalar(FM[:, i % 2, :], BT[:, i, :], col(VEC + 18 + i), OMKA[:, i:i + 1], ALU.mult, ALU.add))
                    g_.tensor_tensor(KK[:, i, :], KK[:, i, :], FM[:, i % 2, :], ALU.mult).then_inc(k_ready, 1)
            for i in range(TILES):
                pool.wait_ge(exp_used, i + 1)
                pool.wait_ge(k_ready, i + 1)
                two = lambda t: t.rearrange("p (c t) -> p c t", c=NT)
                link(g_.tensor_tensor(two(KK[:, i, :]), two(KK[:, i, :]), EI[:, i % 2, :, :], ALU.mult))
                g_.tensor_tensor(two(BT[:, i, :]), two(BT[:, i, :]), EI[:, i % 2, :, :], ALU.mult).then_inc(bk_scaled, 1)

            for g in range(NG):
                for l in range(4):
                    L = lanes[l]
                    PX = L["PX"]
                    pool.wait_ge(lane_dve[l], DVE_N * g + 3)
                    g_.tensor_tensor(PX[:, 2, :], PX[:, 1, :], ID[:, :], ALU.add).then_inc(lane_pool[l], 1)
                for l in range(4):
                    L = lanes[l]
                    g_.tensor_tensor(L["LT"][:, :, :], L["AL"][:, :].rearrange("p (o c) -> p o c", o=1).broadcast_to([P, 3, P]),
                                     LV[:, :, :], ALU.mult).then_inc(lane_pool[l], 1)

            for i in range(TILES):
                wait_emptied(pool, "yt", i)
                g_.tensor_tensor(YT[:, i, :], YT[:, i, :], V[:, i, :], ALU.add).then_inc(yt_bonus, 1)

            def rstd(idx):
                pool.wait_ge(stats_ready, NT * (idx + 1))
                link(g_.tensor_scalar(RS[:, :], MV[:, :, 1], LN_EPS, None, ALU.add))
                link(g_.tensor_tensor(RS[:, :], RS[:, :], EC[:, :], ALU.pow))
                link(g_.tensor_scalar(NM[:, :], MV[:, :, 0], -1.0, None, ALU.mult))
                g_.tensor_tensor(NM[:, :], NM[:, :], RS[:, :], ALU.mult).then_inc(rstd_ready, 1)

            def affine(idx):
                rstd(idx)
                pool.wait_ge(rows_in, 32 * (idx + 1))
                pool.wait_ge(xn_act, idx + 1)
                part = X[:, 1, HALF:D]
                link(g_.tensor_tensor(part, part, GB[:, 0, HALF:D], ALU.mult))
                g_.tensor_tensor(part, part, GB[:, 1, HALF:D], ALU.add).then_inc(x_ready, 1)

            affine(0)
            affine(1)
            for s in range(HEADS + 1):
                if s < HEADS:
                    pool.wait_ge(stick_sp, s + 1)
                    t = SP[:, s % 3, 0:3:2, :]
                    g_.affine_select(out=t, in_=t, compare_op=ALU.is_gt, fill=0.0, base=0, pattern=[[0, 2], [1, P]],
                                     channel_multiplier=-1).then_inc(stick_masked, 1)
                if s:
                    wait_emptied(pool, "z", s - 1)
                    t = WT[:, (s - 1) % 2, 0:3:2, :]
                    g_.affine_select(out=t, in_=t, compare_op=ALU.is_gt, fill=0.0, base=0, pattern=[[0, 2], [1, P]],
                                     channel_multiplier=-1).then_inc(stick_w, 1)
            affine(2)
            g_.memset(CWC[:, :], 0.0)
            link(g_.memset(DTC[:, :, :].bitcast(F32), 0.0))
            g_.memset(OH[:, :, :].bitcast(F32), 0.0).then_inc(cur_ready, 1)
            pool.wait_ge(x2_split, 1)
            g_.tensor_scalar(X[:, :, :], X[:, :, :], ALPHA, None, ALU.mult).then_inc(y_start, 1)

            def current(p):
                pool.wait_ge(ring2_ready, ring_ready(p, 3))
                pool.wait_ge(*ring_count(p - 1, 9))
                g_.tensor_tensor(DTC[:, :, :], DTN[:, :, :].bitcast(F32),
                                 ONE[:, :].rearrange("p (o c) -> p o c", o=1).broadcast_to([P, NT, P]), ALU.mult)
                g_.tensor_copy(CWC[:, :], CWN[:, :]).then_inc(cur_ready, 1)

            with pool.Fori(0, EXPERTS) as p:
                current(p)
            pool.wait_ge(route_ready, 1)
            n_extra = pool.value_load(NUI[0:1, 0:1], min_val=0, max_val=EXTRA)
            for j in range(EXTRA):
                with pool.If(n_extra > j):
                    current(EXPERTS + j)
            affine(3)


_INS = ["x", "mem", "a_w_in_first", "a_mu_first", "a_vec", "a_w_up", "a_a_up", "a_g_up", "a_r_k", "b_w_in",
        "w_kv_shared", "mem_kv", "w_o", "ln", "ffn_gate_up", "ffn_down", "router", "exp_gate_up", "exp_down"]


def kernel(**inputs):
    import numpy as np
    import concourse.bacc as bacc
    from concourse.bass_utils import run_bass_kernel_spmd

    nc = bacc.Bacc("TRN2", target_bir_lowering=False, num_devices=1)
    arrays, args = {}, []
    for name in _INS:
        a = np.ascontiguousarray(inputs[name])
        arrays[f"in_{name}"] = a
        args.append(nc.dram_tensor(f"in_{name}", a.shape, mybir.dt.from_np(a.dtype), kind="ExternalInput").ap())
    out = nc.dram_tensor("out", (1, T, D), F32, kind="ExternalOutput").ap()
    program(nc, *args, out)
    r = run_bass_kernel_spmd(nc, [arrays], core_ids=[0])
    return r.results[0]["out"]
```
